# Optimizing a Trainium2 kernel written in Bass

```python
import math
import numpy as np
import jax
import jax.numpy as jnp
from jax import lax

D_MODEL = 1024
BATCH = 1
SEQ = 512
DEPTH = 1
DEC_BATCH = 8
DEC_SEQ = 4
PAST_LEN = 256
PAGE_SIZE = 128

HEAD_DIM = 64
NSA_HEADS = D_MODEL // 128
NSA_KV_HEADS = 2
DSA_HEADS = D_MODEL // 128
DSA_KV_HEADS = 2
N_NSA_KV = 6
CMP_BLOCK = 32
CMP_STRIDE = 16
CMP_HIDDEN = 2 * HEAD_DIM
SEL_BLOCK = 64
N_SEL = 16
WINDOW = 512
IDX_HEADS = 4
IDX_DIM = 64
DSA_TOPK_MAX = 256
ROPE_THETA = 10000.0
Q_BLOCK = 128
EPS = 1e-6
NEG = -1e30
FORCED_SCORE = 1e4

IN_WIDTHS = (
    NSA_HEADS * HEAD_DIM,
    N_NSA_KV * NSA_KV_HEADS * HEAD_DIM,
    NSA_HEADS * 3,
    NSA_HEADS * HEAD_DIM,
    DSA_HEADS * HEAD_DIM,
    2 * DSA_KV_HEADS * HEAD_DIM,
    IDX_HEADS * IDX_DIM,
    IDX_DIM,
    IDX_HEADS,
    DSA_HEADS * HEAD_DIM,
    2 * D_MODEL,
)
IN_TOTAL = sum(IN_WIDTHS)

kernel_name = 'nsa_dsa_gated_hybrid_step'

def rms_norm(x, g):
    xf = x.astype(jnp.float32)
    y = xf * lax.rsqrt(jnp.mean(xf * xf, axis=-1, keepdims=True) + EPS)
    return (y * g.astype(jnp.float32)).astype(x.dtype)

def rope(x, pos):
    half = x.shape[-1] // 2
    inv = ROPE_THETA ** (-jnp.arange(half, dtype=jnp.float32) / half)
    ang = pos.astype(jnp.float32)[:, None] * inv[None, :]
    cos = jnp.cos(ang)[:, None, :]
    sin = jnp.sin(ang)[:, None, :]
    xf = x.astype(jnp.float32)
    x1, x2 = xf[..., :half], xf[..., half:]
    return jnp.concatenate([x1 * cos - x2 * sin, x2 * cos + x1 * sin], axis=-1).astype(x.dtype)

def masked_softmax(s, mask):
    s = jnp.where(mask, s, NEG)
    p = jnp.where(mask, jnp.exp(s - jnp.max(s, axis=-1, keepdims=True)), 0.0)
    return p / jnp.maximum(jnp.sum(p, axis=-1, keepdims=True), 1e-30)

def ada_norm(x, c, norm_g, w_ada, b_ada):
    mod = jax.nn.silu(c) @ w_ada + b_ada
    shift, scale, gate = jnp.split(mod, 3, axis=-1)
    h = rms_norm(x, norm_g) * (1.0 + scale[:, None, :]) + shift[:, None, :]
    return h, gate

def in_projection(h, w_in, pos):
    Bx, T, _ = h.shape
    cuts = [int(v) for v in np.cumsum(IN_WIDTHS)[:-1]]
    nq, nkv, ng, nz, dq, dkv, iq, ik, iw, dz, mg = jnp.split(h @ w_in, cuts, axis=-1)
    nsa_q = nq.reshape(Bx, T, NSA_HEADS, HEAD_DIM)
    nkv = nkv.reshape(Bx, T, N_NSA_KV, NSA_KV_HEADS, HEAD_DIM)
    nsa_rows = jnp.stack([nkv[:, :, 0], nkv[:, :, 1], rope(nkv[:, :, 2], pos), nkv[:, :, 3]], axis=2)
    win_rows = jnp.stack([rope(nkv[:, :, 4], pos), nkv[:, :, 5]], axis=2)
    dkv = dkv.reshape(Bx, T, 2, DSA_KV_HEADS, HEAD_DIM)
    dsa_rows = jnp.stack([rope(dkv[:, :, 0], pos), dkv[:, :, 1]], axis=2)
    idx_rows = rope(ik[:, :, None, :], pos)[:, :, 0]
    f = {
        'nsa_q': nsa_q,
        'nsa_q_rot': rope(nsa_q, pos),
        'nsa_gate': jax.nn.sigmoid(ng.astype(jnp.float32)).reshape(Bx, T, NSA_HEADS, 3),
        'nsa_z': nz,
        'dsa_q': rope(dq.reshape(Bx, T, DSA_HEADS, HEAD_DIM), pos),
        'idx_q': rope(iq.reshape(Bx, T, IDX_HEADS, IDX_DIM), pos),
        'idx_w': iw,
        'dsa_z': dz,
        'merge': mg,
    }
    return f, nsa_rows, win_rows, dsa_rows, idx_rows

def nsa_context(nsa_all, cmp_pe, cmp_w1, cmp_w2):
    Bx, L = nsa_all.shape[:2]
    G = NSA_KV_HEADS
    n_cmp = (L - CMP_BLOCK) // CMP_STRIDE + 1
    starts = np.arange(n_cmp, dtype=np.int32) * CMP_STRIDE
    blk_idx = starts[:, None] + np.arange(CMP_BLOCK, dtype=np.int32)[None, :]

    def compress(rows, pe, w1, w2):
        blk = rows[:, blk_idx] + pe[None, None, :, None, :]
        flat = jnp.swapaxes(blk, 2, 3).reshape(Bx, n_cmp, G, CMP_BLOCK * HEAD_DIM)
        return jax.nn.silu(flat @ w1) @ w2

    ck = compress(nsa_all[:, :, 0], cmp_pe[0], cmp_w1[0], cmp_w2[0])
    cv = compress(nsa_all[:, :, 1], cmp_pe[1], cmp_w1[1], cmp_w2[1])
    cmp_end = jnp.asarray(starts + CMP_BLOCK - 1)
    n_slc = -(-L // SEL_BLOCK)
    j = np.arange(n_slc, dtype=np.int32)[None, :]
    overlap = (starts[:, None] < (j + 1) * SEL_BLOCK) & (starts[:, None] + CMP_BLOCK > j * SEL_BLOCK)
    overlap = jnp.asarray(overlap, dtype=jnp.float32)
    pad = n_slc * SEL_BLOCK - L
    slc = jnp.pad(nsa_all[:, :, 2:4], ((0, 0), (0, pad), (0, 0), (0, 0), (0, 0)))
    slc = slc.reshape(Bx, n_slc, SEL_BLOCK, 2, G, HEAD_DIM).transpose(3, 0, 4, 1, 2, 5)
    return (ck, cv, cmp_end, overlap, slc[0], slc[1], min(N_SEL, n_slc))

def nsa_attend(q, q_rot, gate, qpos, ctx, win_k, win_v, win_pos):
    ck, cv, cmp_end, overlap, slc_kb, slc_vb, n_sel = ctx
    Bx, Tq = q.shape[:2]
    G, Hg = NSA_KV_HEADS, NSA_HEADS // NSA_KV_HEADS
    scale = HEAD_DIM ** -0.5
    qg = q.reshape(Bx, Tq, G, Hg, HEAD_DIM)
    qr = q_rot.reshape(Bx, Tq, G, Hg, HEAD_DIM)
    s = jnp.einsum('btghd,bngd->btghn', qg, ck).astype(jnp.float32) * scale
    vis = (cmp_end[None, :] <= qpos[:, None])[None, :, None, None, :]
    p_cmp = masked_softmax(s, vis)
    o_cmp = jnp.einsum('btghn,bngd->btghd', p_cmp.astype(cv.dtype), cv)
    imp = jnp.einsum('btgn,nj->btgj', jnp.sum(p_cmp, axis=3), overlap)
    n_slc = slc_kb.shape[2]
    jb = jnp.arange(n_slc, dtype=jnp.int32)[None, :]
    cur = (qpos // SEL_BLOCK)[:, None]
    forced = (jb == 0) | (jb == cur) | (jb == cur - 1)
    imp = jnp.where(forced[None, :, None, :], FORCED_SCORE, imp)
    imp = jnp.where((jb > cur)[None, :, None, :], NEG, imp)
    top_val, top_idx = lax.top_k(imp, n_sel)
    blk_ok = top_val > 0.5 * NEG
    bi = jnp.arange(Bx)[:, None, None, None]
    gi = jnp.arange(G)[None, None, :, None]
    sk = slc_kb[bi, gi, top_idx].reshape(Bx, Tq, G, n_sel * SEL_BLOCK, HEAD_DIM)
    sv = slc_vb[bi, gi, top_idx].reshape(Bx, Tq, G, n_sel * SEL_BLOCK, HEAD_DIM)
    kpos = top_idx[..., None] * SEL_BLOCK + jnp.arange(SEL_BLOCK, dtype=jnp.int32)
    ok = (blk_ok[..., None] & (kpos <= qpos[None, :, None, None, None])).reshape(Bx, Tq, G, 1, n_sel * SEL_BLOCK)
    s = jnp.einsum('btghd,btgmd->btghm', qr, sk).astype(jnp.float32) * scale
    o_slc = jnp.einsum('btghm,btgmd->btghd', masked_softmax(s, ok).astype(sv.dtype), sv)
    s = jnp.einsum('btghd,bwgd->btghw', qr, win_k).astype(jnp.float32) * scale
    dist = qpos[:, None] - win_pos[None, :]
    wok = ((dist >= 0) & (dist < WINDOW) & (win_pos[None, :] >= 0))[None, :, None, None, :]
    o_win = jnp.einsum('btghw,bwgd->btghd', masked_softmax(s, wok).astype(win_v.dtype), win_v)
    g = gate.reshape(Bx, Tq, G, Hg, 3)
    o = g[..., 0:1] * o_cmp + g[..., 1:2] * o_slc + g[..., 2:3] * o_win
    return o.reshape(Bx, Tq, NSA_HEADS * HEAD_DIM).astype(q.dtype)

def dsa_attend(q, idx_q, idx_w, qpos, k, v, idx_k, topk):
    Bx, Tq = q.shape[:2]
    L = k.shape[1]
    G, Hg = DSA_KV_HEADS, DSA_HEADS // DSA_KV_HEADS
    causal = jnp.arange(L, dtype=jnp.int32)[None, :] <= qpos[:, None]
    dots = jnp.einsum('bthd,bsd->bths', idx_q, idx_k).astype(jnp.float32) * (IDX_DIM ** -0.5)
    score = jnp.einsum('bths,bth->bts', jax.nn.relu(dots), idx_w.astype(jnp.float32)) * (IDX_HEADS ** -0.5)
    score = jnp.where(causal[None], score, NEG)
    _, sel = lax.top_k(score, topk)
    bi = jnp.arange(Bx)[:, None, None]
    sk = k[bi, sel]
    sv = v[bi, sel]
    ok = (sel <= qpos[None, :, None])[:, :, None, None, :]
    qg = q.reshape(Bx, Tq, G, Hg, HEAD_DIM)
    s = jnp.einsum('btghd,btkgd->btghk', qg, sk).astype(jnp.float32) * (HEAD_DIM ** -0.5)
    o = jnp.einsum('btghk,btkgd->btghd', masked_softmax(s, ok).astype(sv.dtype), sv)
    return o.reshape(Bx, Tq, DSA_HEADS * HEAD_DIM)

def mixer_out(x, gate_ada, f, o_n, o_d, w_up_nsa, w_up_dsa, w_out):
    u_n = (o_n * jax.nn.silu(f['nsa_z'])) @ w_up_nsa
    u_d = (o_d * jax.nn.silu(f['dsa_z'])) @ w_up_dsa
    g_n, g_d = jnp.split(jax.nn.sigmoid(f['merge']), 2, axis=-1)
    return x + gate_ada[:, None, :] * ((g_n * u_n + g_d * u_d) @ w_out)

def gather_pages(pool, page_table):
    g = pool[page_table]
    return g.reshape((page_table.shape[0], -1) + pool.shape[2:])

def prompt_layer(x, c, norm_g, w_ada, b_ada, w_in, cmp_pe, cmp_w1, cmp_w2, w_up_nsa, w_up_dsa, w_out):
    Bx, T, _ = x.shape
    pos = jnp.arange(T, dtype=jnp.int32)
    h, gate_ada = ada_norm(x, c, norm_g, w_ada, b_ada)
    f, nsa_rows, win_rows, dsa_rows, idx_rows = in_projection(h, w_in, pos)
    ctx = nsa_context(nsa_rows, cmp_pe, cmp_w1, cmp_w2)
    topk = min(DSA_TOPK_MAX, T // 4)
    win_pad = jnp.pad(win_rows, ((0, 0), (WINDOW, 0), (0, 0), (0, 0), (0, 0)))
    dsa_k, dsa_v = dsa_rows[:, :, 0], dsa_rows[:, :, 1]

    def block(i):
        qs = i * Q_BLOCK
        sl = lambda a: lax.dynamic_slice_in_dim(a, qs, Q_BLOCK, axis=1)
        qpos = qs + jnp.arange(Q_BLOCK, dtype=jnp.int32)
        wkv = lax.dynamic_slice_in_dim(win_pad, qs, WINDOW + Q_BLOCK, axis=1)
        wpos = qs - WINDOW + jnp.arange(WINDOW + Q_BLOCK, dtype=jnp.int32)
        o_n = nsa_attend(sl(f['nsa_q']), sl(f['nsa_q_rot']), sl(f['nsa_gate']), qpos, ctx,
                         wkv[:, :, 0], wkv[:, :, 1], wpos)
        o_d = dsa_attend(sl(f['dsa_q']), sl(f['idx_q']), sl(f['idx_w']), qpos, dsa_k, dsa_v, idx_rows, topk)
        return o_n, o_d

    o_n, o_d = lax.map(block, jnp.arange(T // Q_BLOCK, dtype=jnp.int32))
    o_n = jnp.swapaxes(o_n, 0, 1).reshape(Bx, T, NSA_HEADS * HEAD_DIM)
    o_d = jnp.swapaxes(o_d, 0, 1).reshape(Bx, T, DSA_HEADS * HEAD_DIM)
    y = mixer_out(x, gate_ada, f, o_n, o_d, w_up_nsa, w_up_dsa, w_out)
    return y, nsa_rows, dsa_rows, idx_rows, win_rows[:, T - min(WINDOW, T):]

def sample_layer(x, c, cache_nsa, cache_dsa, cache_idx, win_state, page_table,
                 norm_g, w_ada, b_ada, w_in, cmp_pe, cmp_w1, cmp_w2, w_up_nsa, w_up_dsa, w_out):
    Bx, T, _ = x.shape
    past = page_table.shape[1] * cache_nsa.shape[1]
    pos = past + jnp.arange(T, dtype=jnp.int32)
    h, gate_ada = ada_norm(x, c, norm_g, w_ada, b_ada)
    f, nsa_rows, win_rows, dsa_rows, idx_rows = in_projection(h, w_in, pos)
    nsa_all = jnp.concatenate([gather_pages(cache_nsa, page_table), nsa_rows], axis=1)
    dsa_all = jnp.concatenate([gather_pages(cache_dsa, page_table), dsa_rows], axis=1)
    idx_all = jnp.concatenate([gather_pages(cache_idx, page_table), idx_rows], axis=1)
    win_all = jnp.concatenate([win_state, win_rows], axis=1)
    wb = win_state.shape[1]
    wpos = past - wb + jnp.arange(wb + T, dtype=jnp.int32)
    ctx = nsa_context(nsa_all, cmp_pe, cmp_w1, cmp_w2)
    topk = min(DSA_TOPK_MAX, (past + T) // 4)
    o_n = nsa_attend(f['nsa_q'], f['nsa_q_rot'], f['nsa_gate'], pos, ctx, win_all[:, :, 0], win_all[:, :, 1], wpos)
    o_d = dsa_attend(f['dsa_q'], f['idx_q'], f['idx_w'], pos, dsa_all[:, :, 0], dsa_all[:, :, 1], idx_all, topk)
    y = mixer_out(x, gate_ada, f, o_n, o_d, w_up_nsa, w_up_dsa, w_out)
    return y, nsa_rows, dsa_rows, idx_rows, win_all[:, T:]

def setup_inputs(seed: int = 0) -> dict:
    key = jax.random.key(seed)
    ks = jax.random.split(key, 20)
    f32 = jnp.float32
    n_pages = PAST_LEN // PAGE_SIZE
    n_used = DEC_BATCH * n_pages
    n_pool = n_used + (n_used + 3) // 4
    wb = min(WINDOW, PAST_LEN)
    width = NSA_HEADS * HEAD_DIM

    def nrm(k, shape, s=1.0):
        return jax.random.normal(k, shape, f32) * s

    page_table = jax.random.permutation(ks[0], n_pool)[:n_used].reshape(DEC_BATCH, n_pages).astype(jnp.int32)
    return {
        'x_prompt': nrm(ks[1], (BATCH, SEQ, D_MODEL)),
        'x_sample': nrm(ks[2], (DEC_BATCH, DEC_SEQ, D_MODEL)),
        'cache_nsa_kv': nrm(ks[3], (DEPTH, n_pool, PAGE_SIZE, 4, NSA_KV_HEADS, HEAD_DIM)),
        'cache_dsa_kv': nrm(ks[4], (DEPTH, n_pool, PAGE_SIZE, 2, DSA_KV_HEADS, HEAD_DIM)),
        'cache_dsa_idx_k': nrm(ks[5], (DEPTH, n_pool, PAGE_SIZE, IDX_DIM)),
        'state_nsa_win_kv': nrm(ks[6], (DEPTH, DEC_BATCH, wb, 2, NSA_KV_HEADS, HEAD_DIM)),
        'page_table': page_table,
        'c_prompt': nrm(ks[7], (BATCH, D_MODEL)),
        'c_sample': nrm(ks[8], (DEC_BATCH, D_MODEL)),
        'norm_g': 1.0 + nrm(ks[9], (DEPTH, D_MODEL), 0.02),
        'w_ada': nrm(ks[10], (DEPTH, D_MODEL, 3 * D_MODEL), 0.5 * D_MODEL ** -0.5),
        'b_ada': nrm(ks[11], (DEPTH, 3 * D_MODEL), 0.01),
        'w_in': nrm(ks[12], (DEPTH, D_MODEL, IN_TOTAL), D_MODEL ** -0.5),
        'cmp_pe': nrm(ks[13], (DEPTH, 2, CMP_BLOCK, HEAD_DIM), 0.1),
        'cmp_w1': nrm(ks[14], (DEPTH, 2, CMP_BLOCK * HEAD_DIM, CMP_HIDDEN), (CMP_BLOCK * HEAD_DIM) ** -0.5),
        'cmp_w2': nrm(ks[15], (DEPTH, 2, CMP_HIDDEN, HEAD_DIM), CMP_HIDDEN ** -0.5),
        'w_up_nsa': nrm(ks[16], (DEPTH, width, D_MODEL), width ** -0.5),
        'w_up_dsa': nrm(ks[17], (DEPTH, DSA_HEADS * HEAD_DIM, D_MODEL), (DSA_HEADS * HEAD_DIM) ** -0.5),
        'w_out': nrm(ks[18], (DEPTH, D_MODEL, D_MODEL), D_MODEL ** -0.5),
        'final_g': 1.0 + nrm(ks[19], (D_MODEL,), 0.02),
    }

def reference(x_prompt, x_sample, cache_nsa_kv, cache_dsa_kv, cache_dsa_idx_k, state_nsa_win_kv, page_table,
              c_prompt, c_sample, norm_g, w_ada, b_ada, w_in, cmp_pe, cmp_w1, cmp_w2,
              w_up_nsa, w_up_dsa, w_out, final_g):
    yp, ys = x_prompt, x_sample
    l_pn, l_pd, l_pi, l_pw, l_sn, l_sd, l_si, l_sw = [], [], [], [], [], [], [], []
    for l in range(DEPTH):
        w = (norm_g[l], w_ada[l], b_ada[l], w_in[l], cmp_pe[l], cmp_w1[l], cmp_w2[l],
             w_up_nsa[l], w_up_dsa[l], w_out[l])
        yp, pn, pd, pi, pw = prompt_layer(yp, c_prompt, *w)
        ys, sn, sd, si, sw = sample_layer(ys, c_sample, cache_nsa_kv[l], cache_dsa_kv[l], cache_dsa_idx_k[l],
                                          state_nsa_win_kv[l], page_table, *w)
        l_pn.append(pn); l_pd.append(pd); l_pi.append(pi); l_pw.append(pw)
        l_sn.append(sn); l_sd.append(sd); l_si.append(si); l_sw.append(sw)
    y_prompt = rms_norm(yp, final_g)
    y_sample = rms_norm(ys, final_g)
    new_nsa_kv_prompt = jnp.stack(l_pn, axis=0)
    new_dsa_kv_prompt = jnp.stack(l_pd, axis=0)
    new_idx_k_prompt = jnp.stack(l_pi, axis=0)
    new_win_prompt = jnp.stack(l_pw, axis=0)
    new_nsa_kv_sample = jnp.stack(l_sn, axis=0)
    new_dsa_kv_sample = jnp.stack(l_sd, axis=0)
    new_idx_k_sample = jnp.stack(l_si, axis=0)
    new_win_sample = jnp.stack(l_sw, axis=0)
    return (y_prompt, y_sample, new_nsa_kv_prompt, new_dsa_kv_prompt, new_idx_k_prompt, new_win_prompt,
            new_nsa_kv_sample, new_dsa_kv_sample, new_idx_k_sample, new_win_sample)


_drawn_inputs = setup_inputs


def setup_inputs(seed=0):
    import zlib

    import numpy as np

    out = dict(_drawn_inputs(seed))
    spreads = {}
    factors = {'cache_nsa_kv': 4.409,
     'cache_dsa_kv': 2.688,
     'cache_dsa_idx_k': 3.016,
     'norm_g': 2.921,
     'b_ada': 4.218,
     'cmp_pe': 8.0,
     'cmp_w1': 3.86,
     'cmp_w2': 3.099,
     'final_g': 2.84}
    for name, (base, spread) in spreads.items():
        noise = np.random.default_rng([zlib.crc32(name.encode()), seed]).standard_normal(out[name].shape)
        drawn = base * np.exp(spread * noise) if base else spread * noise
        out[name] = jnp.asarray(drawn.astype(out[name].dtype))
    for name, factor in factors.items():
        out[name] = (out[name] * factor).astype(out[name].dtype)
    return out
```

```python
from contextlib import ExitStack

import concourse.bass as bass
from concourse import mybir

F32 = mybir.dt.float32
F32R = mybir.dt.float32r
I32 = mybir.dt.int32
ALU = mybir.AluOpType
ACT = mybir.ActivationFunctionType
AX = mybir.AxisListType

P = 128
D = 1024
KT = D // P
SEQ = 512
NSEQ, NEW = 8, 4
NS = NSEQ * NEW
TOK = SEQ + NS
PAST = 256
PAGE = 128
NPAGE = PAST // PAGE
NT = 5
HD = 64
TOPK_P, TOPK_S = 128, (PAST + NEW) // 4
NCP, NCS = 31, 15
NKS = PAST + NS
EPS = 1e-6
NEG = -1e30
TAKEN = -3e38
SCALE = HD ** -0.5
IDX_SCALE = (HD ** -0.5) * (4 ** -0.5)

NQ, NKV, DQ, DKV, IQ, NZ, DZ, MG = 0, 512, 1816, 2328, 2584, 1304, 2908, 3420
T_JOBS = [(IQ, 324), (NKV, 512), (NQ, 512), (DQ, 512), (DKV, 256), (NKV + 512, 280)]
J_IDX, J_KV, J_NQ, J_DQ, J_DKV, J_WIN = range(6)
ROPED = [(0, 5), (256, 2), (0, 8), (0, 8), (0, 2), (0, 2)]
STG = [0, 1, 0, 1, 2, 0]
ACT_READS = [1, 1, 1, 0, 1, 1]
CMP, SLC, WIN, DSA = range(4)
PLAIN, ROT, DSAQ = range(3)
G_JOBS = [("z", 0), ("z", 1)] + [(k, c) for c in range(2) for k in ("mn", "un", "md", "ud")] + [("y", 0), ("y", 1)]
JOBS = [("T", i) for i in range(6)] + G_JOBS
G_EVAC = {"z": "a", "mn": "a", "md": "a", "un": "v", "ud": "v", "y": "v"}

PIECES = [2 if k in ("un", "ud") else 4 for k, _ in JOBS]
FIRST = [sum(PIECES[:i]) for i in range(len(JOBS) + 1)]

AUX = [(1, "qi", 0, "a"), (1, "qi", 1, "v"), (1, "ki", 0, "a"), (1, "si", 0, "v"),
       (2, "cmpT", 0, "v"), (2, "cmpT", 1, "a"), (2, "k", SLC, "a"), (2, "kn", SLC, "v"),
       (2, "ikT", 0, "a"), (2, "ikT", 1, "v"), (2, "ikT", 2, "a"), (2, "ikT", 3, "v"), (2, "sdots", 0, "a")]
AUX += [(2, "dots", (t, h), "a") for t in (1, 2, 3) for h in range(4)]
AUX += [(2, "ssum", 0, "v")]
for _s in (0, 1):
    AUX += [(3, "q", (_s, j), "av"[j % 2]) for j in range(4)] + [(3, "qs", _s, "v")]
AUX += [(3, "raw", (0, n), "av"[n % 2]) for n in range(4)] + [(3, "hid", 0, "a"), (3, "ck", 0, "v")]
AUX += [(4, "q", (2, j), "av"[j % 2]) for j in range(4)] + [(4, "qs", 2, "v")]
AUX += [(4, "raw", (1, n), "av"[n % 2]) for n in range(4)] + [(4, "hid", 1, "a"), (4, "cvp", 0, "v"),
                                                             (4, "cvs", 0, "a"), (4, "cvs", 1, "v")]
AUX += [(5, "selx", 0, "a"), (5, "selx", 1, "a"), (5, "k", DSA, "a"), (5, "kn", DSA, "v")]
AUX += [(6, "k", WIN, "a"), (6, "kn", WIN, "v"), (6, "grow", 0, "v"), (6, "grow", 1, "v")]
AUX_AT = {(k, n): i for i, (_, k, n, _) in enumerate(AUX)}



def _plan_units():
    units = []
    for T in range(2):
        for j in (2 * T, 2 * T + 1):
            if j % 2:
                units.append(("K", SLC, T))
            units.extend(("P", b, j, t) for t in range(4) for b in (CMP, SLC, WIN))
        units += [("S", CMP, T), ("K", WIN, T), ("S", SLC, T), ("S", WIN, T)]
    for j in range(4):
        if j in (1, 2):
            units.append(("K", DSA, j - 1))
        units.extend(("P", DSA, j, t) for t in range(4))
    return units + [("S", DSA, 0), ("S", DSA, 1)]


UNITS = _plan_units()
LAG = 3
OWNERS = [("n", 0), ("n", 1), ("N", 0), ("n", 2), ("n", 3), ("N", 1), ("d", 0), ("d", 1), ("d", 2), ("d", 3), ("D", 0),
          ("D", 1)]


def owner(u):
    kind, b = u[0], u[1]
    return OWNERS.index((("nd" if kind == "P" else "ND")[b == DSA], u[2]))


REAL = [u[0] != "K" for u in UNITS]
ORD = [sum(REAL[:i]) for i in range(len(UNITS) + 1)]
ORDP = [sum(u[0] == "P" for u in UNITS[:i]) for i in range(len(UNITS) + 1)]
LAST_OF = {owner(u): i for i, u in enumerate(UNITS) if REAL[i]}
FIRST_OF = {w: min(i for i, u in enumerate(UNITS) if REAL[i] and owner(u) == w) for w in LAST_OF}
KV_ORDER = [(u[1], u[2]) for u in UNITS if u[0] == "K"]


def kv_slot(b, T):
    return KV_ORDER.index((b, T)) % 2


LOADS = []


def _plan_loads():
    def weights(job):
        LOADS.extend(("w", job, e) for e in range(PIECES[job] // 2))

    LOADS.extend(("ada", c, e) for c in range(4) for e in range(2))
    for job in range(3):
        weights(job)
    for job, extra in ((3, [("idxraw", 0, 0)]), (4, [("cmpraw", 0, 0), ("cmpw", 0, 0)]),
                       (5, [("cmpraw", 1, 0), ("cmpw", 1, 0)])):
        LOADS.extend([("w", job, 0), *extra, ("w", job, 1)])
    LOADS.append(("w", 6, 0))
    LOADS.extend(("kv", b, T) for b, T in KV_ORDER)
    LOADS.append(("w", 6, 1))
    for job in range(7, len(JOBS) - 1):
        if job == len(JOBS) - 2:
            LOADS.append(("w", job, 0))
            LOADS.extend(("ada", c, e) for c in (4, 5) for e in range(2))
            LOADS.append(("w", job, 1))
        else:
            weights(job)
    weights(len(JOBS) - 1)


_plan_loads()
SLOTS = 2
LOAD_AT = {key: i for i, key in enumerate(LOADS)}
PE_LOADS = [i for i, key in enumerate(LOADS) if key[0] != "w"]
N_DMAS = {"w": 1, "ada": 1, "idxraw": 16, "cmpraw": 16, "cmpw": 1, "kv": 8}


def dmas_of(key):
    if key[0] == "w" and JOBS[key[1]][0] in ("un", "ud"):
        return 2
    if key[0] == "kv" and key[1] == WIN:
        return 1
    return N_DMAS[key[0]]


TAB = {}


def _table_columns():
    at = 0
    for name, n in (("ident", 128), ("mrow", 512), ("mcmp", 128), ("cos", 320), ("sin", 320), ("msamp", 576),
                    ("expand", 256), ("headmask", 24), ("hsum", 32), ("midx", 288), ("gsel", 9), ("bselp", 128),
                    ("bsels", 32), ("vis", 1), ("brow", 192)):
        TAB[name] = (at, at + n)
        at += n
    return at


NTAB = _table_columns()


def tables():
    import numpy as np
    t = np.zeros((P, NTAB), np.float32)

    def put(name, x):
        t[:x.shape[0], TAB[name][0]:TAB[name][0] + x.shape[1]] = x

    p = np.arange(P)
    put("ident", np.eye(P))
    put("mrow", np.concatenate([np.zeros((P, 384)), np.where(p[None] <= p[:, None], 0.0, NEG)], 1))
    ends = np.arange(NCP) * 16 + 31
    mc = np.zeros((P, 4, 32))
    for i in range(4):
        mc[:, i, :NCP] = np.where(ends[None] <= (i * P + p)[:, None], 0.0, NEG)
    put("mcmp", mc.reshape(P, 128))
    inv = np.float32(10000.0) ** (-np.arange(32, dtype=np.float32) / np.float32(32))
    pos = np.zeros((NT, P), np.float32)
    pos[:4] = np.arange(SEQ).reshape(4, P)
    pos[4, :NS] = PAST + np.arange(NS) % NEW
    ang = (pos[:, :, None] * inv).astype(np.float32).transpose(1, 0, 2).astype(np.float64)
    put("cos", np.concatenate([np.cos(ang), np.cos(ang)], 2).reshape(P, 320))
    put("sin", np.concatenate([-np.sin(ang), np.sin(ang)], 2).reshape(P, 320))
    s4, g, j, tt = p // 32, p % 32 // 16, p % 16 // 4, p % 4
    ks, kt = np.arange(NS) // NEW, np.arange(NS) % NEW
    ms = np.zeros((P, 2, NKS))
    ex = np.zeros((NS, 2, P))
    for T in range(2):
        seq = 4 * T + s4
        ms[:, T, PAST:] = np.where((ks[None] == seq[:, None]) & (kt[None] <= tt[:, None]), 0.0, NEG)
        ex[seq * NEW + tt, T, p] = 1
    put("msamp", ms.reshape(P, -1))
    put("expand", ex.reshape(NS, -1))
    hm = np.zeros((P, 8, 3))
    hm[p, g * 4 + j] = 1
    put("headmask", hm.reshape(P, 24))
    put("hsum", np.tile(np.eye(32), (4, 1)))
    mi = np.zeros((NS, NKS))
    mi[:, PAST:] = np.where((ks[None] == ks[:, None]) & (kt[None] <= kt[:, None]), 0.0, NEG)
    put("midx", mi)
    gs = np.zeros((P, 9))
    bp, bs = np.zeros((P, P)), np.zeros((P, NS))
    for q in range(4):
        gs[32 * q + np.arange(9), np.arange(9)] = 1
        bp[32 * q] = 1
        bs[32 * q + 1 + ks, np.arange(NS)] = 1
    put("gsel", gs)
    put("bselp", bp)
    put("bsels", bs)
    put("vis", (p >= 31).astype(np.float32)[:, None])
    put("brow", np.repeat(np.eye(6), 32, axis=1))
    return t


def spread(ap, at, n):
    dims = [list(d) for d in ap.ap]
    return bass.AP(ap.tensor, ap.offset, dims[:at] + [[0, n]] + dims[at:])


def build(nc, a, o):
    ctx = ExitStack()
    with ctx:
        def sb(name, shape, dt=F32, st=ctx):
            return st.enter_context(nc.sbuf_tensor(name, shape, dt))

        def sem(name):
            return ctx.enter_context(nc.semaphore(name))

        tab = sb("tab", [P, NTAB])

        def tb(name, rows=P):
            return tab[0:rows, TAB[name][0]:TAB[name][1]]

        ident = tb("ident")
        hT = [sb(f"hT_{n}", [P, KT, TOK], F32R) for n in ("hi", "lo")]
        stage = [sb(f"stage{i}", [P, 2048]) for i in range(SLOTS)]
        whl = [[sb(f"w_{n}{i}", [P, 2, 512], F32R) for i in range(2)] for n in ("hi", "lo")]
        cT = sb("cT", [P, KT, 32])
        bada = sb("b_ada", [6, 512])
        gates = sb("gates", [P, NT, 24])
        grow = sb("gate_rows", [P, 2, 3])
        gtmp = sb("gate_tmp", [P, 24])
        gT = sb("norm_gT", [P, KT])
        norm = sb("norm_stats", [P, 32])
        stats = sb("softmax_stats", [P, 4, 8])
        pages = sb("page_row", [1, NSEQ * NPAGE], I32)
        top8 = sb("top8", [P, 8])

        abc = ExitStack()
        qT = [sb(f"qT_{n}", [P, 4, SEQ], F32, abc) for n in ("plain", "rot", "dsa")]
        qTi = sb("qT_idx", [P, 2, TOK], F32, abc)
        kz = [None] + [sb(f"kz_{n}", [P, 2, SEQ], F32, abc) for n in ("slc", "win", "dsa")]
        kzi = sb("kz_idx", [P, 2, SEQ], F32, abc)
        knew = [None] + [sb(f"k_new_{n}", [P, NS], F32, abc) for n in ("slc", "win", "dsa")]
        kni = sb("k_new_idx", [HD, NS], F32, abc)
        ckz = sb("ckz", [P, 2, 32], F32, abc)
        ckS = sb("ck_sample", [P, NSEQ * NCS], F32, abc)
        cvP = sb("cv_prompt", [32, P], F32, abc)
        cvS = sb("cv_sample", [16, NSEQ, P], F32, abc)
        V = [None] + [sb(f"v_{n}", [P, NT, P], F32, abc) for n in ("slc", "win", "dsa")]
        qS = [sb(f"q_sample_{n}", [P, 2 * P], F32, abc) for n in ("plain", "rot", "dsa")]
        score = sb("score", [P, 3, SEQ], F32, abc)
        scoreS = sb("score_sample", [NS, NKS], F32, abc)
        selS = sb("sel_sample", [P, 2, NKS], F32, abc)
        ab = ExitStack()
        stg = sb("staging", [P, 3, NT * 512], F32, ab)
        rope_b = sb("rope_b", [P, 2, 512], F32, ab)
        rTs = sb("rT_sample", [P, 16 * P], F32, ab)
        rTp = sb("rT_prompt", [P, 2, 2, PAST], F32, ab)
        aT = sb("cmp_act", [P, 304], F32, ab)
        w2 = sb("cmp_w2", [P, 2, HD], F32, ab)
        peT = sb("cmp_peT", [P, 32], F32, ab)
        relu_d = sb("relu_dots", [P, 2, 512], F32, ab)
        relu_s = sb("relu_dots_sample", [P, NKS], F32, ab)
        iw = sb("idx_w", [P, NT, 4], F32, ab)
        iwr = sb("idx_w_rows", [P, 1], F32, ab)
        AB = sb("mod_AB", [P, 2, KT, 9], F32, ab)
        ab.close()
        c_only = ExitStack()
        prob = sb("prob", [P, 4, 2, SEQ], F32, c_only)
        probT = sb("probT", [P, 2, 2, SEQ], F32, c_only)
        kTs = sb("kT_sample", [P, 2, 4, PAST], F32, c_only)
        oT = sb("oT", [P, 8, TOK], F32, c_only)
        c_only.close()
        abc.close()
        d = ctx
        oz = [sb(f"oz_{n}", [P, 8, TOK], F32R, d) for n in ("hi", "lo")]
        zs = sb("silu_z", [P, 2, TOK], F32, d)
        mT = [sb(f"mT_{n}", [P, KT, TOK], F32R, d) for n in ("hi", "lo")]
        sg = sb("sig_n", [P, 4, TOK], F32, d)
        sg2 = sb("sig_d", [P, 4, TOK], F32, d)
        mt = sb("merged", [P, 4, TOK], F32, d)
        yb = sb("y", [P, NT, D], F32, d)
        fgb = sb("final_g", [P, D], F32, d)
        gateP = sb("gate_prompt", [P, D], F32, d)
        xs = stg[:, :, :].rearrange("p a n -> p (a n)")[:, 0:NT * D].rearrange("p (t n) -> p t n", t=NT)
        mod = stg[:, 2, 0:2048]
        rb_all = rope_b[:, :, :].rearrange("p a n -> p (a n)")
        c_raw = relu_d[:, :, :].rearrange("p a n -> p (a n)")
        ng8 = aT[0:8, 0:P]
        pe32 = aT[0:32, P:2 * P]
        ikTs = rTs[0:HD, :]
        iqz = qT[DSAQ][0:HD, 0:2, :].rearrange("p j n -> p (j n)")
        iqa = qT[DSAQ][0:HD, 2, 0:P]
        gateS = sg2[:, :, :].rearrange("p a n -> p (a n)")[0:NS, 0:D]
        mod_g = zs[:, :, :].rearrange("p a n -> p (a n)")[:, 0:D]

        bank = [ctx.enter_context(nc.psum_tensor(f"bank{i}", [P, 512], F32)) for i in range(8)]

        in_tab, in_c, in_small, in_w2 = sem("in_tab"), sem("in_c"), sem("in_small"), sem("in_w2")
        in_x = [sem(f"in_x{t}") for t in range(NT)]
        in_pages = sem("in_pages")
        loaded = [sem(f"loaded{i}") for i in range(SLOTS)]
        pe_freed = sem("pe_freed")
        hi_made, lo_made = sem("hi_made"), sem("lo_made")
        piece_used = sem("piece_used")
        act_step, dve_step, pool_step = sem("act_step"), sem("dve_step"), sem("pool_step")
        zeroed = sem("zeroed")
        csilu, c_turned, cT_made = sem("csilu"), sem("c_turned"), sem("cT_made")
        small_made = sem("small_made")
        mod_done, mod_copied = sem("mod_done"), sem("mod_copied")
        ab_done, ab_made = sem("ab_done"), sem("ab_made")
        squared, ms_made, rooted, xn_made = sem("squared"), sem("ms_made"), sem("rooted"), sem("xn_made")
        x_turned, h_made, h_hi, h_lo = sem("x_turned"), sem("h_made"), sem("h_hi"), sem("h_lo")
        t_done, t_dve, t_act = sem("t_done"), sem("t_dve"), sem("t_act")
        roped = sem("roped")
        aux_done, aux_act, aux_dve = sem("aux_done"), sem("aux_act"), sem("aux_dve")
        score_added = sem("score_added")
        iq_laid, sdots_weighted, sel_made = sem("iq_laid"), sem("sdots_weighted"), sem("sel_made")
        stored = {n: sem(f"stored_{n}") for n in ("idx", "kv", "dkv", "win", "old", "y")}
        s_done, masked, exped = sem("scores_done"), sem("masked"), sem("exped")
        r_made, scaled = sem("r_made"), sem("scaled")
        pt_done, pt_act, pt_dve = sem("pt_done"), sem("pt_act"), sem("pt_dve")
        pv_done, o_copied = sem("pv_done"), sem("o_copied")
        g_done, g_act, g_dve = sem("g_done"), sem("g_act"), sem("g_dve")
        z_mul, oz_hi, oz_lo = sem("z_mul"), sem("oz_hi"), sem("oz_lo")
        m_made, mT_hi, mT_lo = sem("m_made"), sem("mT_hi"), sem("mT_lo")
        in_fg, in_xy = sem("in_fg"), sem("in_xy")
        gate_made = sem("gate_made")
        y_sum, y_sq, y_ms, y_root, y_out = sem("y_sum"), sem("y_sq"), sem("y_ms"), sem("y_root"), sem("y_out")

        def arrived(eng, key):
            i = LOAD_AT[key]
            eng.wait_ge(loaded[i % SLOTS], 16 * sum(dmas_of(LOADS[k]) for k in range(i % SLOTS, i + 1, SLOTS)))

        def staged(key):
            return stage[LOAD_AT[key] % SLOTS]

        def rows(t):
            return NS if t == 4 else P

        def act_tiles(job, t):
            return 5 * sum(ACT_READS[:job]) + (t + 1 if ACT_READS[job] else 0)

        def aux_wait(eng, kind, n):
            i = AUX_AT[(kind, n)]
            e = AUX[i][3]
            eng.wait_ge(aux_act if e == "a" else aux_dve, sum(x[3] == e for x in AUX[:i + 1]))

        def aux_last_read(job):
            return sum(x[0] <= job + 1 for x in AUX)

        def job_pieces(job):
            return range(FIRST[job], FIRST[job + 1])

        G0 = 6
        GA, GV = [0], [0]
        for kind, _ in G_JOBS:
            GA.append(GA[-1] + NT * (G_EVAC[kind] == "a"))
            GV.append(GV[-1] + NT * (G_EVAC[kind] == "v"))

        def g_read(eng, g, t):
            if G_EVAC[G_JOBS[g][0]] == "a":
                eng.wait_ge(g_act, GA[g] + t + 1)
            else:
                eng.wait_ge(g_dve, GV[g] + t + 1)

        def g_signals(g):
            return sum(4 if k == "y" else 3 for k, _ in G_JOBS[:g])

        def tile_ready(eng, job, t):
            g = job - G0
            if t == NT - 1 or (g >= 0 and t == 3 and G_JOBS[g][0] != "y"):
                eng.wait_ge(piece_used, FIRST[job + 1])
            elif g < 0:
                eng.wait_ge(t_done, (NT - 1) * job + t + 1)
            else:
                eng.wait_ge(g_done, g_signals(g) + t + 1)

        def part(x, b0, t):
            return x[:, b0 + t, 0:SEQ] if t < 4 else x[:, b0:b0 + 4, SEQ:TOK]

        def samples_bank(g):
            return bank[4 + g % 2]

        def piece(n):
            job = max(j for j in range(len(JOBS)) if FIRST[j] <= n)
            q = n - FIRST[job]
            w = T_JOBS[JOBS[job][1]][1] if JOBS[job][0] == "T" else 512
            return ("w", job, q // 2), q % 2, w

        def w_part(which, n, w):
            return whl[which][n % 2][:, :, :].rearrange("p k n -> p (k n)")[:, 0:2 * w]

        def split_views(n, which):
            key, half, w = piece(n)
            dst, hi, src = w_part(which, n, w), w_part(0, n, w), staged(key)[:, 2 * w * half:2 * w * half + 2 * w]
            if JOBS[key[1]][0] != "z":
                return [(dst, src, hi)]
            dst, hi, src = (x.rearrange("p (k n) -> p k n", k=2) for x in (dst, hi, src))
            return [(by_pair(dst[:, k]), by_group(src[:, k]), by_pair(hi[:, k])) for k in range(2)]

        def by_group(x):
            return x.rearrange("p (g j d) -> p g j d", g=2, j=4)

        def by_pair(x):
            return x.rearrange("p (j g d) -> p g j d", g=2, j=4)

        def before_evac(job):
            return range(FIRST[job] + 2, min(FIRST[job + 1] + 1, FIRST[-1]))

        def after_evac(job):
            return range(min(FIRST[job + 1] + 1, FIRST[-1]), min(FIRST[job + 1] + 2, FIRST[-1]))

        def moves(kind, n, src, copy):
            if kind == "qi":
                return copy(qTi[:, n, 0:SEQ], src[:, :])
            if kind in ("ki", "k"):
                dst = kzi if kind == "ki" else kz[n]
                hi = 0 if kind == "ki" else 64
                copy(dst[0:64, 0, :], src[0:64, :])
                return copy(dst[64:128, 1, :], src[hi:hi + 64, :])
            if kind == "kn":
                return copy(knew[n][:, :], src[:, 0:NS])
            if kind == "cmpT":
                v = src[:, :].rearrange("p (q r) -> p r q", r=2)
                for g in range(2):
                    for r in range(2):
                        last = copy(rTp[64 * r:64 * r + 64, n, g, :], v[64 * g:64 * g + 64, r, :])
                return last
            if kind == "ikT":
                return copy(ikTs[:, 512 * n:512 * n + 512], src[0:HD, :])
            if kind == "q":
                return copy(qT[n[0]][:, n[1], :], src[:, :])
            if kind == "qs":
                for g in range(2):
                    v = qS[n][64 * g:64 * g + 64, :].rearrange("p (s g j t) -> p g j s t", s=NSEQ, g=2, j=4)
                    last = copy(v[:, g], src[64 * g:64 * g + 64, 0:P].rearrange("p (j s t) -> p j s t", j=4, s=NSEQ))
                return last
            if kind == "raw":
                v = rTs[:, 512 * n[1]:512 * n[1] + 512].rearrange("p (s g q) -> p s g q", s=2, g=2)
                w = src[:, :].rearrange("p (s r q) -> p s r q", s=2, r=2)
                for g in range(2):
                    for r in range(2):
                        last = copy(v[64 * r:64 * r + 64, :, g, :], w[64 * g:64 * g + 64, :, r, :])
                return last
            if kind == "ck":
                copy(ckz[0:64, 0, 0:NCP], src[0:64, 0:NCP])
                copy(ckz[64:128, 1, 0:NCP], src[64:128, 0:NCP])
                return copy(ckS[:, :], src[:, 32:32 + NSEQ * NCS])
            if kind == "cvp":
                return copy(cvP[0:NCP, :], src[0:NCP, 0:P])
            assert kind == "cvs"
            return copy(cvS[0:NCS, 4 * n:4 * n + 4, :], src[0:NCS, :].rearrange("p (s c) -> p s c", s=4))

        DOTS = [x[2] for x in AUX if x[1] == "dots"]

        block = ctx.enter_context(nc.Block())

        @block.sync
        def _(sp):
            sp.dma_start(pages[:, :], a["page_table"].rearrange("s n -> (s n)").rearrange("(a n) -> a n", a=1)).then_inc(in_pages, 16)
            page_of = {}

            def page(i):
                return sp.value_load(pages[0:1, i:i + 1], min_val=0, max_val=a["cache_nsa_kv"].shape[1] - 1)

            for i, key in enumerate(LOADS):
                kind, x, e = key
                if i >= SLOTS:
                    old = LOADS[i - SLOTS]
                    if old[0] == "w":
                        sp.wait_ge(lo_made, FIRST[old[1]] + 2 * old[2] + 2)
                    else:
                        sp.wait_ge(pe_freed, PE_LOADS.index(i - SLOTS) + 1)
                s = i % SLOTS
                st = stage[s]
                if kind == "w":
                    job, c = JOBS[x]
                    if job in ("un", "ud"):
                        w = a["w_up_nsa" if job == "un" else "w_up_dsa"][0]
                        for g in range(2):
                            sp.dma_start(st[64 * g:64 * g + 64, :].rearrange("p (j n) -> p j n", j=4),
                                         w[256 * g:256 * g + 256, 512 * c:512 * c + 512]
                                         .rearrange("(j d) n -> d j n", j=4)).then_inc(loaded[s], 16)
                        continue
                    if job == "T":
                        w, at, n = a["w_in"][0], *T_JOBS[c]
                    elif job == "z":
                        w, at, n = a["w_in"][0], (NZ, DZ)[c], 512
                    elif job == "y":
                        w, at, n = a["w_out"][0], 512 * c, 512
                    else:
                        w, at, n = a["w_in"][0], MG + (D if job == "md" else 0) + 512 * c, 512
                    sp.dma_start(st[:, 0:4 * n].rearrange("p (k n) -> p k n", k=4),
                                 w[512 * e:512 * e + 512, at:at + n].rearrange("(k p) n -> p k n", p=P))\
                        .then_inc(loaded[s], 16)
                elif kind == "ada":
                    sp.dma_start(st[:, :].rearrange("p (k n) -> p k n", k=4),
                                 a["w_ada"][0][512 * e:512 * e + 512, 512 * x:512 * x + 512]
                                 .rearrange("(k p) n -> p k n", p=P)).then_inc(loaded[s], 16)
                elif kind == "cmpw":
                    sp.dma_start(st[:, :].rearrange("p (i n) -> p i n", i=16),
                                 a["cmp_w1"][0][x].rearrange("(i p) n -> p i n", p=P)).then_inc(loaded[s], 16)
                elif kind == "idxraw":
                    sp.wait_ge(in_pages, 16)
                    v = st[:, 0:16 * HD].rearrange("p (n c) -> p n c", n=16)
                    for n in range(16):
                        sp.dma_start(v[:, n, :], a["cache_dsa_idx_k"][0, bass.ds(page(n), 1)]
                                     .rearrange("a p c -> (a p) c")).then_inc(loaded[s], 16)
                elif kind == "cmpraw":
                    v = st[:, :].rearrange("p (s r c) -> p s r c", s=NSEQ, r=2)
                    for n in range(16):
                        h = n % NPAGE
                        sp.dma_start(v[64 * h:64 * h + 64, n // NPAGE, :, :],
                                     a["cache_nsa_kv"][0, bass.ds(page(n), 1), :, x]
                                     .rearrange("a (q r) g d -> (a q) r (g d)", r=2)).then_inc(loaded[s], 16)
                else:
                    v = st[:, :].rearrange("p (n c) -> p n c", n=8)
                    if x == WIN:
                        sp.dma_start(v, a["state_nsa_win_kv"][0, 4 * e:4 * e + 4]
                                     .rearrange("s (h p) x g d -> p (s h) (x g d)", p=PAGE)).then_inc(loaded[s], 16)
                        continue
                    for n in range(8):
                        pg = bass.ds(page(8 * e + n), 1)
                        src = a["cache_nsa_kv"][0, pg, :, 2:4] if x == SLC else a["cache_dsa_kv"][0, pg]
                        sp.dma_start(v[:, n, :], src.rearrange("a p x g d -> (a p) (x g d)")).then_inc(loaded[s], 16)

        @block.gpsimd
        def _(pool):
            pool.memset(cT[:, :, :], 0.0).then_inc(zeroed, 1)
            for b in (SLC, WIN, DSA):
                pool.memset(kz[b][:, :, :], 0.0)
            pool.memset(kzi[:, :, :], 0.0)
            pool.memset(ckz[:, :, :], 0.0)
            for q in qS:
                pool.memset(q[:, :], 0.0)
            pool.memset(iqz, 0.0).then_inc(zeroed, 1)
            pool.dma_start(o["win_s"][0, :, 0:PAST - NEW].rearrange("s w x g d -> s (w x g d)"),
                           a["state_nsa_win_kv"][0, :, NEW:PAST].rearrange("s w x g d -> s (w x g d)"))\
                .then_inc(stored["old"], 16)

            def stores(name, buf, n, prompt, sample):
                pool.dma_start(prompt, stg[:, buf, :].rearrange("p (t n) -> p t n", t=NT)[:, 0:4, n[0]:n[1]])\
                    .then_inc(stored[name], 16)
                pool.dma_start(sample, stg[0:NS, buf, 4 * 512 + n[0]:4 * 512 + n[1]]).then_inc(stored[name], 16)

            for job in range(6):
                c0, H = ROPED[job]
                for t in range(NT):
                    r = rows(t)
                    n = NT * job + t
                    dst = stg[0:r, STG[job], 512 * t + c0:512 * t + c0 + HD * H]
                    pool.wait_ge(t_dve, n + 1)
                    pool.tensor_tensor(dst, dst, rope_b[0:r, n % 2, 0:HD * H], ALU.add).then_inc(roped, 1)
                pool.wait_ge(roped, NT * (job + 1))
                if job == J_IDX:
                    stores("idx", 0, (256, 320), o["idx_p"][0, 0].rearrange("(t p) c -> p t c", p=P),
                           o["idx_s"][0].rearrange("s t c -> (s t) c"))
                elif job == J_KV:
                    pool.wait_ge(t_act, act_tiles(J_KV, 4))
                    stores("kv", 1, (0, 512), o["nsa_p"][0, 0].rearrange("(t p) x g d -> p t (x g d)", p=P),
                           o["nsa_s"][0].rearrange("s t x g d -> (s t) (x g d)"))
                elif job == J_DKV:
                    pool.wait_ge(t_act, act_tiles(J_DKV, 4))
                    stores("dkv", 2, (0, 256), o["dsa_p"][0, 0].rearrange("(t p) x g d -> p t (x g d)", p=P),
                           o["dsa_s"][0].rearrange("s t x g d -> (s t) (x g d)"))
                elif job == J_WIN:
                    pool.wait_ge(t_act, act_tiles(J_WIN, 4))
                    stores("win", 0, (0, 256), o["win_p"][0, 0].rearrange("(t p) x g d -> p t (x g d)", p=P),
                           o["win_s"][0, :, PAST - NEW:PAST].rearrange("s t x g d -> s t (x g d)"))

            for u, unit in enumerate(UNITS):
                if not REAL[u]:
                    continue
                kind, b, _, t = (*unit, 0)[:4]
                pool.wait_ge(r_made, ORD[u] + 1)
                pool.wait_ge(exped, u + 1)
                s = stats[:, u % 4, :]
                if kind == "P":
                    n = NCP if b == CMP else P * (t + 1)
                    pool.tensor_scalar(prob[:, u % 4, 0, 0:n], prob[:, u % 4, 0, 0:n], s[:, 6:7], 1.0, ALU.mult, ALU.mult)
                    pool.tensor_scalar(prob[:, u % 4, 1, 0:n], prob[:, u % 4, 1, 0:n], s[:, 7:8], 1.0, ALU.mult,
                                       ALU.mult).then_inc(scaled, 1)
                else:
                    n = NCS if b == CMP else NKS
                    pool.tensor_scalar(prob[:, u % 4, 0, 0:n], prob[:, u % 4, 0, 0:n], s[:, 6:7], 1.0, ALU.mult,
                                       ALU.mult).then_inc(scaled, 1)

            for t in range(NT):
                pool.wait_ge(y_out, t + 1)
                dst = o["y_s"].rearrange("s t n -> (s t) n") if t == 4 else o["y_p"][0, P * t:P * t + P]
                pool.dma_start(dst, yb[0:rows(t), t, :]).then_inc(stored["y"], 16)
            pool.wait_ge(stored["y"], 16 * NT)
            for name in ("idx", "kv", "dkv", "win"):
                pool.wait_ge(stored[name], 32)
            pool.wait_ge(stored["old"], 16)

        @block.tensor
        def _(pe):
            mm = pe.matmul

            def three(out, left, right, first, last, **kw):
                mm(out, left[0], right[0], start=first, stop=False, skip_group_check=True)
                mm(out, left[1], right[0], start=False, stop=False, skip_group_check=True)
                return mm(out, left[0], right[1], start=False, stop=last, skip_group_check=True)

            pe.wait_ge(in_tab, 16)
            pe.wait_ge(csilu, 1)
            for k in range(KT):
                last = pe.transpose(bank[5][:, 9 * k:9 * k + 9], rb_all[0:9, P * k:P * k + P], ident[0:9, 0:9])
            last.then_inc(c_turned, 1)
            pe.wait_ge(in_small, 48)
            pe.transpose(bank[6][:, 0:8], ng8, ident[0:8, 0:8])
            pe.transpose(bank[6][:, 8:40], pe32, ident[0:32, 0:32]).then_inc(c_turned, 1)

            def modulation(c, out):
                mm(out[0:32, :], tb("brow", 6)[:, 32 * c:32 * c + 32], bada[:, :], start=True, stop=False,
                   skip_group_check=True)
                for e in range(2):
                    arrived(pe, ("ada", c, e))
                    w = staged(("ada", c, e))[:, :].rearrange("p (k n) -> p k n", k=4)
                    for k in range(4):
                        last = mm(out[32 * k:32 * k + 32, :], cT[:, 4 * e + k, :], w[:, k, :],
                                  start=(e == 0 and k > 0), stop=(e == 1), skip_group_check=True)
                    last.then_inc(pe_freed, 1)

            pe.wait_ge(cT_made, 1)
            for c in range(4):
                modulation(c, bank[c])
                pe.wait_ge(pe_freed, 2 * c + 2)
                pe.nop().then_inc(mod_done, 1)
            pe.wait_ge(mod_copied, 4)
            for w in range(2):
                for k in range(KT):
                    last = mm(bank[7][:, 16 * (w * KT + k):16 * (w * KT + k) + 9],
                              mod[:, D * w + P * k:D * w + P * k + P], tb("gsel"), start=True, stop=True)
            last.then_inc(ab_done, 1)
            for t in range(NT):
                pe.wait_ge(xn_made, t + 1)
            pe.wait_ge(small_made, 1)
            for k in range(KT):
                if k == 2:
                    pe.wait_ge(ab_made, 1)
                if k >= 3:
                    pe.wait_ge(h_made, k - 2)
                for t in range(4):
                    last = pe.transpose(bank[5 + k % 3][:, P * t:P * t + P], xs[:, t, P * k:P * k + P], ident)
                last.then_inc(x_turned, 1)
            for k in range(KT):
                last = pe.transpose(bank[4][:, NS * k:NS * k + NS], xs[0:NS, 4, P * k:P * k + P], ident[0:NS, 0:NS])
            last.then_inc(x_turned, 1)

            def token_major(job, left):
                for n in range(FIRST[job], FIRST[job + 1]):
                    pe.wait_ge(lo_made, n + 1)
                    q = n - FIRST[job]
                    _, _, w = piece(n)
                    final = n == FIRST[job + 1] - 1
                    for t in range(NT):
                        r = rows(t)
                        if q == 0 and 0 < job < G0:
                            pe.wait_ge(t_dve, NT * (job - 1) + t + 1)
                        if q == 0 and job > G0:
                            g_read(pe, job - G0 - 1, t)
                            if t == 4:
                                g_read(pe, job - G0 - 2, t)
                        for i in range(2):
                            k = 2 * q + i
                            last = three(bank[t][0:r, 0:w], [x[:, k, P * t:P * t + r] for x in left],
                                         [w_part(x, n, w)[:, i * w:i * w + w] for x in range(2)],
                                         q == 0 and i == 0, final and i == 1)
                        if final and t < NT - 1:
                            last.then_inc(t_done if job < G0 else g_done, 1)
                    last.then_inc(piece_used, 1)

            def feature_major(job):
                kind, c = JOBS[job]
                for n in range(FIRST[job], FIRST[job + 1]):
                    pe.wait_ge(lo_made, n + 1)
                    q = n - FIRST[job]
                    final = n == FIRST[job + 1] - 1
                    for b in range(4):
                        if q == 0 and job > G0:
                            g_read(pe, job - G0 - 1, b)
                            if b == 0 and job > G0 + 1:
                                g_read(pe, job - G0 - 2, 4)
                        if q == 0 and b == 0 and kind in ("un", "ud"):
                            pe.wait_ge(oz_lo, 5 if kind == "un" else 10)
                        for i in range(2):
                            k = 2 * q + i
                            wk = [w_part(x, n, 512)[:, i * 512:i * 512 + 512] for x in range(2)]
                            left = [x[:, P * b:P * b + P] for x in wk]
                            mov = ([x[:, k, :] for x in hT] if kind in ("z", "mn", "md") else
                                   [x[:, k + (0 if kind == "un" else 4), :] for x in oz])
                            for at, out in ((0, bank[b][:, :]), (SEQ, samples_bank(job - G0)[:, NS * b:NS * b + NS])):
                                m = [x[:, at:at + (SEQ if at == 0 else NS)] for x in mov]
                                first = q == 0 and i == 0 and (at == 0 or b == 0)
                                last = three(out, left, m, first, final and i == 1)
                        if final and b < 3:
                            last.then_inc(g_done, 1)
                    last.then_inc(piece_used, 1)

            def stg_tile(buf, t):
                return stg[0:rows(t), buf, 512 * t:512 * t + 512]

            def turn_tiles(out, pick, m=P):
                for t in range(4):
                    last = pe.transpose(out[0:m, P * t:P * t + P], pick(t), ident)
                return last

            def aux(slot):
                for i, (at, kind, n, _) in enumerate(AUX):
                    if at != slot:
                        continue
                    out = bank[5 + i % 3]
                    if i >= 3:
                        e = AUX[i - 3][3]
                        pe.wait_ge(aux_act if e == "a" else aux_dve, sum(x[3] == e for x in AUX[:i - 2]))
                    if kind == "qi":
                        pe.wait_ge(roped, NT * (J_IDX + 1))
                        last = turn_tiles(out, lambda t: stg_tile(0, t)[:, P * n:P * n + P])
                    elif kind == "ki":
                        last = turn_tiles(out, lambda t: stg_tile(0, t)[:, 256:320], HD)
                    elif kind == "si":
                        src = stg_tile(0, 4)
                        pe.transpose(out[:, 0:NS], src[:, 0:P], ident[0:NS, 0:NS])
                        pe.transpose(out[:, NS:2 * NS], src[:, P:2 * P], ident[0:NS, 0:NS])
                        last = pe.transpose(out[0:HD, 2 * NS:3 * NS], src[:, 256:320], ident[0:NS, 0:NS])
                    elif kind == "cmpT":
                        pe.wait_ge(t_act, act_tiles(J_KV, 4))
                        last = turn_tiles(out, lambda t: stg_tile(1, t)[:, P * n:P * n + P])
                    elif kind in ("k", "kn"):
                        job, c0 = {SLC: (J_KV, 256), DSA: (J_DKV, 0), WIN: (J_WIN, 0)}[n]
                        pe.wait_ge(roped, NT * (job + 1))
                        if kind == "k":
                            last = turn_tiles(out, lambda t: stg_tile(STG[job], t)[:, c0:c0 + P])
                        else:
                            last = pe.transpose(out[:, 0:NS], stg_tile(STG[job], 4)[:, c0:c0 + P], ident[0:NS, 0:NS])
                    elif kind == "ikT":
                        arrived(pe, ("idxraw", 0, 0))
                        src = staged(("idxraw", 0, 0))[:, 0:16 * HD].rearrange("p (n c) -> p n c", n=16)
                        for m in range(4):
                            last = pe.transpose(out[0:HD, P * m:P * m + P], src[:, 4 * n + m, :], ident)
                        if n == 3:
                            last.then_inc(pe_freed, 1)
                            pe.wait_ge(pe_freed, PE_LOADS.index(LOAD_AT[("idxraw", 0, 0)]) + 1)
                            last = pe.nop()
                    elif kind == "sdots":
                        pe.wait_ge(iq_laid, 1)
                        for m in range(4):
                            aux_wait(pe, "ikT", m)
                        for s in range(NSEQ):
                            mm(out[:, 0:PAST], iqz[:, P * s:P * s + P], ikTs[:, PAST * s:PAST * s + PAST],
                               start=(s == 0), stop=(s == NSEQ - 1))
                        last = mm(out[:, PAST:NKS], iqa, kni[:, :], start=True, stop=True)
                    elif kind == "ssum":
                        pe.wait_ge(sdots_weighted, 1)
                        last = mm(out[0:NS, 0:NKS], tb("hsum"), relu_s[:, :], start=True, stop=True)
                    elif kind == "dots":
                        t, h = n
                        aux_wait(pe, "qi", h // 2)
                        aux_wait(pe, "ki", 0)
                        last = mm(out[:, 0:P * (t + 1)], qTi[:, h // 2, P * t:P * t + P],
                                  kzi[:, h % 2, 0:P * (t + 1)], start=True, stop=True)
                    elif kind in ("q", "qs"):
                        which, j = n if kind == "q" else (n, 0)
                        job, buf = {PLAIN: (J_NQ, 2), ROT: (J_NQ, 0), DSAQ: (J_DQ, 1)}[which]
                        if which == PLAIN:
                            pe.wait_ge(t_act, act_tiles(J_NQ, 4))
                        else:
                            pe.wait_ge(roped, NT * (job + 1))

                        def pair(t, j):
                            return stg_tile(buf, t)[:, P * j:P * j + P]
                        if kind == "q":
                            last = turn_tiles(out, lambda t: pair(t, j))
                        else:
                            for j in range(4):
                                last = pe.transpose(out[:, NS * j:NS * j + NS], pair(4, j), ident[0:NS, 0:NS])
                    elif kind == "raw":
                        s, m = n
                        arrived(pe, ("cmpraw", s, 0))
                        src = staged(("cmpraw", s, 0))[:, :].rearrange("p (s r c) -> p s r c", s=NSEQ, r=2)
                        for x in range(4):
                            last = pe.transpose(out[:, P * x:P * x + P], src[:, 2 * m + x // 2, x % 2, :], ident)
                        if m == 3:
                            last.then_inc(pe_freed, 1)
                            pe.wait_ge(pe_freed, PE_LOADS.index(LOAD_AT[("cmpraw", s, 0)]) + 1)
                            last = pe.nop()
                    elif kind == "hid":
                        arrived(pe, ("cmpw", n, 0))
                        for m in range(4):
                            aux_wait(pe, "raw", (n, m))
                        aux_wait(pe, "cmpT", n)
                        w1 = staged(("cmpw", n, 0))[:, :].rearrange("p (i n) -> p i n", i=16)
                        rs = rTs[:, :].rearrange("p (x c) -> p x c", x=16)
                        for i in range(16):
                            mm(out[:, 0:240], w1[:, i, :], rs[:, :, i:i + 8 * (NCS - 1) + 1:8], start=(i == 0),
                               stop=(i == 15), skip_group_check=True)
                            mm(out[:, 240:302], w1[:, i, :], rTp[:, n, :, i:i + 8 * (NCP - 1) + 1:8], start=False,
                               stop=(i == 15), skip_group_check=True)
                            last = mm(out[:, 302:303], w1[:, i, :], peT[:, 16 * n + i:16 * n + i + 1], start=False,
                                      stop=(i == 15), skip_group_check=True)
                        last.then_inc(pe_freed, 1)
                        pe.wait_ge(pe_freed, PE_LOADS.index(LOAD_AT[("cmpw", n, 0)]) + 1)
                        last = pe.nop()
                    elif kind == "ck":
                        aux_wait(pe, "hid", 0)
                        pe.wait_ge(in_w2, 16)
                        for g in range(2):
                            mm(out[64 * g:64 * g + 64, 0:NCP], w2[:, 0, :], aT[:, 240 + NCP * g:240 + NCP * g + NCP],
                               start=True, stop=True)
                            last = mm(out[64 * g:64 * g + 64, 32:32 + NSEQ * NCS], w2[:, 0, :],
                                      aT[:, 0:240].rearrange("p (s g n) -> p s g n", s=NSEQ, g=2)[:, :, g, :],
                                      start=True, stop=True)
                    elif kind == "cvp":
                        aux_wait(pe, "hid", 1)
                        for g in range(2):
                            last = mm(out[0:NCP, HD * g:HD * g + HD], aT[:, 240 + NCP * g:240 + NCP * g + NCP],
                                      w2[:, 1, :], start=True, stop=True)
                    elif kind == "cvs":
                        for x in range(8):
                            at = NCS * (8 * n + x)
                            last = mm(out[0:NCS, HD * x:HD * x + HD], aT[:, at:at + NCS], w2[:, 1, :],
                                      start=True, stop=True)
                    elif kind == "selx":
                        pe.wait_ge(sel_made, 1)
                        last = mm(out[:, 0:NKS], tb("expand", NS)[:, P * n:P * n + P], scoreS[:, :], start=True,
                                  stop=True)
                    elif kind == "grow":
                        pe.wait_ge(t_act, act_tiles(J_WIN, 4))
                        last = mm(out[:, 0:24], tb("expand", NS)[:, P * n:P * n + P], gates[0:NS, 4, :], start=True,
                                  stop=True)
                    last.then_inc(aux_done, 1)

            pe.wait_ge(h_lo, 9)
            for job in range(G0):
                token_major(job, hT)
                aux(job)
            aux(G0)

            def keys(b, t):
                return NCP if b == CMP else P * (t + 1)

            def scores(u):
                unit = UNITS[u]
                kind, b = unit[:2]
                out = [bank[2 * (u % 2) + g] for g in range(2)]
                if u >= 2:
                    pe.wait_ge(exped, u - 1)
                if kind == "P":
                    j, t = unit[2:]
                    left = qT[PLAIN if b == CMP else ROT if b < DSA else DSAQ][:, j, P * t:P * t + P]
                    for g in range(2):
                        right = ckz[:, g, 0:NCP] if b == CMP else kz[b][:, g, 0:P * (t + 1)]
                        last = mm(out[g][:, 0:keys(b, t)], left, right, start=True, stop=True)
                    last.then_inc(s_done, 1)
                elif kind == "K":
                    key = ("kv", b, unit[2])
                    arrived(pe, key)
                    raw = staged(key)[:, :].rearrange("p (n c) -> p n c", n=8)
                    for n in range(8):
                        last = pe.transpose(out[n // 4][:, P * (n % 4):P * (n % 4) + P], raw[:, n, 0:P], ident)
                    last.then_inc(s_done, 1)
                else:
                    T = unit[2]
                    q = qS[PLAIN if b == CMP else ROT if b < DSA else DSAQ][:, P * T:P * T + P]
                    if b != CMP:
                        n = UNITS.index(("K", b, T))
                        pe.wait_ge(exped, n + 1)
                        pe.wait_ge(masked, n + 1)
                    for s in range(4):
                        right = (ckS[:, NCS * (4 * T + s):NCS * (4 * T + s) + NCS] if b == CMP
                                 else kTs[:, kv_slot(b, T), s, :])
                        last = mm(out[0][32 * s:32 * s + 32, 0:NCS if b == CMP else PAST], q[:, 32 * s:32 * s + 32],
                                  right, start=True, stop=True)
                    if b != CMP:
                        last = mm(out[0][:, PAST:NKS], q, knew[b][:, :], start=True, stop=True)
                    last.then_inc(s_done, 1)

            def turn(u):
                unit = UNITS[u]
                if not REAL[u]:
                    return
                kind, b = unit[:2]
                pe.wait_ge(scaled, ORD[u] + 1)
                if ORD[u] > 0:
                    pe.wait_ge(pt_act, ORD[u])
                    pe.wait_ge(pt_dve, ORDP[u])
                src = prob[:, u % 4]
                if kind == "P":
                    t = unit[3]
                    for g in range(2):
                        if b == CMP:
                            last = pe.transpose(bank[4 + g][0:NCP, 0:P], src[:, g, 0:NCP], ident)
                        else:
                            for n in range(t + 1):
                                last = pe.transpose(bank[4 + g][:, P * n:P * n + P], src[:, g, P * n:P * n + P], ident)
                elif b == CMP:
                    last = pe.transpose(bank[4][0:NCS, 0:P], src[:, 0, 0:NCS], ident)
                else:
                    for n in range(2):
                        pe.transpose(bank[4][:, P * n:P * n + P], src[:, 0, P * n:P * n + P], ident)
                    last = pe.transpose(bank[4][0:NS, PAST:PAST + P], src[:, 0, PAST:NKS], ident)
                last.then_inc(pt_done, 1)

            def values(u):
                unit = UNITS[u]
                if not REAL[u]:
                    return
                kind, b = unit[:2]
                w = owner(unit)
                out = bank[6 + w % 2]
                first = u == FIRST_OF[w]
                final = u == LAST_OF[w]
                pe.wait_ge(pt_act, ORD[u] + 1)
                pe.wait_ge(pt_dve, ORDP[u + 1])
                if first and w >= 2:
                    pe.wait_ge(o_copied, w - 1)
                pt = probT[:, ORD[u] % 2]
                if kind == "P":
                    t = unit[3]
                    blocks = [(n, P) for n in range(t + 1)] if b != CMP else [(0, NCP)]
                    for n, m in blocks:
                        for g in range(2):
                            v = cvP[0:m, HD * g:HD * g + HD] if b == CMP else V[b][:, n, HD * g:HD * g + HD]
                            last = mm(out[64 * g:64 * g + 64, P * t:P * t + P], v, pt[0:m, g, P * n:P * n + P],
                                      start=(first and n == 0), stop=final, skip_group_check=True)
                elif b == CMP:
                    for s in range(4):
                        last = mm(out[:, 32 * s:32 * s + 32], cvS[0:NCS, 4 * unit[2] + s, :],
                                  pt[0:NCS, 0, 32 * s:32 * s + 32], start=(first and s == 0), stop=final,
                                  skip_group_check=True)
                else:
                    T = unit[2]
                    mm(out[:, 0:P], V[b][0:NS, 4, :], pt[0:NS, 0, PAST:PAST + P], start=first, stop=False,
                       skip_group_check=True)
                    raw = staged(("kv", b, T))[:, :].rearrange("p (n c) -> p n c", n=8)
                    for s in range(4):
                        for n in range(2):
                            last = mm(out[:, 32 * s:32 * s + 32], raw[:, 2 * s + n, P:2 * P],
                                      pt[:, 0, P * n + 32 * s:P * n + 32 * s + 32], start=False, stop=final,
                                      skip_group_check=True)
                    last.then_inc(pe_freed, 1)
                    pe.wait_ge(pe_freed, PE_LOADS.index(LOAD_AT[("kv", b, T)]) + 1)
                    last = pe.nop()
                last.then_inc(pv_done, 1)

            pe.wait_ge(aux_act, sum(x[3] == "a" for x in AUX))
            pe.wait_ge(aux_dve, sum(x[3] == "v" for x in AUX))
            pe.wait_ge(t_act, act_tiles(5, 4))
            for i in range(len(UNITS) + LAG + 1):
                if i < len(UNITS):
                    scores(i)
                if 0 <= i - LAG < len(UNITS):
                    turn(i - LAG)
                if 0 <= i - LAG - 1 < len(UNITS):
                    values(i - LAG - 1)

            pe.wait_ge(exped, len(UNITS))
            for job in range(G0, len(JOBS)):
                if JOBS[job][0] == "y":
                    if JOBS[job][1] == 0:
                        g_read(pe, job - G0 - 1, 4)
                        g_read(pe, job - G0 - 2, 4)
                        for c in (4, 5):
                            modulation(c, bank[c + 1])
                            pe.wait_ge(pe_freed, len(PE_LOADS) - 2 * (5 - c))
                            pe.nop().then_inc(mod_done, 1)
                        pe.wait_ge(mod_copied, 6)
                        for c in range(2):
                            mm(bank[5 + c][:, :], tb("bselp"), mod_g[:, 512 * c:512 * c + 512], start=True, stop=True)
                        mm(bank[7][0:NS, :], tb("bsels"), mod_g[:, 0:512], start=True, stop=True).then_inc(ab_done, 1)
                        pe.wait_ge(gate_made, 1)
                        mm(bank[7][0:NS, :], tb("bsels"), mod_g[:, 512:1024], start=True, stop=True).then_inc(ab_done, 1)
                        pe.wait_ge(mT_lo, 2 * NT)
                    token_major(job, mT)
                else:
                    feature_major(job)

        @block.scalar
        def _(act):
            A = act.activation
            told = {}
            latest = []

            def tell(s):
                told[id(s)] = told.get(id(s), 0) + 1
                latest[:] = [s, told[id(s)]]
                return s, 1

            def own():
                if latest:
                    act.wait_ge(*latest)

            def link(ins):
                ins.then_inc(*tell(act_step))
                own()

            act.dma_start(c_raw[0:1, :], a["c_prompt"]).then_inc(in_c, 16)
            act.dma_start(c_raw[1:9, :], a["c_sample"]).then_inc(in_c, 16)
            act.dma_start(tab[:, :], a["tables"]).then_inc(in_tab, 16)
            act.dma_start(ng8, a["norm_g"].rearrange("l (k p) -> (l k) p", p=P)).then_inc(in_small, 16)
            act.dma_start(pe32, a["cmp_pe"][0].rearrange("s (i r) d -> (s i) (r d)", r=2)).then_inc(in_small, 16)
            act.dma_start(bada[:, :], a["b_ada"].rearrange("l (c n) -> (l c) n", c=6)).then_inc(in_small, 16)
            for t in range(NT):
                src = a["x_sample"].rearrange("s t n -> (s t) n") if t == 4 else a["x_prompt"][0, P * t:P * t + P]
                act.dma_start(xs[0:rows(t), t, :], src).then_inc(in_x[t], 16)
            act.dma_start(w2[:, :, :], a["cmp_w2"][0].rearrange("s p d -> p s d")).then_inc(in_w2, 16)
            act.wait_ge(in_c, 32)
            A(rb_all[0:9, :], c_raw[0:9, :], ACT.Silu).then_inc(*tell(csilu))
            for t in range(NT):
                act.wait_ge(in_x[t], 16)
                if t:
                    act.wait_ge(squared, t)
                A(rTs[0:rows(t), 0:D], xs[0:rows(t), t, :], ACT.Square, accum_out=norm[0:rows(t), t:t + 1])\
                    .then_inc(*tell(squared))
            act.wait_ge(ms_made, 2)
            A(norm[:, 16:20], norm[:, 8:12], ACT.Sqrt)
            A(norm[0:NS, 20:21], norm[0:NS, 12:13], ACT.Sqrt).then_inc(*tell(rooted))
            for c in range(4):
                act.wait_ge(mod_done, c + 1)
                A(mod[:, 512 * c:512 * c + 512], bank[c][:, :], ACT.Copy).then_inc(*tell(mod_copied))
            for k in range(KT):
                act.wait_ge(h_made, k + 1)
                own()
                A(hT[0][:, k, 0:SEQ], rope_b[:, k % 2, :], ACT.Copy).then_inc(*tell(h_hi))
            act.wait_ge(h_made, KT + 1)
            A(hT[0][:, :, SEQ:TOK], rope_b[:, 0, 0:KT * NS].rearrange("p (k n) -> p k n", k=KT), ACT.Copy)\
                .then_inc(*tell(h_hi))

            def split_hi(n):
                own()
                arrived(act, piece(n)[0])
                if n >= 2:
                    act.wait_ge(piece_used, n - 1)
                for dst, src, _ in split_views(n, 0):
                    last = A(dst, src, ACT.Copy)
                last.then_inc(*tell(hi_made))

            def read_tiles(job):
                if not ACT_READS[job]:
                    return
                if job == J_KV:
                    act.wait_ge(x_turned, KT + 1)
                if job == J_NQ:
                    act.wait_ge(ab_done, 1)
                if job == J_DKV:
                    act.wait_ge(aux_done, aux_last_read(J_NQ))
                if job == J_WIN:
                    act.wait_ge(aux_done, aux_last_read(J_NQ))
                for t in range(NT):
                    r = rows(t)
                    tile_ready(act, job, t)
                    own()
                    ps = bank[t][0:r, :]
                    st = stg[0:r, STG[job], 512 * t:512 * t + 512]
                    if job == J_IDX:
                        last = A(iw[0:r, t, :], ps[:, 320:324], ACT.Copy)
                    elif job == J_KV:
                        A(st[:, 0:256], ps[:, 0:256], ACT.Copy)
                        A(st[:, 384:512], ps[:, 384:512], ACT.Copy)
                        last = A(V[SLC][0:r, t, :], ps[:, 384:512], ACT.Copy)
                    elif job == J_NQ:
                        last = A(by_pair(stg[0:r, 2, 512 * t:512 * t + 512]), by_group(ps[:, :]), ACT.Copy)
                    else:
                        A(st[:, 128:256], ps[:, 128:256], ACT.Copy)
                        last = A(V[DSA if job == J_DKV else WIN][0:r, t, :], ps[:, 128:256], ACT.Copy)
                        if job == J_WIN:
                            last = A(gates[0:r, t, :], ps[:, 256:280], ACT.Sigmoid)
                    last.then_inc(*tell(t_act))

            def aux(slot):
                for i, (at, kind, n, e) in enumerate(AUX):
                    if at != slot or e != "a":
                        continue
                    src = bank[5 + i % 3]
                    own()
                    if kind == "hid":
                        act.wait_ge(aux_done, i + 1)
                        if n:
                            act.wait_ge(aux_done, AUX_AT[("ck", 0)] + 1)
                        link(A(norm[:, 31:32], src[:, 302:303], ACT.Copy))
                        A(aT[:, 0:302], src[:, 0:302], ACT.Silu, bias=norm[:, 31:32]).then_inc(*tell(aux_act))
                        continue
                    if kind == "dots":
                        d = DOTS.index(n)
                        if d >= 2:
                            act.wait_ge(score_added, d - 1)
                        act.wait_ge(aux_done, i + 1)
                        m = P * (n[0] + 1)
                        A(relu_d[:, d % 2, 0:m], src[:, 0:m], ACT.Relu, scale=IDX_SCALE).then_inc(*tell(aux_act))
                        continue
                    act.wait_ge(aux_done, i + 1)
                    if kind == "sdots":
                        A(relu_s[:, :], src[:, 0:NKS], ACT.Relu, scale=IDX_SCALE).then_inc(*tell(aux_act))
                        continue
                    if kind == "selx":
                        A(selS[:, n, :], src[:, 0:NKS], ACT.Copy).then_inc(*tell(aux_act))
                        continue
                    moves(kind, n, src, lambda o, x: A(o, x, ACT.Copy)).then_inc(*tell(aux_act))

            split_hi(0)
            split_hi(1)
            for job in range(G0):
                for n in before_evac(job):
                    split_hi(n)
                read_tiles(job)
                for n in after_evac(job):
                    split_hi(n)
                aux(job)
            aux(G0)

            act.wait_ge(aux_done, len(AUX))
            act.wait_ge(aux_dve, sum(x[3] == "v" for x in AUX))
            act.wait_ge(roped, NT * G0)
            for name in ("idx", "kv", "dkv", "win"):
                act.wait_ge(stored[name], 32)
            for i in range(len(UNITS) + LAG):
                if i < len(UNITS):
                    kind, b = UNITS[i][:2]
                    src = [bank[2 * (i % 2) + g] for g in range(2)]
                    s = stats[:, i % 4, :]
                    act.wait_ge(masked, i + 1)
                    own()
                    if i >= 4 and REAL[i - 4]:
                        act.wait_ge(pt_done, ORD[i - 3])
                    if kind == "K":
                        act.wait_ge(s_done, i + 1)
                        m = KV_ORDER.index((b, UNITS[i][2]))
                        if m >= 2:
                            act.wait_ge(s_done, UNITS.index(("S", *KV_ORDER[m - 2])) + 1)
                        A(kTs[:, m % 2, 2:4, :].rearrange("p s n -> p (s n)"), src[1][:, :], ACT.Copy)\
                            .then_inc(*tell(exped))
                    elif kind == "P":
                        n = NCP if b == CMP else P * (UNITS[i][3] + 1)
                        for g in range(2):
                            last = A(prob[:, i % 4, g, 0:n], src[g][:, 0:n], ACT.Exp, bias=s[:, 2 + g:3 + g],
                                     scale=SCALE, accum_out=s[:, 4 + g:5 + g])
                        last.then_inc(*tell(exped))
                    else:
                        n = NCS if b == CMP else NKS
                        A(prob[:, i % 4, 0, 0:n], src[0][:, 0:n], ACT.Exp, bias=s[:, 2:3], scale=SCALE,
                          accum_out=s[:, 4:5]).then_inc(*tell(exped))
                u = i - LAG
                if u >= 0 and REAL[u]:
                    kind, b = UNITS[u][:2]
                    act.wait_ge(pt_done, ORD[u] + 1)
                    own()
                    if ORD[u] >= 2:
                        act.wait_ge(pv_done, ORD[u] - 1)
                    pt = probT[:, ORD[u] % 2]
                    if kind == "P" and b == CMP:
                        x = A(pt[0:NCP, 0, 0:P], bank[4][0:NCP, 0:P], ACT.Copy)
                    elif kind == "P":
                        n = P * (UNITS[u][3] + 1)
                        x = A(pt[:, 0, 0:n], bank[4][:, 0:n], ACT.Copy)
                    elif b == CMP:
                        x = A(pt[0:NCS, 0, 0:P], bank[4][0:NCS, 0:P], ACT.Copy)
                    else:
                        A(pt[:, 0, 0:PAST], bank[4][:, 0:PAST], ACT.Copy)
                        x = A(pt[0:NS, 0, PAST:PAST + P], bank[4][0:NS, PAST:PAST + P], ACT.Copy)
                    x.then_inc(*tell(pt_act))

            for job in range(G0, len(JOBS)):
                g = job - G0
                kind, c = JOBS[job]
                for n in before_evac(job):
                    split_hi(n)
                if kind == "z":
                    for t in range(NT):
                        n = NT * c + t
                        tile_ready(act, job, t)
                        own()
                        if n >= 2:
                            act.wait_ge(z_mul, n - 1)
                        A(zs[:, n % 2, 0:512 if t < 4 else 4 * NS],
                          bank[t][:, :] if t < 4 else samples_bank(g)[:, 0:4 * NS], ACT.Silu).then_inc(*tell(g_act))
                        act.wait_ge(z_mul, n + 1)
                        A(part(oz[0], 4 * c, t), part(oT, 4 * c, t), ACT.Copy).then_inc(*tell(oz_hi))
                elif kind in ("mn", "md"):
                    dst = sg if kind == "mn" else sg2
                    if kind == "mn" and c == 0:
                        act.wait_ge(oz_lo, 2 * NT)
                        for t in range(NT):
                            src = (a["x_sample"].rearrange("s t n -> (s t) n") if t == 4
                                   else a["x_prompt"][0, P * t:P * t + P])
                            act.dma_start(yb[0:rows(t), t, :], src).then_inc(in_xy, 16)
                        act.dma_start(fgb[:, :], a["final_g"].rearrange("(a n) -> a n", a=1).to_broadcast([P, D]))\
                            .then_inc(in_fg, 16)
                    for t in range(NT):
                        tile_ready(act, job, t)
                        own()
                        if c == 1:
                            act.wait_ge(g_dve, GV[g - 3] + t + 1)
                        A(part(dst, 0, t), bank[t][:, :] if t < 4 else samples_bank(g)[:, 0:4 * NS]
                          .rearrange("p (b n) -> p b n", b=4), ACT.Sigmoid).then_inc(*tell(g_act))
                elif kind == "ud":
                    for t in range(NT):
                        act.wait_ge(m_made, NT * c + t + 1)
                        own()
                        A(part(mT[0], 4 * c, t), part(mt, 0, t), ACT.Copy).then_inc(*tell(mT_hi))
                elif kind == "y":
                    for t in range(NT):
                        r = rows(t)
                        act.wait_ge(y_sum, NT * c + t + 1)
                        own()
                        A(mt[0:r, 0, 0:512], yb[0:r, t, 512 * c:512 * c + 512], ACT.Square,
                          accum_out=norm[0:r, 2 * t + c:2 * t + c + 1]).then_inc(*tell(y_sq))
                        if c:
                            act.wait_ge(y_ms, t + 1)
                            A(norm[0:r, 18 + t:19 + t], norm[0:r, 12 + t:13 + t], ACT.Sqrt).then_inc(*tell(y_root))
                for n in after_evac(job):
                    split_hi(n)
                if kind == "ud" and c == 1:
                    for h in range(2):
                        act.wait_ge(mod_done, 5 + h)
                        A(mod_g[:, 512 * h:512 * h + 512], bank[5 + h][:, :], ACT.Copy).then_inc(*tell(mod_copied))

        @block.vector
        def _(dve):
            told = {}
            latest = []

            def tell(s):
                told[id(s)] = told.get(id(s), 0) + 1
                latest[:] = [s, told[id(s)]]
                return s, 1

            def own():
                if latest:
                    dve.wait_ge(*latest)

            def link(ins):
                ins.then_inc(*tell(dve_step))
                own()

            tt, ts, stt, cp = dve.tensor_tensor, dve.tensor_scalar, dve.scalar_tensor_tensor, dve.tensor_copy

            dve.wait_ge(c_turned, 1)
            dve.wait_ge(zeroed, 1)
            cp(cT[:, :, 0:9], bank[5][:, 0:72].rearrange("p (k n) -> p k n", k=KT)).then_inc(*tell(cT_made))
            dve.wait_ge(c_turned, 2)
            cp(gT[:, :], bank[6][:, 0:8])
            cp(peT[:, :], bank[6][:, 8:40]).then_inc(*tell(small_made))
            dve.wait_ge(squared, NT)
            ts(norm[:, 8:12], norm[:, 0:4], 1.0 / D, EPS, ALU.mult, ALU.add).then_inc(*tell(ms_made))
            ts(norm[0:NS, 12:13], norm[0:NS, 4:5], 1.0 / D, EPS, ALU.mult, ALU.add).then_inc(*tell(ms_made))
            dve.wait_ge(rooted, 1)
            link(dve.reciprocal(norm[:, 24:28], norm[:, 16:20]))
            link(dve.reciprocal(norm[0:NS, 28:29], norm[0:NS, 20:21]))
            for t in range(NT):
                r = rows(t)
                ts(xs[0:r, t, :], xs[0:r, t, :], norm[0:r, 24 + t:25 + t], None, ALU.mult).then_inc(*tell(xn_made))
            dve.wait_ge(small_made, 1)
            dve.wait_ge(ab_done, 1)
            mod_ps = bank[7][:, 0:256].rearrange("p (w k n) -> p w k n", w=2, k=KT)[:, :, :, 0:9]
            cp(AB[:, 0], mod_ps[:, 0])
            stt(out=AB[:, 1], in0=mod_ps[:, 1], scalar=1.0, in1=spread(gT[:, :], 2, 9), op0=ALU.add, op1=ALU.mult)\
                .then_inc(*tell(ab_made))
            dve.wait_ge(ab_made, 1)

            def lo_of_h(k):
                own()
                dve.wait_ge(h_hi, k + 1)
                dve.wait_ge(h_made, k + 1)
                if k == KT:
                    tmp = rope_b[:, 0, 0:KT * NS].rearrange("p (k n) -> p k n", k=KT)
                    tt(hT[1][:, :, SEQ:TOK], tmp, hT[0][:, :, SEQ:TOK].bitcast(F32), ALU.subtract).then_inc(*tell(h_lo))
                else:
                    tt(hT[1][:, k, 0:SEQ], rope_b[:, k % 2, :], hT[0][:, k, 0:SEQ].bitcast(F32), ALU.subtract)\
                        .then_inc(*tell(h_lo))

            for k in range(KT):
                dve.wait_ge(x_turned, k + 1)
                own()
                ts(rope_b[:, k % 2, :], bank[5 + k % 3][:, :], AB[:, 1, k, 0:1], AB[:, 0, k, 0:1], ALU.mult, ALU.add)\
                    .then_inc(*tell(h_made))
                if k:
                    lo_of_h(k - 1)
            lo_of_h(KT - 1)
            dve.wait_ge(x_turned, KT + 1)
            tmp = rope_b[:, 0, 0:KT * NS].rearrange("p (k s t) -> p k s t", k=KT, s=NSEQ)
            link(tt(tmp, bank[4][:, 0:KT * NS].rearrange("p (k s t) -> p k s t", k=KT, s=NSEQ),
                    spread(AB[:, 1, :, 1:9], 3, NEW), ALU.mult))
            tt(tmp, tmp, spread(AB[:, 0, :, 1:9], 3, NEW), ALU.add).then_inc(*tell(h_made))
            lo_of_h(KT)

            def split_lo(n):
                own()
                dve.wait_ge(hi_made, n + 1)
                arrived(dve, piece(n)[0])
                for dst, src, hi in split_views(n, 1):
                    last = tt(dst, src, hi.bitcast(F32), ALU.subtract)
                last.then_inc(*tell(lo_made))

            def read_tiles(job):
                c0, H = ROPED[job]
                if job == J_IDX:
                    dve.wait_ge(x_turned, KT + 1)
                if job == J_NQ:
                    dve.wait_ge(stored["idx"], 32)
                    dve.wait_ge(aux_done, aux_last_read(J_IDX))
                if job == J_DQ:
                    dve.wait_ge(stored["kv"], 32)
                    dve.wait_ge(aux_done, aux_last_read(J_KV))
                if job in (J_DKV, J_WIN):
                    dve.wait_ge(aux_done, aux_last_read(J_NQ))
                for t in range(NT):
                    r = rows(t)
                    n = NT * job + t
                    tile_ready(dve, job, t)
                    if ACT_READS[job]:
                        dve.wait_ge(t_act, act_tiles(job, t))
                    own()
                    if n >= 2:
                        dve.wait_ge(roped, n - 1)
                    x = bank[t][0:r, c0:c0 + HD * H]
                    ra = stg[0:r, STG[job], 512 * t + c0:512 * t + c0 + HD * H]
                    rb = rope_b[0:r, n % 2, 0:HD * H]
                    cos = tb("cos", r)[:, HD * t:HD * t + HD]
                    sin = tb("sin", r)[:, HD * t:HD * t + HD]
                    if H == 8:
                        x, ra, rb = by_group(x), by_pair(ra), by_pair(rb)
                        cos, sin = (spread(spread(y, 1, 4), 1, 2) for y in (cos, sin))
                    else:
                        x, ra, rb = (y.rearrange("p (h d) -> p h d", h=H) for y in (x, ra, rb))
                        cos, sin = (spread(y, 1, H) for y in (cos, sin))
                    tt(ra, x, cos, ALU.mult)
                    tt(rb[..., 0:32], x[..., 32:64], sin[..., 0:32], ALU.mult)
                    tt(rb[..., 32:64], x[..., 0:32], sin[..., 32:64], ALU.mult).then_inc(*tell(t_dve))

            def aux(slot):
                for i, (at, kind, n, e) in enumerate(AUX):
                    if at != slot:
                        continue
                    src = bank[5 + i % 3]
                    own()
                    if kind == "dots":
                        d = DOTS.index(n)
                        t, h = n
                        m = P * (t + 1)
                        aux_wait(dve, "dots", n)
                        dve.wait_ge(t_act, act_tiles(J_IDX, 4))
                        if d:
                            dve.wait_ge(score_added, d)
                        acc = tb("mrow")[:, SEQ - m:SEQ] if h == 0 else score[:, t - 1, 0:m]
                        stt(out=score[:, t - 1, 0:m], in0=relu_d[:, d % 2, 0:m], scalar=iw[:, t, h:h + 1], in1=acc,
                            op0=ALU.mult, op1=ALU.add).then_inc(*tell(score_added))
                        continue
                    if kind == "sdots":
                        aux_wait(dve, "sdots", 0)
                        dve.wait_ge(t_act, act_tiles(J_IDX, 4))
                        for h in range(4):
                            x = cp(iwr[NS * h:NS * h + NS, :], iw[0:NS, 4, h:h + 1])
                        link(x)
                        ts(relu_s[:, :], relu_s[:, :], iwr[:, 0:1], None, ALU.mult).then_inc(*tell(sdots_weighted))
                        continue
                    if e != "v":
                        continue
                    dve.wait_ge(aux_done, i + 1)
                    if kind == "ssum":
                        tt(scoreS[:, :], src[0:NS, 0:NKS], tb("midx", NS), ALU.add).then_inc(*tell(aux_dve))
                    elif kind == "grow":
                        link(tt(gtmp[:, :], src[:, 0:24], tb("headmask"), ALU.mult))
                        dve.tensor_reduce(grow[:, n, :], gtmp[:, :].rearrange("p (h b) -> p b h", b=3), AX.X, ALU.add)\
                            .then_inc(*tell(aux_dve))
                    elif kind == "si":
                        cp(qTi[:, :, SEQ:TOK], src[:, 0:2 * NS].rearrange("p (j n) -> p j n", j=2))
                        cp(kni[:, :], src[0:HD, 2 * NS:3 * NS]).then_inc(*tell(aux_dve))
                        aux_wait(dve, "si", 0)
                        dve.wait_ge(zeroed, 2)
                        for h in range(4):
                            x = qTi[64 * (h % 2):64 * (h % 2) + 64, h // 2, SEQ:TOK]
                            dst = bass.AP(iqz.tensor, iqz.offset + NS * h, [iqz.ap[0], [P + NEW, NSEQ], [1, NEW]])
                            cp(dst, x.rearrange("p (s t) -> p s t", s=NSEQ))
                            y = cp(iqa[:, NS * h:NS * h + NS], x)
                        y.then_inc(*tell(iq_laid))
                    else:
                        moves(kind, n, src, lambda o, x: cp(o, x)).then_inc(*tell(aux_dve))

            def take_top(row, n):
                link(dve.max(top8[0:n, :], row))
                link(dve.match_replace(out=row, in_to_replace=top8[0:n, :], in_values=row, imm_value=TAKEN))

            def rounds(t, count):
                for _ in range(count):
                    take_top(score[:, t - 1, 0:P * (t + 1)], P)

            def mask_rest(row):
                own()
                return ts(row, row, 0.99 * TAKEN, NEG, ALU.is_gt, ALU.mult)

            todo = [(t, 4) for t in (1, 2, 3) for _ in range(TOPK_P // 8 // 4)]

            def some_rounds():
                if todo:
                    t, count = todo.pop(0)
                    rounds(t, count)

            dve.wait_ge(zeroed, 2)
            split_lo(0)
            split_lo(1)
            for job in range(G0):
                for n in before_evac(job):
                    split_lo(n)
                    if job >= 3:
                        some_rounds()
                read_tiles(job)
                for n in after_evac(job):
                    split_lo(n)
                aux(job)
                if job == 2:
                    dve.wait_ge(aux_dve, sum(x[3] == "v" for x in AUX[:AUX_AT[("ssum", 0)] + 1]))
                    dve.wait_ge(score_added, len(DOTS))
                    for n in range(TOPK_S // 8):
                        take_top(scoreS[:, :], NS)
                    link(dve.max(top8[0:NS, :], scoreS[:, :]))
                    link(dve.memset(top8[0:NS, TOPK_S % 8:8], TAKEN))
                    link(dve.match_replace(out=scoreS[:, :], in_to_replace=top8[0:NS, :], in_values=scoreS[:, :],
                                           imm_value=TAKEN))
                    mask_rest(scoreS[:, :]).then_inc(*tell(sel_made))
                if job >= 2:
                    some_rounds()
            while todo:
                some_rounds()
            aux(G0)
            for t in (1, 2, 3):
                x = mask_rest(score[:, t - 1, 0:P * (t + 1)])
            link(x)
            dve.wait_ge(t_act, act_tiles(J_WIN, 4))
            gv = gates[:, 0, :].rearrange("p (h b) -> p h b", b=3)[:, :, 0]
            link(ts(gv, gv, tb("vis"), None, ALU.mult))

            for name in ("idx", "kv", "dkv", "win"):
                dve.wait_ge(stored[name], 32)
            dve.wait_ge(roped, NT * G0)
            dve.wait_ge(aux_act, sum(x[3] == "a" for x in AUX))

            def mask_max(u):
                own()
                kind, b = UNITS[u][:2]
                src = [bank[2 * (u % 2) + g] for g in range(2)]
                s = stats[:, u % 4, :]
                dve.wait_ge(s_done, u + 1)
                if kind == "K":
                    m = KV_ORDER.index((b, UNITS[u][2]))
                    if m >= 2:
                        dve.wait_ge(s_done, UNITS.index(("S", *KV_ORDER[m - 2])) + 1)
                    cp(kTs[:, m % 2, 0:2, :].rearrange("p s n -> p (s n)"), src[0][:, :]).then_inc(*tell(masked))
                    return
                if u >= 4 and REAL[u - 4]:
                    dve.wait_ge(scaled, ORD[u - 3])
                if kind == "P":
                    t = UNITS[u][3]
                    n = NCP if b == CMP else P * (t + 1)
                    m = (tb("mcmp")[:, 32 * t:32 * t + NCP] if b == CMP else
                         score[:, t - 1, 0:n] if b == DSA and t else tb("mrow")[:, SEQ - n:SEQ])
                    g2 = 2
                else:
                    T = UNITS[u][2]
                    n = NCS if b == CMP else NKS
                    m = (tb("mrow")[:, 0:n] if b == CMP else selS[:, T, :] if b == DSA
                         else tb("msamp")[:, NKS * T:NKS * T + NKS])
                    g2 = 1
                for g in range(g2):
                    x = dve.tensor_tensor_reduce(out=src[g][:, 0:n], in0=src[g][:, 0:n], in1=m, scale=1.0, scalar=TAKEN,
                                                 op0=ALU.add, op1=ALU.max, accum_out=s[:, g:g + 1])
                link(x)
                ts(s[:, 2:2 + g2], s[:, 0:g2], -SCALE, None, ALU.mult).then_inc(*tell(masked))

            def gate_over_sum(u):
                own()
                if not REAL[u]:
                    return
                kind, b = UNITS[u][:2]
                s = stats[:, u % 4, :]
                dve.wait_ge(exped, u + 1)
                g2 = 2 if kind == "P" else 1
                if b == DSA:
                    dve.reciprocal(s[:, 6:6 + g2], s[:, 4:4 + g2]).then_inc(*tell(r_made))
                    return
                link(dve.reciprocal(s[:, 6:6 + g2], s[:, 4:4 + g2]))
                if kind == "P":
                    j, t = UNITS[u][2:]
                    gate = gates[:, t, :].rearrange("p (g j b) -> p g j b", g=2, j=4)[:, :, j, b]
                else:
                    gate = grow[:, UNITS[u][2], b:b + 1]
                tt(s[:, 6:6 + g2], s[:, 6:6 + g2], gate, ALU.mult).then_inc(*tell(r_made))

            def copy_turned(u):
                if UNITS[u][0] != "P":
                    return
                own()
                kind, b = UNITS[u][:2]
                dve.wait_ge(pt_done, ORD[u] + 1)
                if ORD[u] >= 2:
                    dve.wait_ge(pv_done, ORD[u] - 1)
                pt = probT[:, ORD[u] % 2]
                if kind == "P" and b == CMP:
                    x = cp(pt[0:NCP, 1, 0:P], bank[5][0:NCP, 0:P])
                else:
                    n = P * (UNITS[u][3] + 1)
                    x = cp(pt[:, 1, 0:n], bank[5][:, 0:n])
                x.then_inc(*tell(pt_dve))

            def copy_out(w):
                own()
                kind, j = OWNERS[w]
                src = bank[6 + w % 2]
                dve.wait_ge(pv_done, ORD[LAST_OF[w]] + 1)
                if kind in "nd":
                    cp(oT[:, j + (4 if kind == "d" else 0), 0:SEQ], src[:, :]).then_inc(*tell(o_copied))
                    return
                b0 = 4 if kind == "D" else 0
                for g in range(2):
                    x = cp(oT[64 * g:64 * g + 64, b0:b0 + 4, SEQ + 16 * j:SEQ + 16 * j + 16]
                           .rearrange("p j (s t) -> p j s t", s=4),
                           src[64 * g:64 * g + 64, 0:P].rearrange("p (s g j t) -> p g j s t", s=4, g=2, j=4)[:, g])
                x.then_inc(*tell(o_copied))

            for i in range(len(UNITS) + LAG + 2):
                if i < len(UNITS):
                    mask_max(i)
                if 0 <= i - 1 < len(UNITS):
                    gate_over_sum(i - 1)
                if 0 <= i - LAG < len(UNITS):
                    copy_turned(i - LAG)
                for w, u in LAST_OF.items():
                    if u == i - LAG - 2:
                        copy_out(w)
            dve.wait_ge(o_copied, len(OWNERS))
            for job in range(G0, len(JOBS)):
                g = job - G0
                kind, c = JOBS[job]
                for n in before_evac(job):
                    split_lo(n)
                if kind == "z":
                    for t in range(NT):
                        n = NT * c + t
                        dve.wait_ge(g_act, GA[g] + t + 1)
                        own()
                        x = part(oT, 4 * c, t)
                        z = (zs[:, n % 2, 0:512] if t < 4 else
                             zs[:, n % 2, 0:4 * NS].rearrange("p (b n) -> p b n", b=4))
                        tt(x, x, z, ALU.mult).then_inc(*tell(z_mul))
                        own()
                        dve.wait_ge(oz_hi, n + 1)
                        tt(part(oz[1], 4 * c, t), x, part(oz[0], 4 * c, t).bitcast(F32), ALU.subtract)\
                            .then_inc(*tell(oz_lo))
                elif kind in ("un", "ud"):
                    gate = sg if kind == "un" else sg2
                    dst = mt if kind == "un" else gate
                    dve.wait_ge(g_act, GA[g])
                    for t in range(NT):
                        tile_ready(dve, job, t)
                        own()
                        if kind == "un" and c:
                            dve.wait_ge(mT_hi, t + 1)
                        x = bank[t][:, :] if t < 4 else samples_bank(g)[:, 0:4 * NS].rearrange("p (b n) -> p b n", b=4)
                        tt(part(dst, 0, t), x, part(gate, 0, t), ALU.mult).then_inc(*tell(g_dve))
                        if kind == "ud":
                            own()
                            tt(part(mt, 0, t), part(mt, 0, t), part(gate, 0, t), ALU.add).then_inc(*tell(m_made))
                            own()
                            dve.wait_ge(mT_hi, NT * c + t + 1)
                            tt(part(mT[1], 4 * c, t), part(mt, 0, t), part(mT[0], 4 * c, t).bitcast(F32),
                               ALU.subtract).then_inc(*tell(mT_lo))
                elif kind == "y":
                    if c == 0:
                        dve.wait_ge(in_xy, 16 * NT)
                    for t in range(NT):
                        r = rows(t)
                        tile_ready(dve, job, t)
                        own()
                        gate = (gateS if t == 4 else gateP)[0:r, 512 * c:512 * c + 512]
                        tmp = sg[0:r, t % 4, 0:512]
                        tt(tmp, bank[t][0:r, :], gate, ALU.mult).then_inc(*tell(g_dve))
                        dve.wait_ge(g_dve, GV[g] + t + 1)
                        y = yb[0:r, t, 512 * c:512 * c + 512]
                        tt(y, y, tmp, ALU.add).then_inc(*tell(y_sum))
                        if c:
                            dve.wait_ge(y_sq, NT + t + 1)
                            link(tt(norm[0:r, 12 + t:13 + t], norm[0:r, 2 * t:2 * t + 1],
                                    norm[0:r, 2 * t + 1:2 * t + 2], ALU.add))
                            ts(norm[0:r, 12 + t:13 + t], norm[0:r, 12 + t:13 + t], 1.0 / D, EPS, ALU.mult, ALU.add)\
                                .then_inc(*tell(y_ms))
                            dve.wait_ge(y_root, t + 1)
                            link(dve.reciprocal(norm[0:r, 24 + t:25 + t], norm[0:r, 18 + t:19 + t]))
                            if t == 0:
                                dve.wait_ge(in_fg, 16)
                            stt(out=yb[0:r, t, :], in0=yb[0:r, t, :], scalar=norm[0:r, 24 + t:25 + t],
                                in1=fgb[0:r, :], op0=ALU.mult, op1=ALU.mult).then_inc(*tell(y_out))
                for n in after_evac(job):
                    split_lo(n)
                if kind == "ud" and c == 1:
                    dve.wait_ge(ab_done, 2)
                    cp(gateP[:, 0:512], bank[5][:, :])
                    cp(gateP[:, 512:1024], bank[6][:, :])
                    cp(gateS[:, 0:512], bank[7][0:NS, :]).then_inc(*tell(gate_made))
                    dve.wait_ge(ab_done, 3)
                    link(cp(gateS[:, 512:1024], bank[7][0:NS, :]))


INPUTS = ["x_prompt", "x_sample", "cache_nsa_kv", "cache_dsa_kv", "cache_dsa_idx_k", "state_nsa_win_kv", "page_table",
          "c_prompt", "c_sample", "norm_g", "w_ada", "b_ada", "w_in", "cmp_pe", "cmp_w1", "cmp_w2", "w_up_nsa",
          "w_up_dsa", "w_out", "final_g"]
OUTPUTS = [("y_p", (1, SEQ, D)), ("y_s", (NSEQ, NEW, D)), ("nsa_p", (1, 1, SEQ, 4, 2, HD)),
           ("dsa_p", (1, 1, SEQ, 2, 2, HD)), ("idx_p", (1, 1, SEQ, HD)), ("win_p", (1, 1, SEQ, 2, 2, HD)),
           ("nsa_s", (1, NSEQ, NEW, 4, 2, HD)), ("dsa_s", (1, NSEQ, NEW, 2, 2, HD)), ("idx_s", (1, NSEQ, NEW, HD)),
           ("win_s", (1, NSEQ, PAST, 2, 2, HD))]


def kernel(**inputs):
    import numpy as np
    import concourse.bacc as bacc
    from concourse.bass_utils import run_bass_kernel_spmd

    nc = bacc.Bacc("TRN2", target_bir_lowering=False, num_devices=1)
    arrays, args, outs = {}, {}, {}
    for name in INPUTS + ["tables"]:
        x = tables() if name == "tables" else np.ascontiguousarray(inputs[name])
        arrays[f"in_{name}"] = x
        args[name] = nc.dram_tensor(f"in_{name}", x.shape, mybir.dt.from_np(x.dtype), kind="ExternalInput").ap()
    for name, shape in OUTPUTS:
        outs[name] = nc.dram_tensor(f"out_{name}", shape, F32, kind="ExternalOutput").ap()
    build(nc, args, outs)
    r = run_bass_kernel_spmd(nc, [arrays], core_ids=[0])
    return tuple(r.results[0][f"out_{name}"] for name, _ in OUTPUTS)
```

```python
from contextlib import ExitStack

import concourse.bass as bass
from concourse import mybir

F32 = mybir.dt.float32
F32R = mybir.dt.float32r
I32 = mybir.dt.int32
ALU = mybir.AluOpType
ACT = mybir.ActivationFunctionType
AX = mybir.AxisListType

P = 128
D = 1024
KT = D // P
SEQ = 512
NSEQ, NEW = 8, 4
NS = NSEQ * NEW
TOK = SEQ + NS
PAST = 256
PAGE = 128
NPAGE = PAST // PAGE
NT = 5
HD = 64
TOPK_P, TOPK_S = 128, (PAST + NEW) // 4
NCP, NCS = 31, 15
R_PROMPT, R_PE, R_SAMPLE = (0, 21 * P), (4 * P, 25 * P), 5 * P
R_BASE = (0, R_SAMPLE)
R_ALL = 26 * P + 16
R_COLS = 21 * 16


def r_col(n, at):
    return (at - R_BASE[n]) // 8


NKS = PAST + NS
EPS = 1e-6
NEG = -1e30
TAKEN = -3e38
SCALE = HD ** -0.5
IDX_SCALE = (HD ** -0.5) * (4 ** -0.5)

NQ, NKV, DQ, DKV, IQ, NZ, DZ, MG = 0, 512, 1816, 2328, 2584, 1304, 2908, 3420
T_JOBS = [(IQ, 324), (NKV, 512), (NQ, 512), (DQ, 512), (NKV + 512, 280), (DKV, 256)]
J_IDX, J_KV, J_NQ, J_DQ, J_WIN, J_DKV = range(6)
ROPED = [(0, 5), (256, 2), (0, 8), (0, 8), (0, 2), (0, 2)]
STG = [0, 1, 0, 1, 2, 0]
ACT_READS = [1, 1, 1, 0, 1, 1]
CMP, SLC, WIN, DSA = range(4)
PLAIN, ROT, DSAQ = range(3)
G_JOBS = [("z", 0), ("z", 1)] + [(k, c) for c in range(2) for k in ("mn", "un", "md", "ud")] + [("y", 0), ("y", 1)]
JOBS = [("T", i) for i in range(6)] + G_JOBS
G_EVAC = {"z": "a", "mn": "a", "md": "a", "un": "v", "ud": "v", "y": "v"}

PIECES = [2 if k in ("un", "ud") else 4 for k, _ in JOBS]
FIRST = [sum(PIECES[:i]) for i in range(len(JOBS) + 1)]

AUX = [(1, "qi", 0, "a"), (1, "qi", 1, "v"), (1, "ki", 0, "a"), (1, "si", 0, "v"),
       (2, "cmpT", 0, "v"), (2, "cmpT", 1, "a"), (2, "k", SLC, "a"), (2, "kn", SLC, "v"),
       (2, "ikT", 0, "a"), (2, "ikT", 1, "v"), (2, "ikT", 2, "a"), (2, "ikT", 3, "v"), (2, "sdots", 0, "a")]
AUX += [(2, "dots", (t, h), "a") for t in (1, 2, 3) for h in range(4)]
AUX += [(2, "ssum", 0, "v")]
for _s in (0, 1):
    AUX += [(3, "q", (_s, j), "av"[j % 2]) for j in range(4)] + [(3, "qs", _s, "v")]
AUX += [(3, "raw", (0, n), "av"[n % 2]) for n in range(4)] + [(3, "hid", 0, "a"), (3, "ck", 0, "v")]
AUX += [(4, "q", (2, j), "av"[j % 2]) for j in range(4)] + [(4, "qs", 2, "v")]
AUX += [(4, "raw", (1, n), "av"[n % 2]) for n in range(4)] + [(4, "hid", 1, "a"), (4, "cvp", 0, "v"),
                                                             (4, "cvs", 0, "a"), (4, "cvs", 1, "v")]
AUX += [(5, "selx", 0, "a"), (5, "selx", 1, "a"), (5, "k", WIN, "a"), (5, "kn", WIN, "v"),
        (5, "grow", 0, "v"), (5, "grow", 1, "v")]
AUX_AT = {(k, n): i for i, (_, k, n, _) in enumerate(AUX)}



def _plan_units():
    units = []
    for T in range(2):
        for j in (2 * T, 2 * T + 1):
            if j % 2:
                units.append(("K", SLC, T))
            units.extend(("P", b, j, t) for t in (3, 2, 1, 0) for b in (CMP, SLC, WIN))
        units += [("S", CMP, T), ("K", WIN, T), ("S", SLC, T), ("S", WIN, T)]
    units.insert(4, ("T", DSA))
    for j in range(4):
        if j in (2, 3):
            units.append(("K", DSA, j - 2))
        units.extend(("P", DSA, j, t) for t in (3, 2, 1, 0))
    return units + [("S", DSA, 0), ("S", DSA, 1)]


UNITS = _plan_units()
LAG = 3
OWNERS = [("n", 0), ("n", 1), ("N", 0), ("n", 2), ("n", 3), ("N", 1), ("d", 0), ("d", 1), ("d", 2), ("d", 3), ("D", 0),
          ("D", 1)]


def owner(u):
    kind, b = u[0], u[1]
    return OWNERS.index((("nd" if kind == "P" else "ND")[b == DSA], u[2]))


REAL = [u[0] in "PS" for u in UNITS]
ORD = [sum(REAL[:i]) for i in range(len(UNITS) + 1)]
ORDP = [sum(u[0] == "P" for u in UNITS[:i]) for i in range(len(UNITS) + 1)]
AT = [sum(1 + (u[0] != "S") for u in UNITS[:i]) for i in range(len(UNITS) + 1)]
SIG = [sum(1 + (u[0] == "P") for u in UNITS[:i]) for i in range(len(UNITS) + 1)]
TURNS = [sum({"P": 2, "S": 1}.get(u[0], 0) for u in UNITS[:i]) for i in range(len(UNITS) + 1)]
LAST_OF = {owner(u): i for i, u in enumerate(UNITS) if REAL[i]}
FIRST_OF = {w: min(i for i, u in enumerate(UNITS) if REAL[i] and owner(u) == w) for w in LAST_OF}
KV_ORDER = [(u[1], u[2]) for u in UNITS if u[0] == "K"]


def kv_slot(b, T):
    return KV_ORDER.index((b, T)) % 2


LOADS = []


def _plan_loads():
    def weights(job):
        LOADS.extend(("w", job, e) for e in range(PIECES[job] // 2))

    LOADS.extend(("ada", c, e) for c in range(4) for e in range(2))
    for job in range(2):
        weights(job)
    for job, extra in ((2, [("idxraw", 0, 0)]), (3, [("cmpraw", 0, 0), ("cmpw", 0, 0)]),
                       (4, [("cmpw", 1, 0)])):
        LOADS.extend([("w", job, 0), *extra, ("w", job, 1)])
    weights(5)
    LOADS.append(("w", 6, 0))
    LOADS.extend(("kv", b, T) for b, T in KV_ORDER)
    LOADS.append(("w", 6, 1))
    for job in range(7, len(JOBS) - 1):
        if job == len(JOBS) - 2:
            LOADS.append(("w", job, 0))
            LOADS.extend(("ada", c, e) for c in (4, 5) for e in range(2))
            LOADS.append(("w", job, 1))
        else:
            weights(job)
    weights(len(JOBS) - 1)


_plan_loads()
SLOTS = 2
LOAD_AT = {key: i for i, key in enumerate(LOADS)}
PE_LOADS = [i for i, key in enumerate(LOADS) if key[0] != "w"]
N_DMAS = {"w": 1, "ada": 1, "idxraw": 16, "cmpraw": 16, "cmpw": 1, "kv": 8}


def dmas_of(key):
    if key[0] == "w" and JOBS[key[1]][0] in ("un", "ud", "z"):
        return 2
    if key[0] == "kv" and key[1] == WIN:
        return 1
    return N_DMAS[key[0]]


TAB = {}


def _table_columns():
    at = 0
    for name, n in (("ident", 128), ("mrow", 512), ("mcmp", 128), ("cos", 320), ("sin", 320), ("msamp", 576),
                    ("expand", 256), ("headmask", 24), ("hsum", 32), ("midx", 288), ("gsel", 9), ("bselp", 128),
                    ("bsels", 32), ("vis", 1), ("brow", 192)):
        TAB[name] = (at, at + n)
        at += n
    return at


NTAB = _table_columns()


def tables():
    import numpy as np
    t = np.zeros((P, NTAB), np.float32)

    def put(name, x):
        t[:x.shape[0], TAB[name][0]:TAB[name][0] + x.shape[1]] = x

    p = np.arange(P)
    put("ident", np.eye(P))
    put("mrow", np.concatenate([np.zeros((P, 384)), np.where(p[None] <= p[:, None], 0.0, NEG)], 1))
    ends = np.arange(NCP) * 16 + 31
    mc = np.zeros((P, 4, 32))
    for i in range(4):
        mc[:, i, :NCP] = np.where(ends[None] <= (i * P + p)[:, None], 0.0, NEG)
    put("mcmp", mc.reshape(P, 128))
    inv = np.float32(10000.0) ** (-np.arange(32, dtype=np.float32) / np.float32(32))
    pos = np.zeros((NT, P), np.float32)
    pos[:4] = np.arange(SEQ).reshape(4, P)
    pos[4, :NS] = PAST + np.arange(NS) % NEW
    ang = (pos[:, :, None] * inv).astype(np.float32).transpose(1, 0, 2).astype(np.float64)
    put("cos", np.concatenate([np.cos(ang), np.cos(ang)], 2).reshape(P, 320))
    put("sin", np.concatenate([-np.sin(ang), np.sin(ang)], 2).reshape(P, 320))
    s4, g, j, tt = p // 32, p % 32 // 16, p % 16 // 4, p % 4
    ks, kt = np.arange(NS) // NEW, np.arange(NS) % NEW
    ms = np.zeros((P, 2, NKS))
    ex = np.zeros((NS, 2, P))
    for T in range(2):
        seq = 4 * T + s4
        ms[:, T, PAST:] = np.where((ks[None] == seq[:, None]) & (kt[None] <= tt[:, None]), 0.0, NEG)
        ex[seq * NEW + tt, T, p] = 1
    put("msamp", ms.reshape(P, -1))
    put("expand", ex.reshape(NS, -1))
    hm = np.zeros((P, 8, 3))
    hm[p, g * 4 + j] = 1
    put("headmask", hm.reshape(P, 24))
    put("hsum", np.tile(np.eye(32), (4, 1)))
    mi = np.zeros((NS, NKS))
    mi[:, PAST:] = np.where((ks[None] == ks[:, None]) & (kt[None] <= kt[:, None]), 0.0, NEG)
    put("midx", mi)
    gs = np.zeros((P, 9))
    bp, bs = np.zeros((P, P)), np.zeros((P, NS))
    for q in range(4):
        gs[32 * q + np.arange(9), np.arange(9)] = 1
        bp[32 * q] = 1
        bs[32 * q + 1 + ks, np.arange(NS)] = 1
    put("gsel", gs)
    put("bselp", bp)
    put("bsels", bs)
    put("vis", (p >= 31).astype(np.float32)[:, None])
    put("brow", np.repeat(np.eye(6), 32, axis=1))
    return t


def spread(ap, at, n):
    dims = [list(d) for d in ap.ap]
    return bass.AP(ap.tensor, ap.offset, dims[:at] + [[0, n]] + dims[at:])


def build(nc, a, o):
    ctx = ExitStack()
    with ctx:
        def sb(name, shape, dt=F32, st=ctx):
            return st.enter_context(nc.sbuf_tensor(name, shape, dt))

        def sem(name):
            return ctx.enter_context(nc.semaphore(name))

        tab = sb("tab", [P, NTAB])

        def tb(name, rows=P):
            return tab[0:rows, TAB[name][0]:TAB[name][1]]

        ident = tb("ident")
        hT = [sb(f"hT_{n}", [P, KT, TOK], F32R) for n in ("hi", "lo")]
        stage = [sb(f"stage{i}", [P, 2048]) for i in range(SLOTS)]
        whl = [[sb(f"w_{n}{i}", [P, 2, 512], F32R) for i in range(2)] for n in ("hi", "lo")]
        cT = sb("cT", [P, KT, 32])
        bada = sb("b_ada", [6, 512])
        gates = sb("gates", [P, NT, 24])
        grow = sb("gate_rows", [P, 2, 3])
        gtmp = sb("gate_tmp", [P, 24])
        gT = sb("norm_gT", [P, KT])
        norm = sb("norm_stats", [P, 32])
        stats = sb("softmax_stats", [P, 4, 8])
        pages = sb("page_row", [1, NSEQ * NPAGE], I32)
        top8 = sb("top8", [P, 8])

        abc = ExitStack()
        qT = [sb(f"qT_{n}", [P, 4, SEQ], F32, abc) for n in ("plain", "rot", "dsa")]
        qTi = sb("qT_idx", [P, 2, TOK], F32, abc)
        kz2 = sb("kz_win_dsa", [P, 2, 2, SEQ], F32, abc)
        kz = [None, sb("kz_slc", [P, 2, SEQ], F32, abc), kz2[:, 0], kz2[:, 1]]
        kzi = sb("kz_idx", [P, 2, SEQ], F32, abc)
        knew = [None] + [sb(f"k_new_{n}", [P, NS], F32, abc) for n in ("slc", "win", "dsa")]
        kni = sb("k_new_idx", [HD, NS], F32, abc)
        ckz = sb("ckz", [P, 2, 32], F32, abc)
        ckS = sb("ck_sample", [P, NSEQ * NCS], F32, abc)
        cvP = sb("cv_prompt", [32, P], F32, abc)
        cvS = sb("cv_sample", [16, NSEQ, P], F32, abc)
        V = [None] + [sb(f"v_{n}", [P, NT, P], F32, abc) for n in ("slc", "win", "dsa")]
        qS = [sb(f"q_sample_{n}", [P, 2 * P], F32, abc) for n in ("plain", "rot", "dsa")]
        score = sb("score", [P, 3, SEQ], F32, abc)
        scoreS = sb("score_sample", [NS, NKS], F32, abc)
        selS = sb("sel_sample", [P, 2, NKS], F32, abc)
        ab = ExitStack()
        stg = sb("staging", [P, 3, NT * 512], F32, ab)
        rope_b = sb("rope_b", [P, 2, 512], F32, ab)
        rT = sb("rT", [P, R_ALL], F32, ab)
        aT = sb("cmp_act", [P, R_COLS], F32, ab)
        w2 = sb("cmp_w2", [P, 2, HD], F32, ab)
        relu_d = sb("relu_dots", [P, 2, 512], F32, ab)
        relu_s = sb("relu_dots_sample", [P, NKS], F32, ab)
        iw = sb("idx_w", [P, NT, 4], F32, ab)
        iwr = sb("idx_w_rows", [P, 1], F32, ab)
        AB = sb("mod_AB", [P, 2, KT, 9], F32, ab)
        ab.close()
        c_only = ExitStack()
        oT = sb("oT", [P, 8, TOK], F32, c_only)
        probT = sb("probT", [P, 2, 2, SEQ], F32, c_only)
        kTs = sb("kT_sample", [P, 2, 4, PAST], F32, c_only)
        sb("rope_tail", [P, 256], F32, c_only)
        prob = sb("prob", [P, 4, 2, SEQ], F32, c_only)
        c_only.close()
        abc.close()
        d = ctx
        oz = [sb(f"oz_{n}", [P, 8, TOK], F32R, d) for n in ("hi", "lo")]
        zs = sb("silu_z", [P, 2, TOK], F32, d)
        mT = [sb(f"mT_{n}", [P, KT, TOK], F32R, d) for n in ("hi", "lo")]
        sg = sb("sig_n", [P, 4, TOK], F32, d)
        sg2 = sb("sig_d", [P, 4, TOK], F32, d)
        mt = sb("merged", [P, 4, TOK], F32, d)
        yb = sb("y", [P, NT, D], F32, d)
        fgb = sb("final_g", [P, D], F32, d)
        gateP = sb("gate_prompt", [P, D], F32, d)
        xs = stg[:, :, :].rearrange("p a n -> p (a n)")[:, 0:NT * D].rearrange("p (t n) -> p t n", t=NT)
        mod = stg[:, 2, 0:2048]
        rb_all = rope_b[:, :, :].rearrange("p a n -> p (a n)")
        c_raw = relu_d[:, :, :].rearrange("p a n -> p (a n)")
        rTs = rT[:, R_SAMPLE:R_SAMPLE + 16 * P]
        raw_v = kz2[:, :, :, :].rearrange("p a g n -> p (a g n)")
        ng8 = aT[0:8, 0:P]
        pe32 = aT[0:32, P:2 * P]
        ikTs = rTs[0:HD, :]
        iqz = qT[DSAQ][0:HD, 0:2, :].rearrange("p j n -> p (j n)")
        iqa = qT[DSAQ][0:HD, 2, 0:P]
        gateS = sg2[:, :, :].rearrange("p a n -> p (a n)")[0:NS, 0:D]
        mod_g = zs[:, :, :].rearrange("p a n -> p (a n)")[:, 0:D]

        psum = ctx.enter_context(nc.psum_tensor("psum", [P, 8, 512], F32))
        bank = [psum[:, i, :] for i in range(8)]

        in_tab, in_c, in_small, in_w2, in_raw_v = sem("in_tab"), sem("in_c"), sem("in_small"), sem("in_w2"), sem("in_raw_v")
        in_x = [sem(f"in_x{t}") for t in range(NT)]
        in_pages = sem("in_pages")
        loaded = [sem(f"loaded{i}") for i in range(SLOTS)]
        pe_freed = sem("pe_freed")
        hi_made, lo_made = sem("hi_made"), sem("lo_made")
        piece_used = sem("piece_used")
        act_step, dve_step, pool_step = sem("act_step"), sem("dve_step"), sem("pool_step")
        zeroed = sem("zeroed")
        csilu, c_turned, cT_made = sem("csilu"), sem("c_turned"), sem("cT_made")
        small_made = sem("small_made")
        mod_done, mod_copied = sem("mod_done"), sem("mod_copied")
        ab_done, ab_made = sem("ab_done"), sem("ab_made")
        squared, ms_made, rooted, xn_made = sem("squared"), sem("ms_made"), sem("rooted"), sem("xn_made")
        x_turned, h_made, h_hi, h_lo = sem("x_turned"), sem("h_made"), sem("h_hi"), sem("h_lo")
        t_done, t_dve, t_act = sem("t_done"), sem("t_dve"), sem("t_act")
        roped = sem("roped")
        aux_done, aux_act, aux_dve = sem("aux_done"), sem("aux_act"), sem("aux_dve")
        score_added = sem("score_added")
        iq_laid, sdots_weighted, sel_made = sem("iq_laid"), sem("sdots_weighted"), sem("sel_made")
        stored = {n: sem(f"stored_{n}") for n in ("idx", "kv", "dkv", "win", "old", "y")}
        s_done, masked, exped = sem("scores_done"), sem("masked"), sem("exped")
        r_made, scaled = sem("r_made"), sem("scaled")
        pt_done, pt_act, pt_dve = sem("pt_done"), sem("pt_act"), sem("pt_dve")
        pv_done, o_copied = sem("pv_done"), sem("o_copied")
        g_done, g_act, g_dve = sem("g_done"), sem("g_act"), sem("g_dve")
        z_mul, oz_hi, oz_lo = sem("z_mul"), sem("oz_hi"), sem("oz_lo")
        m_made, mT_hi, mT_lo = sem("m_made"), sem("mT_hi"), sem("mT_lo")
        in_fg, in_xy = sem("in_fg"), sem("in_xy")
        gate_made = sem("gate_made")
        y_sum, y_sq, y_ms, y_root, y_out = sem("y_sum"), sem("y_sq"), sem("y_ms"), sem("y_root"), sem("y_out")

        def arrived(eng, key):
            i = LOAD_AT[key]
            eng.wait_ge(loaded[i % SLOTS], 16 * sum(dmas_of(LOADS[k]) for k in range(i % SLOTS, i + 1, SLOTS)))

        def staged(key):
            return stage[LOAD_AT[key] % SLOTS]

        def rows(t):
            return NS if t == 4 else P

        def act_tiles(job, t):
            return 5 * sum(ACT_READS[:job]) + (t + 1 if ACT_READS[job] else 0)

        def aux_wait(eng, kind, n):
            i = AUX_AT[(kind, n)]
            e = AUX[i][3]
            eng.wait_ge(aux_act if e == "a" else aux_dve, sum(x[3] == e for x in AUX[:i + 1]))

        def aux_last_read(job):
            return sum(x[0] <= job + 1 for x in AUX)

        def job_pieces(job):
            return range(FIRST[job], FIRST[job + 1])

        G0 = 6
        POOL_SPLITS = FIRST[G0]
        GA, GV = [0], [0]
        for kind, _ in G_JOBS:
            tiles = NT if kind == "y" else 4
            GA.append(GA[-1] + tiles * (G_EVAC[kind] == "a"))
            GV.append(GV[-1] + tiles * (G_EVAC[kind] == "v"))

        def g_read(eng, g, t):
            if G_EVAC[G_JOBS[g][0]] == "a":
                eng.wait_ge(g_act, GA[g] + t + 1)
            else:
                eng.wait_ge(g_dve, GV[g] + t + 1)

        def g_signals(g):
            return sum({"y": 4, "un": 2, "ud": 2}.get(k, 0) for k, _ in G_JOBS[:g])

        def tile_ready(eng, job, t):
            g = job - G0
            if g >= 0 and G_JOBS[g][0] != "y":
                each = blocks_of(job)
                if t % each == each - 1:
                    eng.wait_ge(piece_used, FIRST[job] + t // each + 1)
                else:
                    eng.wait_ge(g_done, g_signals(g) + t // 2 + 1)
            elif t == NT - 1:
                eng.wait_ge(piece_used, FIRST[job + 1])
            elif g < 0:
                eng.wait_ge(t_done, (NT - 1) * job + t + 1)
            else:
                eng.wait_ge(g_done, g_signals(g) + t + 1)

        def halves(x):
            return x.rearrange("p (h n) -> p h n", h=2)

        def part(x, b):
            return halves(x[:, b, :])

        def product(job, t):
            b = 4 * (job - G0) + t
            return psum[:, 2 * (b % 4):2 * (b % 4) + 2, 0:TOK // 2]

        def piece(n):
            job = max(j for j in range(len(JOBS)) if FIRST[j] <= n)
            q = n - FIRST[job]
            w = T_JOBS[JOBS[job][1]][1] if JOBS[job][0] == "T" else 512
            return ("w", job, q // 2), q % 2, w

        def w_part(which, n, w):
            return whl[which][n % 2][:, :, :].rearrange("p k n -> p (k n)")[:, 0:2 * w]

        def split_views(n, which):
            key, half, w = piece(n)
            kind = JOBS[key[1]][0]
            dst, hi = w_part(which, n, w), w_part(0, n, w)
            if kind == "T" or kind == "y":
                return [(dst, staged(key)[:, 2 * w * half:2 * w * half + 2 * w], hi)]
            m = {"z": 64, "un": 256, "ud": 256}.get(kind, P)
            src = staged(key)[:, :].rearrange("p (k n) -> p k n", n=2 * m)[:, :, half * m:half * m + m]
            return [(dst.rearrange("p (k n) -> p k n", n=m), src, hi.rearrange("p (k n) -> p k n", n=m))]

        def blocks_of(job):
            return 2 if JOBS[job][0] in ("un", "ud") else 1

        def by_group(x):
            return x.rearrange("p (g j d) -> p g j d", g=2, j=4)

        def by_pair(x):
            return x.rearrange("p (j g d) -> p g j d", g=2, j=4)

        def before_evac(job):
            return range(FIRST[job] + 2, min(FIRST[job + 1] + 1, FIRST[-1]))

        def after_evac(job):
            return range(min(FIRST[job + 1] + 1, FIRST[-1]), min(FIRST[job + 1] + 2, FIRST[-1]))

        def moves(kind, n, src, copy):
            if kind == "qi":
                return copy(qTi[:, n, 0:SEQ], src[:, :])
            if kind in ("ki", "k"):
                dst = kzi if kind == "ki" else kz[n]
                hi = 0 if kind == "ki" else 64
                copy(dst[0:64, 0, :], src[0:64, :])
                return copy(dst[64:128, 1, :], src[hi:hi + 64, :])
            if kind == "kn":
                return copy(knew[n][:, :], src[:, 0:NS])
            if kind == "cmpT":
                v = src[:, :].rearrange("p (q r) -> p r q", r=2)
                for g in range(2):
                    for r in range(2):
                        at = R_PROMPT[n] + PAST * g
                        last = copy(rT[64 * r:64 * r + 64, at:at + PAST], v[64 * g:64 * g + 64, r, :])
                return last
            if kind == "ikT":
                return copy(ikTs[:, 512 * n:512 * n + 512], src[0:HD, :])
            if kind == "q":
                return copy(qT[n[0]][:, n[1], :], src[:, :])
            if kind == "qs":
                for g in range(2):
                    v = qS[n][64 * g:64 * g + 64, :].rearrange("p (s g j t) -> p g j s t", s=NSEQ, g=2, j=4)
                    last = copy(v[:, g], src[64 * g:64 * g + 64, 0:P].rearrange("p (j s t) -> p j s t", j=4, s=NSEQ))
                return last
            if kind == "raw":
                v = rTs[:, 512 * n[1]:512 * n[1] + 512].rearrange("p (s g q) -> p s g q", s=2, g=2)
                w = src[:, :].rearrange("p (s r q) -> p s r q", s=2, r=2)
                for g in range(2):
                    for r in range(2):
                        last = copy(v[64 * r:64 * r + 64, :, g, :], w[64 * g:64 * g + 64, :, r, :])
                return last
            if kind == "ck":
                copy(ckz[0:64, 0, 0:NCP], src[0:64, 0:NCP])
                copy(ckz[64:128, 1, 0:NCP], src[64:128, 0:NCP])
                return copy(ckS[:, :], src[:, 32:32 + NSEQ * NCS])
            if kind == "cvp":
                return copy(cvP[0:NCP, :], src[0:NCP, 0:P])
            assert kind == "cvs"
            return copy(cvS[0:NCS, 4 * n:4 * n + 4, :], src[0:NCS, :].rearrange("p (s c) -> p s c", s=4))

        DOTS = [x[2] for x in AUX if x[1] == "dots"]

        block = ctx.enter_context(nc.Block())

        @block.sync
        def _(sp):
            sp.dma_start(pages[:, :], a["page_table"].rearrange("s n -> (s n)").rearrange("(a n) -> a n", a=1)).then_inc(in_pages, 16)
            page_of = {}

            def page(i):
                return sp.value_load(pages[0:1, i:i + 1], min_val=0, max_val=a["cache_nsa_kv"].shape[1] - 1)

            def compressed_rows(st, x, count):
                v = st.rearrange("p (s r c) -> p s r c", s=NSEQ, r=2)
                for n in range(16):
                    h = n % NPAGE
                    sp.dma_start(v[64 * h:64 * h + 64, n // NPAGE, :, :],
                                 a["cache_nsa_kv"][0, bass.ds(page(n), 1), :, x]
                                 .rearrange("a (q r) g d -> (a q) r (g d)", r=2)).then_inc(count, 16)

            for i, key in enumerate(LOADS):
                kind, x, e = key
                if key == ("w", 4, 0):
                    compressed_rows(raw_v, 1, in_raw_v)
                if i >= SLOTS:
                    old = LOADS[i - SLOTS]
                    if old[0] == "w":
                        sp.wait_ge(lo_made, FIRST[old[1]] + 2 * old[2] + 2)
                    else:
                        sp.wait_ge(pe_freed, PE_LOADS.index(i - SLOTS) + 1)
                s = i % SLOTS
                st = stage[s]
                if kind == "w":
                    job, c = JOBS[x]
                    if job in ("un", "ud"):
                        w = a["w_up_nsa" if job == "un" else "w_up_dsa"][0]
                        for g in range(2):
                            sp.dma_start(st[64 * g:64 * g + 64, :].rearrange("p (j n) -> p j n", j=4),
                                         w[256 * g:256 * g + 256, 512 * c:512 * c + 512]
                                         .rearrange("(j d) n -> d j n", j=4)).then_inc(loaded[s], 16)
                        continue
                    if job == "T":
                        w, at, n = a["w_in"][0], *T_JOBS[c]
                    elif job == "z":
                        w, at, n = a["w_in"][0], (NZ, DZ)[c], 512
                    elif job == "y":
                        w, at, n = a["w_out"][0], 512 * c, 512
                    else:
                        w, at, n = a["w_in"][0], MG + (D if job == "md" else 0) + 512 * c, 512
                    if job == "z":
                        v = st[:, :].rearrange("p (k g n) -> p k g n", k=KT, g=2)
                        for g in range(2):
                            lo = at + 256 * g + P * e
                            sp.dma_start(v[:, :, g, :], w[:, lo:lo + P].rearrange("(k p) n -> p k n", p=P))\
                                .then_inc(loaded[s], 16)
                    elif job in ("mn", "md"):
                        sp.dma_start(st[:, :].rearrange("p (k n) -> p k n", k=KT),
                                     w[:, at + 256 * e:at + 256 * e + 256].rearrange("(k p) n -> p k n", p=P))\
                            .then_inc(loaded[s], 16)
                    else:
                        sp.dma_start(st[:, 0:4 * n].rearrange("p (k n) -> p k n", k=4),
                                     w[512 * e:512 * e + 512, at:at + n].rearrange("(k p) n -> p k n", p=P))\
                            .then_inc(loaded[s], 16)
                elif kind == "ada":
                    sp.dma_start(st[:, :].rearrange("p (k n) -> p k n", k=4),
                                 a["w_ada"][0][512 * e:512 * e + 512, 512 * x:512 * x + 512]
                                 .rearrange("(k p) n -> p k n", p=P)).then_inc(loaded[s], 16)
                elif kind == "cmpw":
                    sp.dma_start(st[:, :].rearrange("p (i n) -> p i n", i=16),
                                 a["cmp_w1"][0][x].rearrange("(i p) n -> p i n", p=P)).then_inc(loaded[s], 16)
                elif kind == "idxraw":
                    sp.wait_ge(in_pages, 16)
                    v = st[:, 0:16 * HD].rearrange("p (n c) -> p n c", n=16)
                    for n in range(16):
                        sp.dma_start(v[:, n, :], a["cache_dsa_idx_k"][0, bass.ds(page(n), 1)]
                                     .rearrange("a p c -> (a p) c")).then_inc(loaded[s], 16)
                elif kind == "cmpraw":
                    compressed_rows(st[:, :], 0, loaded[s])
                else:
                    v = st[:, :].rearrange("p (n c) -> p n c", n=8)
                    if x == WIN:
                        sp.dma_start(v, a["state_nsa_win_kv"][0, 4 * e:4 * e + 4]
                                     .rearrange("s (h p) x g d -> p (s h) (x g d)", p=PAGE)).then_inc(loaded[s], 16)
                        continue
                    for n in range(8):
                        pg = bass.ds(page(8 * e + n), 1)
                        src = a["cache_nsa_kv"][0, pg, :, 2:4] if x == SLC else a["cache_dsa_kv"][0, pg]
                        sp.dma_start(v[:, n, :], src.rearrange("a p x g d -> (a p) (x g d)")).then_inc(loaded[s], 16)

        @block.gpsimd
        def _(pool):
            pool.memset(cT[:, :, :], 0.0)
            pool.memset(rT[:, R_PE[0]:R_PE[0] + P], 0.0)
            pool.memset(rT[:, R_PE[1]:R_ALL], 0.0).then_inc(zeroed, 1)
            pool.memset(kz[SLC][:, :, :], 0.0)
            pool.memset(kzi[:, :, :], 0.0)
            pool.memset(ckz[:, :, :], 0.0)
            for q in qS:
                pool.memset(q[:, :], 0.0)
            pool.memset(iqz, 0.0).then_inc(zeroed, 1)
            pool.dma_start(o["win_s"][0, :, 0:PAST - NEW].rearrange("s w x g d -> s (w x g d)"),
                           a["state_nsa_win_kv"][0, :, NEW:PAST].rearrange("s w x g d -> s (w x g d)"))\
                .then_inc(stored["old"], 16)

            def stores(name, buf, n, prompt, sample):
                pool.dma_start(prompt, stg[:, buf, :].rearrange("p (t n) -> p t n", t=NT)[:, 0:4, n[0]:n[1]])\
                    .then_inc(stored[name], 16)
                pool.dma_start(sample, stg[0:NS, buf, 4 * 512 + n[0]:4 * 512 + n[1]]).then_inc(stored[name], 16)

            def split_lo(n):
                pool.wait_ge(hi_made, n + 1)
                arrived(pool, piece(n)[0])
                if n >= 2:
                    pool.wait_ge(piece_used, n - 1)
                for dst, src, hi in split_views(n, 1):
                    last = pool.tensor_tensor(dst, src, hi.bitcast(F32), ALU.subtract)
                last.then_inc(lo_made, 1)

            split_lo(0)
            split_lo(1)
            for job in range(6):
                for n in before_evac(job):
                    if n < POOL_SPLITS:
                        split_lo(n)
                c0, H = ROPED[job]
                for t in range(NT):
                    r = rows(t)
                    n = NT * job + t
                    dst = stg[0:r, STG[job], 512 * t + c0:512 * t + c0 + HD * H]
                    pool.wait_ge(t_dve, n + 1)
                    pool.tensor_tensor(dst, dst, rope_b[0:r, n % 2, 0:HD * H], ALU.add).then_inc(roped, 1)
                for m in after_evac(job):
                    if m < POOL_SPLITS:
                        split_lo(m)
                if job == 4:
                    pool.wait_ge(aux_done, AUX_AT[("raw", (1, 3))] + 1)
                    pool.memset(raw_v, 0.0).then_inc(zeroed, 1)
                pool.wait_ge(roped, NT * (job + 1))
                if job == J_IDX:
                    stores("idx", 0, (256, 320), o["idx_p"][0, 0].rearrange("(t p) c -> p t c", p=P),
                           o["idx_s"][0].rearrange("s t c -> (s t) c"))
                elif job == J_KV:
                    pool.wait_ge(t_act, act_tiles(J_KV, 4))
                    stores("kv", 1, (0, 512), o["nsa_p"][0, 0].rearrange("(t p) x g d -> p t (x g d)", p=P),
                           o["nsa_s"][0].rearrange("s t x g d -> (s t) (x g d)"))
                elif job == J_DKV:
                    pool.wait_ge(t_act, act_tiles(J_DKV, 4))
                    stores("dkv", 0, (0, 256), o["dsa_p"][0, 0].rearrange("(t p) x g d -> p t (x g d)", p=P),
                           o["dsa_s"][0].rearrange("s t x g d -> (s t) (x g d)"))
                elif job == J_WIN:
                    pool.wait_ge(t_act, act_tiles(J_WIN, 4))
                    stores("win", 2, (0, 256), o["win_p"][0, 0].rearrange("(t p) x g d -> p t (x g d)", p=P),
                           o["win_s"][0, :, PAST - NEW:PAST].rearrange("s t x g d -> s t (x g d)"))

            for u, unit in enumerate(UNITS):
                if not REAL[u]:
                    continue
                kind, b, _, t = (*unit, 0)[:4]
                pool.wait_ge(r_made, ORD[u] + 1)
                pool.wait_ge(exped, SIG[u + 1])
                s = stats[:, u % 4, :]
                if kind == "P":
                    n = NCP if b == CMP else P * (t + 1)
                    for g in range(2):
                        pool.tensor_scalar(prob[:, u % 4, g, 0:n], prob[:, u % 4, g, 0:n], s[:, 6 + g:7 + g], 1.0,
                                           ALU.mult, ALU.mult).then_inc(scaled, 1)
                else:
                    n = NCS if b == CMP else NKS
                    pool.tensor_scalar(prob[:, u % 4, 0, 0:n], prob[:, u % 4, 0, 0:n], s[:, 6:7], 1.0, ALU.mult,
                                       ALU.mult).then_inc(scaled, 1)

            for t in range(NT):
                pool.wait_ge(y_out, t + 1)
                dst = o["y_s"].rearrange("s t n -> (s t) n") if t == 4 else o["y_p"][0, P * t:P * t + P]
                pool.dma_start(dst, yb[0:rows(t), t, :]).then_inc(stored["y"], 16)
            pool.wait_ge(stored["y"], 16 * NT)
            for name in ("idx", "kv", "dkv", "win"):
                pool.wait_ge(stored[name], 32)
            pool.wait_ge(stored["old"], 16)

        @block.tensor
        def _(pe):
            mm = pe.matmul

            def three(out, left, right, first, last, **kw):
                mm(out, left[0], right[0], start=first, stop=False, skip_group_check=True)
                mm(out, left[1], right[0], start=False, stop=False, skip_group_check=True)
                return mm(out, left[0], right[1], start=False, stop=last, skip_group_check=True)

            pe.wait_ge(in_tab, 16)
            pe.wait_ge(csilu, 1)
            for k in range(KT):
                last = pe.transpose(bank[5][:, 9 * k:9 * k + 9], rb_all[0:9, P * k:P * k + P], ident[0:9, 0:9])
            last.then_inc(c_turned, 1)
            pe.wait_ge(in_small, 48)
            pe.transpose(bank[6][:, 0:8], ng8, ident[0:8, 0:8])
            pe.transpose(bank[6][:, 8:40], pe32, ident[0:32, 0:32]).then_inc(c_turned, 1)

            def modulation(c, out):
                mm(out[0:32, :], tb("brow", 6)[:, 32 * c:32 * c + 32], bada[:, :], start=True, stop=False,
                   skip_group_check=True)
                for e in range(2):
                    arrived(pe, ("ada", c, e))
                    w = staged(("ada", c, e))[:, :].rearrange("p (k n) -> p k n", k=4)
                    for k in range(4):
                        last = mm(out[32 * k:32 * k + 32, :], cT[:, 4 * e + k, :], w[:, k, :],
                                  start=(e == 0 and k > 0), stop=(e == 1), skip_group_check=True)
                    last.then_inc(pe_freed, 1)

            pe.wait_ge(cT_made, 1)
            for c in range(4):
                modulation(c, bank[c])
                pe.wait_ge(pe_freed, 2 * c + 2)
                pe.nop().then_inc(mod_done, 1)
            pe.wait_ge(mod_copied, 4)
            for w in range(2):
                for k in range(KT):
                    last = mm(bank[7][:, 16 * (w * KT + k):16 * (w * KT + k) + 9],
                              mod[:, D * w + P * k:D * w + P * k + P], tb("gsel"), start=True, stop=True)
            last.then_inc(ab_done, 1)
            for t in range(NT):
                pe.wait_ge(xn_made, t + 1)
            pe.wait_ge(small_made, 1)
            for k in range(KT):
                if k == 2:
                    pe.wait_ge(ab_made, 1)
                if k >= 3:
                    pe.wait_ge(h_made, k - 2)
                for t in range(4):
                    last = pe.transpose(bank[5 + k % 3][:, P * t:P * t + P], xs[:, t, P * k:P * k + P], ident)
                last.then_inc(x_turned, 1)
            for k in range(KT):
                last = pe.transpose(bank[4][:, NS * k:NS * k + NS], xs[0:NS, 4, P * k:P * k + P], ident[0:NS, 0:NS])
            last.then_inc(x_turned, 1)

            def token_major(job, left):
                for n in range(FIRST[job], FIRST[job + 1]):
                    pe.wait_ge(lo_made, n + 1)
                    q = n - FIRST[job]
                    _, _, w = piece(n)
                    final = n == FIRST[job + 1] - 1
                    for t in range(NT):
                        r = rows(t)
                        if q == 0 and 0 < job < G0:
                            pe.wait_ge(t_dve, NT * (job - 1) + t + 1)
                        if q == 0 and JOBS[job] == ("y", 1):
                            g_read(pe, job - G0 - 1, t)
                        for i in range(2):
                            k = 2 * q + i
                            last = three(bank[t][0:r, 0:w], [x[:, k, P * t:P * t + r] for x in left],
                                         [w_part(x, n, w)[:, i * w:i * w + w] for x in range(2)],
                                         q == 0 and i == 0, final and i == 1)
                        if final and t < NT - 1:
                            last.then_inc(t_done if job < G0 else g_done, 1)
                    last.then_inc(piece_used, 1)
                    if q == 0 and job < G0:
                        aux(job)

            def feature_major(job):
                kind, c = JOBS[job]
                g = job - G0
                each = blocks_of(job)
                tiles = KT // each
                for n in range(FIRST[job], FIRST[job + 1]):
                    pe.wait_ge(lo_made, n + 1)
                    if n == FIRST[job] and kind in ("un", "ud"):
                        pe.wait_ge(oz_lo, 4 if kind == "un" else 8)
                    left = [w_part(x, n, 512).rearrange("p (k n) -> p k n", k=tiles) for x in range(2)]
                    for x in range(each):
                        b = each * (n - FIRST[job]) + x
                        if g:
                            g_read(pe, g - 1, b)
                        elif b == 2:
                            pe.wait_ge(pt_act, ORD[-1])
                            pe.wait_ge(pt_dve, ORDP[-1])
                        elif b == 3:
                            pe.wait_ge(o_copied, len(OWNERS))
                        out = product(job, b)
                        for k in range(tiles):
                            mov = [y[:, k + (4 if kind == "ud" else 0), :] for y in (oz if each == 2 else hT)]
                            for w, m in ((0, 0), (1, 0), (0, 1)):
                                for h in range(2):
                                    last = mm(out[:, h, :], left[w][:, k, P * x:P * x + P], halves(mov[m])[:, h, :],
                                              start=(k == 0 and w + m == 0), stop=(k == tiles - 1 and m == 1),
                                              skip_group_check=True)
                        if x < each - 1:
                            last.then_inc(g_done, 1)
                    last.then_inc(piece_used, 1)

            def stg_tile(buf, t):
                return stg[0:rows(t), buf, 512 * t:512 * t + 512]

            def turn_tiles(out, pick, m=P):
                for t in range(4):
                    last = pe.transpose(out[0:m, P * t:P * t + P], pick(t), ident)
                return last

            def aux(slot):
                for i, (at, kind, n, _) in enumerate(AUX):
                    if at != slot:
                        continue
                    out = bank[5 + i % 3]
                    if i >= 3:
                        e = AUX[i - 3][3]
                        pe.wait_ge(aux_act if e == "a" else aux_dve, sum(x[3] == e for x in AUX[:i - 2]))
                    if kind == "qi":
                        pe.wait_ge(roped, NT * (J_IDX + 1))
                        last = turn_tiles(out, lambda t: stg_tile(0, t)[:, P * n:P * n + P])
                    elif kind == "ki":
                        last = turn_tiles(out, lambda t: stg_tile(0, t)[:, 256:320], HD)
                    elif kind == "si":
                        src = stg_tile(0, 4)
                        pe.transpose(out[:, 0:NS], src[:, 0:P], ident[0:NS, 0:NS])
                        pe.transpose(out[:, NS:2 * NS], src[:, P:2 * P], ident[0:NS, 0:NS])
                        last = pe.transpose(out[0:HD, 2 * NS:3 * NS], src[:, 256:320], ident[0:NS, 0:NS])
                    elif kind == "cmpT":
                        pe.wait_ge(t_act, act_tiles(J_KV, 4))
                        last = turn_tiles(out, lambda t: stg_tile(1, t)[:, P * n:P * n + P])
                    elif kind in ("k", "kn"):
                        job, c0 = {SLC: (J_KV, 256), DSA: (J_DKV, 0), WIN: (J_WIN, 0)}[n]
                        pe.wait_ge(roped, NT * (job + 1))
                        if kind == "k":
                            last = turn_tiles(out, lambda t: stg_tile(STG[job], t)[:, c0:c0 + P])
                        else:
                            last = pe.transpose(out[:, 0:NS], stg_tile(STG[job], 4)[:, c0:c0 + P], ident[0:NS, 0:NS])
                    elif kind == "ikT":
                        arrived(pe, ("idxraw", 0, 0))
                        src = staged(("idxraw", 0, 0))[:, 0:16 * HD].rearrange("p (n c) -> p n c", n=16)
                        for m in range(4):
                            last = pe.transpose(out[0:HD, P * m:P * m + P], src[:, 4 * n + m, :], ident)
                        if n == 3:
                            last.then_inc(pe_freed, 1)
                            pe.wait_ge(pe_freed, PE_LOADS.index(LOAD_AT[("idxraw", 0, 0)]) + 1)
                            last = pe.nop()
                    elif kind == "sdots":
                        pe.wait_ge(iq_laid, 1)
                        for m in range(4):
                            aux_wait(pe, "ikT", m)
                        for s in range(NSEQ):
                            mm(out[:, 0:PAST], iqz[:, P * s:P * s + P], ikTs[:, PAST * s:PAST * s + PAST],
                               start=(s == 0), stop=(s == NSEQ - 1))
                        last = mm(out[:, PAST:NKS], iqa, kni[:, :], start=True, stop=True)
                    elif kind == "ssum":
                        pe.wait_ge(sdots_weighted, 1)
                        last = mm(out[0:NS, 0:NKS], tb("hsum"), relu_s[:, :], start=True, stop=True)
                    elif kind == "dots":
                        t, h = n
                        aux_wait(pe, "qi", h // 2)
                        aux_wait(pe, "ki", 0)
                        last = mm(out[:, 0:P * (t + 1)], qTi[:, h // 2, P * t:P * t + P],
                                  kzi[:, h % 2, 0:P * (t + 1)], start=True, stop=True)
                    elif kind in ("q", "qs"):
                        which, j = n if kind == "q" else (n, 0)
                        job, buf = {PLAIN: (J_NQ, 2), ROT: (J_NQ, 0), DSAQ: (J_DQ, 1)}[which]
                        if which == PLAIN:
                            pe.wait_ge(t_act, act_tiles(J_NQ, 4))
                        else:
                            pe.wait_ge(roped, NT * (job + 1))

                        def pair(t, j):
                            return stg_tile(buf, t)[:, P * j:P * j + P]
                        if kind == "q":
                            last = turn_tiles(out, lambda t: pair(t, j))
                        else:
                            for j in range(4):
                                last = pe.transpose(out[:, NS * j:NS * j + NS], pair(4, j), ident[0:NS, 0:NS])
                    elif kind == "raw":
                        s, m = n
                        if s:
                            pe.wait_ge(in_raw_v, 16 * 16)
                            src = raw_v
                        else:
                            arrived(pe, ("cmpraw", s, 0))
                            src = staged(("cmpraw", s, 0))[:, :]
                        src = src.rearrange("p (s r c) -> p s r c", s=NSEQ, r=2)
                        for x in range(4):
                            last = pe.transpose(out[:, P * x:P * x + P], src[:, 2 * m + x // 2, x % 2, :], ident)
                        if m == 3 and s == 0:
                            last.then_inc(pe_freed, 1)
                            pe.wait_ge(pe_freed, PE_LOADS.index(LOAD_AT[("cmpraw", s, 0)]) + 1)
                            last = pe.nop()
                    elif kind == "hid":
                        arrived(pe, ("cmpw", n, 0))
                        for m in range(4):
                            aux_wait(pe, "raw", (n, m))
                        aux_wait(pe, "cmpT", 0)
                        aux_wait(pe, "cmpT", 1)
                        w1 = staged(("cmpw", n, 0))[:, :].rearrange("p (i n) -> p i n", i=16)
                        for i in range(16):
                            at = R_BASE[n] + i
                            last = mm(out[:, 0:R_COLS], w1[:, i, :], rT[:, at:at + 21 * P]
                                      .rearrange("p (x c) -> p x c", c=P)[:, :, 0:121:8], start=(i == 0), stop=(i == 15))
                        last.then_inc(pe_freed, 1)
                        pe.wait_ge(pe_freed, PE_LOADS.index(LOAD_AT[("cmpw", n, 0)]) + 1)
                        last = pe.nop()
                    elif kind == "ck":
                        aux_wait(pe, "hid", 0)
                        pe.wait_ge(in_w2, 16)
                        for g in range(2):
                            mm(out[64 * g:64 * g + 64, 0:NCP], w2[:, 0, :], aT[:, 32 * g:32 * g + NCP],
                               start=True, stop=True)
                            last = mm(out[64 * g:64 * g + 64, 32:32 + NSEQ * NCS], w2[:, 0, :],
                                      aT[:, r_col(0, R_SAMPLE):R_COLS]
                                      .rearrange("p (s g n) -> p s g n", s=NSEQ, g=2)[:, :, g, 0:NCS],
                                      start=True, stop=True)
                    elif kind == "cvp":
                        aux_wait(pe, "hid", 1)
                        for g in range(2):
                            at = r_col(1, R_PROMPT[1]) + 32 * g
                            last = mm(out[0:NCP, HD * g:HD * g + HD], aT[:, at:at + NCP],
                                      w2[:, 1, :], start=True, stop=True)
                    elif kind == "cvs":
                        for x in range(8):
                            at = 16 * (8 * n + x)
                            last = mm(out[0:NCS, HD * x:HD * x + HD], aT[:, at:at + NCS], w2[:, 1, :],
                                      start=True, stop=True)
                    elif kind == "selx":
                        pe.wait_ge(sel_made, 1)
                        last = mm(out[:, 0:NKS], tb("expand", NS)[:, P * n:P * n + P], scoreS[:, :], start=True,
                                  stop=True)
                    elif kind == "grow":
                        pe.wait_ge(t_act, act_tiles(J_WIN, 4))
                        last = mm(out[:, 0:24], tb("expand", NS)[:, P * n:P * n + P], gates[0:NS, 4, :], start=True,
                                  stop=True)
                    last.then_inc(aux_done, 1)

            pe.wait_ge(h_lo, 9)
            for job in range(G0):
                token_major(job, hT)

            def keys(b, t):
                return NCP if b == CMP else P * (t + 1)

            def bank_free(h):
                if h < 4:
                    pe.wait_ge(t_dve, NT * (G0 - 1) + h + 1)
                    return
                u = max(i for i in range(len(UNITS)) if AT[i] <= h - 4)
                if UNITS[u][0] in "KT":
                    pe.wait_ge(exped if h - 4 > AT[u] else masked, SIG[u] + 1)
                else:
                    pe.wait_ge(exped, SIG[u] + h - 4 - AT[u] + 1)

            def scores(u):
                unit = UNITS[u]
                kind, b = unit[:2]
                out = [bank[(AT[u] + g) % 4] for g in range(2)]
                bank_free(AT[u])
                if kind in "PS" and b == DSA:
                    n = UNITS.index(("T", DSA))
                    pe.wait_ge(exped, SIG[n + 1])
                    pe.wait_ge(masked, SIG[n + 1])
                    pe.wait_ge(t_act, act_tiles(J_DKV, 4))
                if kind == "T":
                    pe.wait_ge(roped, NT * (J_DKV + 1))
                    turn_tiles(out[0], lambda t: stg_tile(STG[J_DKV], t)[:, 0:P]).then_inc(s_done, 1)
                    bank_free(AT[u] + 1)
                    pe.transpose(out[1][:, 0:NS], stg_tile(STG[J_DKV], 4)[:, 0:P], ident[0:NS, 0:NS]).then_inc(s_done, 1)
                elif kind == "P":
                    j, t = unit[2:]
                    left = qT[PLAIN if b == CMP else ROT if b < DSA else DSAQ][:, j, P * t:P * t + P]
                    for g in range(2):
                        if g:
                            bank_free(AT[u] + 1)
                        right = ckz[:, g, 0:NCP] if b == CMP else kz[b][:, g, 0:P * (t + 1)]
                        mm(out[g][:, 0:keys(b, t)], left, right, start=True, stop=True).then_inc(s_done, 1)
                elif kind == "K":
                    key = ("kv", b, unit[2])
                    arrived(pe, key)
                    raw = staged(key)[:, :].rearrange("p (n c) -> p n c", n=8)
                    for g in range(2):
                        if g:
                            bank_free(AT[u] + 1)
                        for n in range(4):
                            last = pe.transpose(out[g][:, P * n:P * n + P], raw[:, 4 * g + n, 0:P], ident)
                        last.then_inc(s_done, 1)
                else:
                    T = unit[2]
                    q = qS[PLAIN if b == CMP else ROT if b < DSA else DSAQ][:, P * T:P * T + P]
                    if b != CMP:
                        n = UNITS.index(("K", b, T))
                        pe.wait_ge(exped, SIG[n + 1])
                        pe.wait_ge(masked, SIG[n + 1])
                    for s in range(4):
                        right = (ckS[:, NCS * (4 * T + s):NCS * (4 * T + s) + NCS] if b == CMP
                                 else kTs[:, kv_slot(b, T), s, :])
                        last = mm(out[0][32 * s:32 * s + 32, 0:NCS if b == CMP else PAST], q[:, 32 * s:32 * s + 32],
                                  right, start=True, stop=True)
                    if b != CMP:
                        last = mm(out[0][:, PAST:NKS], q, knew[b][:, :], start=True, stop=True)
                    last.then_inc(s_done, 1)

            def turn(u):
                unit = UNITS[u]
                if not REAL[u]:
                    return
                kind, b = unit[:2]
                src = prob[:, u % 4]
                for g in range(2 if kind == "P" else 1):
                    pe.wait_ge(scaled, TURNS[u] + g + 1)
                    if g and ORDP[u]:
                        pe.wait_ge(pt_dve, ORDP[u])
                    elif not g and ORD[u]:
                        pe.wait_ge(pt_act, ORD[u])
                    if kind == "P" and b != CMP:
                        for n in range(unit[3] + 1):
                            last = pe.transpose(bank[4 + g][:, P * n:P * n + P], src[:, g, P * n:P * n + P], ident)
                    elif b == CMP:
                        n = NCP if kind == "P" else NCS
                        last = pe.transpose(bank[4 + g][0:n, 0:P], src[:, g, 0:n], ident)
                    else:
                        for n in range(2):
                            pe.transpose(bank[4][:, P * n:P * n + P], src[:, 0, P * n:P * n + P], ident)
                        last = pe.transpose(bank[4][0:NS, PAST:PAST + P], src[:, 0, PAST:NKS], ident)
                    last.then_inc(pt_done, 1)

            def values(u):
                unit = UNITS[u]
                if not REAL[u]:
                    return
                kind, b = unit[:2]
                w = owner(unit)
                out = bank[6 + w % 2]
                first = u == FIRST_OF[w]
                final = u == LAST_OF[w]
                pe.wait_ge(pt_act, ORD[u] + 1)
                pe.wait_ge(pt_dve, ORDP[u + 1])
                if first and w >= 2:
                    pe.wait_ge(o_copied, w - 1)
                pt = probT[:, ORD[u] % 2]
                if kind == "P":
                    t = unit[3]
                    blocks = [(n, P) for n in range(t + 1)] if b != CMP else [(0, NCP)]
                    for n, m in blocks:
                        for g in range(2):
                            v = cvP[0:m, HD * g:HD * g + HD] if b == CMP else V[b][:, n, HD * g:HD * g + HD]
                            last = mm(out[64 * g:64 * g + 64, P * t:P * t + P], v, pt[0:m, g, P * n:P * n + P],
                                      start=(first and n == 0), stop=final, skip_group_check=True)
                elif b == CMP:
                    for s in range(4):
                        last = mm(out[:, 32 * s:32 * s + 32], cvS[0:NCS, 4 * unit[2] + s, :],
                                  pt[0:NCS, 0, 32 * s:32 * s + 32], start=(first and s == 0), stop=final,
                                  skip_group_check=True)
                else:
                    T = unit[2]
                    mm(out[:, 0:P], V[b][0:NS, 4, :], pt[0:NS, 0, PAST:PAST + P], start=first, stop=False,
                       skip_group_check=True)
                    raw = staged(("kv", b, T))[:, :].rearrange("p (n c) -> p n c", n=8)
                    for s in range(4):
                        for n in range(2):
                            last = mm(out[:, 32 * s:32 * s + 32], raw[:, 2 * s + n, P:2 * P],
                                      pt[:, 0, P * n + 32 * s:P * n + 32 * s + 32], start=False, stop=final,
                                      skip_group_check=True)
                    last.then_inc(pe_freed, 1)
                    pe.wait_ge(pe_freed, PE_LOADS.index(LOAD_AT[("kv", b, T)]) + 1)
                    last = pe.nop()
                last.then_inc(pv_done, 1)

            pe.wait_ge(aux_act, sum(x[3] == "a" for x in AUX))
            pe.wait_ge(aux_dve, sum(x[3] == "v" for x in AUX))
            for i in range(len(UNITS) + LAG + 1):
                if i < len(UNITS):
                    scores(i)
                if 0 <= i - LAG < len(UNITS):
                    turn(i - LAG)
                if 0 <= i - LAG - 1 < len(UNITS):
                    values(i - LAG - 1)

            pe.wait_ge(exped, SIG[-1])
            for job in range(G0, len(JOBS)):
                if JOBS[job][0] == "y":
                    if JOBS[job][1] == 0:
                        g_read(pe, job - G0 - 1, 3)
                        g_read(pe, job - G0 - 2, 3)
                        for c in (4, 5):
                            modulation(c, bank[c + 1])
                            pe.wait_ge(pe_freed, len(PE_LOADS) - 2 * (5 - c))
                            pe.nop().then_inc(mod_done, 1)
                        pe.wait_ge(mod_copied, 6)
                        for c in range(2):
                            mm(bank[5 + c][:, :], tb("bselp"), mod_g[:, 512 * c:512 * c + 512], start=True, stop=True)
                        mm(bank[7][0:NS, :], tb("bsels"), mod_g[:, 0:512], start=True, stop=True).then_inc(ab_done, 1)
                        pe.wait_ge(gate_made, 1)
                        mm(bank[7][0:NS, :], tb("bsels"), mod_g[:, 512:1024], start=True, stop=True).then_inc(ab_done, 1)
                        pe.wait_ge(mT_lo, KT)
                    token_major(job, mT)
                else:
                    feature_major(job)

        @block.scalar
        def _(act):
            A = act.activation
            told = {}
            latest = []

            def tell(s):
                told[id(s)] = told.get(id(s), 0) + 1
                latest[:] = [s, told[id(s)]]
                return s, 1

            def own():
                if latest:
                    act.wait_ge(*latest)

            def link(ins):
                ins.then_inc(*tell(act_step))
                own()

            act.dma_start(c_raw[0:1, :], a["c_prompt"]).then_inc(in_c, 16)
            act.dma_start(c_raw[1:9, :], a["c_sample"]).then_inc(in_c, 16)
            act.dma_start(tab[:, :], a["tables"]).then_inc(in_tab, 16)
            act.dma_start(ng8, a["norm_g"].rearrange("l (k p) -> (l k) p", p=P)).then_inc(in_small, 16)
            act.dma_start(pe32, a["cmp_pe"][0].rearrange("s (i r) d -> (s i) (r d)", r=2)).then_inc(in_small, 16)
            act.dma_start(bada[:, :], a["b_ada"].rearrange("l (c n) -> (l c) n", c=6)).then_inc(in_small, 16)
            for t in range(NT):
                src = a["x_sample"].rearrange("s t n -> (s t) n") if t == 4 else a["x_prompt"][0, P * t:P * t + P]
                act.dma_start(xs[0:rows(t), t, :], src).then_inc(in_x[t], 16)
            act.dma_start(w2[:, :, :], a["cmp_w2"][0].rearrange("s p d -> p s d")).then_inc(in_w2, 16)
            act.wait_ge(in_c, 32)
            A(rb_all[0:9, :], c_raw[0:9, :], ACT.Silu).then_inc(*tell(csilu))
            for t in range(NT):
                act.wait_ge(in_x[t], 16)
                if t:
                    act.wait_ge(squared, t)
                A(rTs[0:rows(t), 0:D], xs[0:rows(t), t, :], ACT.Square, accum_out=norm[0:rows(t), t:t + 1])\
                    .then_inc(*tell(squared))
            act.wait_ge(ms_made, 2)
            A(norm[:, 16:20], norm[:, 8:12], ACT.Sqrt)
            A(norm[0:NS, 20:21], norm[0:NS, 12:13], ACT.Sqrt).then_inc(*tell(rooted))
            for c in range(4):
                act.wait_ge(mod_done, c + 1)
                A(mod[:, 512 * c:512 * c + 512], bank[c][:, :], ACT.Copy).then_inc(*tell(mod_copied))
            for k in range(KT):
                act.wait_ge(h_made, k + 1)
                own()
                A(hT[0][:, k, 0:SEQ], rope_b[:, k % 2, :], ACT.Copy).then_inc(*tell(h_hi))
            act.wait_ge(h_made, KT + 1)
            A(hT[0][:, :, SEQ:TOK], rope_b[:, 0, 0:KT * NS].rearrange("p (k n) -> p k n", k=KT), ACT.Copy)\
                .then_inc(*tell(h_hi))

            def split_hi(n):
                own()
                arrived(act, piece(n)[0])
                if n >= 2:
                    act.wait_ge(piece_used, n - 1)
                for dst, src, _ in split_views(n, 0):
                    last = A(dst, src, ACT.Copy)
                last.then_inc(*tell(hi_made))

            def read_tiles(job):
                if not ACT_READS[job]:
                    return
                if job == J_KV:
                    act.wait_ge(x_turned, KT + 1)
                if job == J_NQ:
                    act.wait_ge(ab_done, 1)
                if job == J_DKV:
                    act.wait_ge(aux_done, aux_last_read(J_NQ))
                if job == J_WIN:
                    act.wait_ge(aux_done, aux_last_read(J_NQ))
                for t in range(NT):
                    r = rows(t)
                    tile_ready(act, job, t)
                    own()
                    ps = bank[t][0:r, :]
                    st = stg[0:r, STG[job], 512 * t:512 * t + 512]
                    if job == J_IDX:
                        last = A(iw[0:r, t, :], ps[:, 320:324], ACT.Copy)
                    elif job == J_KV:
                        A(st[:, 0:256], ps[:, 0:256], ACT.Copy)
                        A(st[:, 384:512], ps[:, 384:512], ACT.Copy)
                        last = A(V[SLC][0:r, t, :], ps[:, 384:512], ACT.Copy)
                    elif job == J_NQ:
                        last = A(by_pair(stg[0:r, 2, 512 * t:512 * t + 512]), by_group(ps[:, :]), ACT.Copy)
                    else:
                        A(st[:, 128:256], ps[:, 128:256], ACT.Copy)
                        last = A(V[DSA if job == J_DKV else WIN][0:r, t, :], ps[:, 128:256], ACT.Copy)
                        if job == J_WIN:
                            last = A(gates[0:r, t, :], ps[:, 256:280], ACT.Sigmoid)
                    last.then_inc(*tell(t_act))

            def aux(slot):
                for i, (at, kind, n, e) in enumerate(AUX):
                    if at != slot or e != "a":
                        continue
                    src = bank[5 + i % 3]
                    own()
                    if kind == "hid":
                        act.wait_ge(aux_done, i + 1)
                        if n:
                            act.wait_ge(aux_done, AUX_AT[("ck", 0)] + 1)
                        at = r_col(n, R_PE[n])
                        link(A(norm[:, 31:32], src[:, at:at + 1], ACT.Copy))
                        A(aT[:, :], src[:, 0:R_COLS], ACT.Silu, bias=norm[:, 31:32]).then_inc(*tell(aux_act))
                        continue
                    if kind == "dots":
                        d = DOTS.index(n)
                        if d >= 2:
                            act.wait_ge(score_added, d - 1)
                        act.wait_ge(aux_done, i + 1)
                        m = P * (n[0] + 1)
                        A(relu_d[:, d % 2, 0:m], src[:, 0:m], ACT.Relu, scale=IDX_SCALE).then_inc(*tell(aux_act))
                        continue
                    act.wait_ge(aux_done, i + 1)
                    if kind == "k" and n == WIN:
                        act.wait_ge(zeroed, 3)
                    if kind == "sdots":
                        A(relu_s[:, :], src[:, 0:NKS], ACT.Relu, scale=IDX_SCALE).then_inc(*tell(aux_act))
                        continue
                    if kind == "selx":
                        A(selS[:, n, :], src[:, 0:NKS], ACT.Copy).then_inc(*tell(aux_act))
                        continue
                    moves(kind, n, src, lambda o, x: A(o, x, ACT.Copy)).then_inc(*tell(aux_act))

            split_hi(0)
            split_hi(1)
            for job in range(G0):
                aux(job)
                for n in before_evac(job):
                    split_hi(n)
                read_tiles(job)
                for n in after_evac(job):
                    split_hi(n)

            act.wait_ge(aux_done, len(AUX))
            act.wait_ge(aux_dve, sum(x[3] == "v" for x in AUX))
            for i in range(len(UNITS) + LAG):
                if i < len(UNITS):
                    kind, b = UNITS[i][:2]
                    src = [bank[(AT[i] + g) % 4] for g in range(2)]
                    s = stats[:, i % 4, :]
                    if i >= 4 and REAL[i - 4]:
                        act.wait_ge(pt_done, TURNS[i - 3])
                    if kind == "K":
                        act.wait_ge(s_done, AT[i] + 2)
                        act.wait_ge(roped, NT * G0)
                        own()
                        m = KV_ORDER.index((b, UNITS[i][2]))
                        if m >= 2:
                            act.wait_ge(s_done, AT[UNITS.index(("S", *KV_ORDER[m - 2])) + 1])
                        A(kTs[:, m % 2, 2:4, :].rearrange("p s n -> p (s n)"), src[1][:, :], ACT.Copy)\
                            .then_inc(*tell(exped))
                    elif kind == "T":
                        act.wait_ge(s_done, AT[i] + 2)
                        own()
                        A(knew[DSA][:, :], src[1][:, 0:NS], ACT.Copy).then_inc(*tell(exped))
                    else:
                        n = (P * (UNITS[i][3] + 1) if kind == "P" else NKS) if b != CMP else NCP if kind == "P" else NCS
                        for g in range(2 if kind == "P" else 1):
                            act.wait_ge(masked, SIG[i] + g + 1)
                            own()
                            A(prob[:, i % 4, g, 0:n], src[g][:, 0:n], ACT.Exp, bias=s[:, 2 + g:3 + g],
                              scale=-1.0, accum_out=s[:, 4 + g:5 + g]).then_inc(*tell(exped))
                u = i - LAG
                if u >= 0 and REAL[u]:
                    kind, b = UNITS[u][:2]
                    act.wait_ge(pt_done, TURNS[u] + 1)
                    if ORD[u] == 0:
                        act.wait_ge(stored["win"], 32)
                    own()
                    if ORD[u] >= 2:
                        act.wait_ge(pv_done, ORD[u] - 1)
                    pt = probT[:, ORD[u] % 2]
                    if kind == "P" and b == CMP:
                        x = A(pt[0:NCP, 0, 0:P], bank[4][0:NCP, 0:P], ACT.Copy)
                    elif kind == "P":
                        n = P * (UNITS[u][3] + 1)
                        x = A(pt[:, 0, 0:n], bank[4][:, 0:n], ACT.Copy)
                    elif b == CMP:
                        x = A(pt[0:NCS, 0, 0:P], bank[4][0:NCS, 0:P], ACT.Copy)
                    else:
                        A(pt[:, 0, 0:PAST], bank[4][:, 0:PAST], ACT.Copy)
                        x = A(pt[0:NS, 0, PAST:PAST + P], bank[4][0:NS, PAST:PAST + P], ACT.Copy)
                    x.then_inc(*tell(pt_act))

            for job in range(G0, len(JOBS)):
                g = job - G0
                kind, c = JOBS[job]
                if kind == "mn" and c == 0:
                    act.wait_ge(oz_lo, 8)
                    for t in range(NT):
                        src = (a["x_sample"].rearrange("s t n -> (s t) n") if t == 4
                               else a["x_prompt"][0, P * t:P * t + P])
                        act.dma_start(yb[0:rows(t), t, :], src).then_inc(in_xy, 16)
                    act.dma_start(fgb[:, :], a["final_g"].rearrange("(a n) -> a n", a=1).to_broadcast([P, D]))\
                        .then_inc(in_fg, 16)
                for t in range(4 if kind != "y" else 0):
                    if t % blocks_of(job) == 0:
                        split_hi(FIRST[job] + t // blocks_of(job) + 2)
                    if kind == "z":
                        n = 4 * c + t
                        tile_ready(act, job, t)
                        own()
                        if n >= 2:
                            act.wait_ge(z_mul, n - 1)
                        A(halves(zs[:, n % 2, :]), product(job, t), ACT.Silu).then_inc(*tell(g_act))
                        act.wait_ge(z_mul, n + 1)
                        A(oz[0][:, n, :], oT[:, n, :], ACT.Copy).then_inc(*tell(oz_hi))
                    elif kind in ("mn", "md"):
                        tile_ready(act, job, t)
                        own()
                        if c == 1:
                            act.wait_ge(g_dve, GV[g - 3] + t + 1)
                        A(part(sg if kind == "mn" else sg2, t), product(job, t), ACT.Sigmoid).then_inc(*tell(g_act))
                    elif kind == "ud":
                        act.wait_ge(m_made, 4 * c + t + 1)
                        own()
                        A(mT[0][:, 4 * c + t, :], mt[:, t, :], ACT.Copy).then_inc(*tell(mT_hi))
                if kind == "y":
                    for n in before_evac(job):
                        split_hi(n)
                    for t in range(NT):
                        r = rows(t)
                        act.wait_ge(y_sum, NT * c + t + 1)
                        own()
                        A(mt[0:r, 0, 0:512], yb[0:r, t, 512 * c:512 * c + 512], ACT.Square,
                          accum_out=norm[0:r, 2 * t + c:2 * t + c + 1]).then_inc(*tell(y_sq))
                        if c:
                            act.wait_ge(y_ms, t + 1)
                            A(norm[0:r, 18 + t:19 + t], norm[0:r, 12 + t:13 + t], ACT.Sqrt).then_inc(*tell(y_root))
                    for n in after_evac(job):
                        split_hi(n)
                if kind == "ud" and c == 1:
                    for h in range(2):
                        act.wait_ge(mod_done, 5 + h)
                        A(mod_g[:, 512 * h:512 * h + 512], bank[5 + h][:, :], ACT.Copy).then_inc(*tell(mod_copied))

        @block.vector
        def _(dve):
            told = {}
            latest = []

            def tell(s):
                told[id(s)] = told.get(id(s), 0) + 1
                latest[:] = [s, told[id(s)]]
                return s, 1

            def own():
                if latest:
                    dve.wait_ge(*latest)

            def link(ins):
                ins.then_inc(*tell(dve_step))
                own()

            tt, ts, stt, cp = dve.tensor_tensor, dve.tensor_scalar, dve.scalar_tensor_tensor, dve.tensor_copy

            dve.wait_ge(c_turned, 1)
            dve.wait_ge(zeroed, 1)
            cp(cT[:, :, 0:9], bank[5][:, 0:72].rearrange("p (k n) -> p k n", k=KT)).then_inc(*tell(cT_made))
            dve.wait_ge(c_turned, 2)
            cp(gT[:, :], bank[6][:, 0:8])
            cp(rT[:, R_PE[0]:R_PE[0] + 16], bank[6][:, 8:24])
            cp(rT[:, R_PE[1]:R_PE[1] + 16], bank[6][:, 24:40]).then_inc(*tell(small_made))
            dve.wait_ge(squared, NT)
            ts(norm[:, 8:12], norm[:, 0:4], 1.0 / D, EPS, ALU.mult, ALU.add).then_inc(*tell(ms_made))
            ts(norm[0:NS, 12:13], norm[0:NS, 4:5], 1.0 / D, EPS, ALU.mult, ALU.add).then_inc(*tell(ms_made))
            dve.wait_ge(rooted, 1)
            link(dve.reciprocal(norm[:, 24:28], norm[:, 16:20]))
            link(dve.reciprocal(norm[0:NS, 28:29], norm[0:NS, 20:21]))
            for t in range(NT):
                r = rows(t)
                ts(xs[0:r, t, :], xs[0:r, t, :], norm[0:r, 24 + t:25 + t], None, ALU.mult).then_inc(*tell(xn_made))
            dve.wait_ge(small_made, 1)
            dve.wait_ge(ab_done, 1)
            mod_ps = bank[7][:, 0:256].rearrange("p (w k n) -> p w k n", w=2, k=KT)[:, :, :, 0:9]
            cp(AB[:, 0], mod_ps[:, 0])
            stt(out=AB[:, 1], in0=mod_ps[:, 1], scalar=1.0, in1=spread(gT[:, :], 2, 9), op0=ALU.add, op1=ALU.mult)\
                .then_inc(*tell(ab_made))
            dve.wait_ge(ab_made, 1)

            def lo_of_h(k):
                own()
                dve.wait_ge(h_hi, k + 1)
                dve.wait_ge(h_made, k + 1)
                if k == KT:
                    tmp = rope_b[:, 0, 0:KT * NS].rearrange("p (k n) -> p k n", k=KT)
                    tt(hT[1][:, :, SEQ:TOK], tmp, hT[0][:, :, SEQ:TOK].bitcast(F32), ALU.subtract).then_inc(*tell(h_lo))
                else:
                    tt(hT[1][:, k, 0:SEQ], rope_b[:, k % 2, :], hT[0][:, k, 0:SEQ].bitcast(F32), ALU.subtract)\
                        .then_inc(*tell(h_lo))

            for k in range(KT):
                dve.wait_ge(x_turned, k + 1)
                own()
                ts(rope_b[:, k % 2, :], bank[5 + k % 3][:, :], AB[:, 1, k, 0:1], AB[:, 0, k, 0:1], ALU.mult, ALU.add)\
                    .then_inc(*tell(h_made))
                if k:
                    lo_of_h(k - 1)
            lo_of_h(KT - 1)
            dve.wait_ge(x_turned, KT + 1)
            tmp = rope_b[:, 0, 0:KT * NS].rearrange("p (k s t) -> p k s t", k=KT, s=NSEQ)
            link(tt(tmp, bank[4][:, 0:KT * NS].rearrange("p (k s t) -> p k s t", k=KT, s=NSEQ),
                    spread(AB[:, 1, :, 1:9], 3, NEW), ALU.mult))
            tt(tmp, tmp, spread(AB[:, 0, :, 1:9], 3, NEW), ALU.add).then_inc(*tell(h_made))
            lo_of_h(KT)

            def split_lo(n):
                own()
                dve.wait_ge(hi_made, n + 1)
                arrived(dve, piece(n)[0])
                for dst, src, hi in split_views(n, 1):
                    last = tt(dst, src, hi.bitcast(F32), ALU.subtract)
                last.then_inc(*tell(lo_made))

            def read_tiles(job):
                c0, H = ROPED[job]
                if job == J_IDX:
                    dve.wait_ge(x_turned, KT + 1)
                if job == J_NQ:
                    dve.wait_ge(stored["idx"], 32)
                    dve.wait_ge(aux_done, aux_last_read(J_IDX))
                if job == J_DQ:
                    dve.wait_ge(stored["kv"], 32)
                    dve.wait_ge(aux_done, aux_last_read(J_KV))
                if job in (J_DKV, J_WIN):
                    dve.wait_ge(aux_done, aux_last_read(J_NQ))
                for t in range(NT):
                    r = rows(t)
                    n = NT * job + t
                    tile_ready(dve, job, t)
                    if ACT_READS[job]:
                        dve.wait_ge(t_act, act_tiles(job, t))
                    own()
                    if n >= 2:
                        dve.wait_ge(roped, n - 1)
                    x = bank[t][0:r, c0:c0 + HD * H]
                    ra = stg[0:r, STG[job], 512 * t + c0:512 * t + c0 + HD * H]
                    rb = rope_b[0:r, n % 2, 0:HD * H]
                    cos = tb("cos", r)[:, HD * t:HD * t + HD]
                    sin = tb("sin", r)[:, HD * t:HD * t + HD]
                    if H == 8:
                        x, ra, rb = by_group(x), by_pair(ra), by_pair(rb)
                        cos, sin = (spread(spread(y, 1, 4), 1, 2) for y in (cos, sin))
                    else:
                        x, ra, rb = (y.rearrange("p (h d) -> p h d", h=H) for y in (x, ra, rb))
                        cos, sin = (spread(y, 1, H) for y in (cos, sin))
                    tt(ra, x, cos, ALU.mult)
                    tt(rb[..., 0:32], x[..., 32:64], sin[..., 0:32], ALU.mult)
                    tt(rb[..., 32:64], x[..., 0:32], sin[..., 32:64], ALU.mult).then_inc(*tell(t_dve))

            def aux(slot):
                for i, (at, kind, n, e) in enumerate(AUX):
                    if at != slot:
                        continue
                    src = bank[5 + i % 3]
                    own()
                    if kind == "dots":
                        d = DOTS.index(n)
                        t, h = n
                        m = P * (t + 1)
                        aux_wait(dve, "dots", n)
                        dve.wait_ge(t_act, act_tiles(J_IDX, 4))
                        if d:
                            dve.wait_ge(score_added, d)
                        acc = tb("mrow")[:, SEQ - m:SEQ] if h == 0 else score[:, t - 1, 0:m]
                        stt(out=score[:, t - 1, 0:m], in0=relu_d[:, d % 2, 0:m], scalar=iw[:, t, h:h + 1], in1=acc,
                            op0=ALU.mult, op1=ALU.add).then_inc(*tell(score_added))
                        continue
                    if kind == "sdots":
                        aux_wait(dve, "sdots", 0)
                        dve.wait_ge(t_act, act_tiles(J_IDX, 4))
                        for h in range(4):
                            x = cp(iwr[NS * h:NS * h + NS, :], iw[0:NS, 4, h:h + 1])
                        link(x)
                        ts(relu_s[:, :], relu_s[:, :], iwr[:, 0:1], None, ALU.mult).then_inc(*tell(sdots_weighted))
                        continue
                    if e != "v":
                        continue
                    if kind in ("ck", "cvp"):
                        some_rounds(2)
                    dve.wait_ge(aux_done, i + 1)
                    if kind == "ssum":
                        tt(scoreS[:, :], src[0:NS, 0:NKS], tb("midx", NS), ALU.add).then_inc(*tell(aux_dve))
                    elif kind == "grow":
                        link(tt(gtmp[:, :], src[:, 0:24], tb("headmask"), ALU.mult))
                        dve.tensor_reduce(grow[:, n, :], gtmp[:, :].rearrange("p (h b) -> p b h", b=3), AX.X, ALU.add)\
                            .then_inc(*tell(aux_dve))
                    elif kind == "si":
                        cp(qTi[:, :, SEQ:TOK], src[:, 0:2 * NS].rearrange("p (j n) -> p j n", j=2))
                        cp(kni[:, :], src[0:HD, 2 * NS:3 * NS]).then_inc(*tell(aux_dve))
                        aux_wait(dve, "si", 0)
                        dve.wait_ge(zeroed, 2)
                        for h in range(4):
                            x = qTi[64 * (h % 2):64 * (h % 2) + 64, h // 2, SEQ:TOK]
                            dst = bass.AP(iqz.tensor, iqz.offset + NS * h, [iqz.ap[0], [P + NEW, NSEQ], [1, NEW]])
                            cp(dst, x.rearrange("p (s t) -> p s t", s=NSEQ))
                            y = cp(iqa[:, NS * h:NS * h + NS], x)
                        y.then_inc(*tell(iq_laid))
                    else:
                        moves(kind, n, src, lambda o, x: cp(o, x)).then_inc(*tell(aux_dve))

            def take_top(row, n):
                link(dve.max(top8[0:n, :], row))
                link(dve.match_replace(out=row, in_to_replace=top8[0:n, :], in_values=row, imm_value=TAKEN))

            def rounds(t, count):
                for _ in range(count):
                    take_top(score[:, t - 1, 0:P * (t + 1)], P)

            def mask_rest(row):
                own()
                return ts(row, row, 0.99 * TAKEN, NEG, ALU.is_gt, ALU.mult)

            todo = [(t, 4) for t in (1, 2, 3) for _ in range(TOPK_P // 8 // 4)]

            def some_rounds(n):
                for t, count in todo[:n]:
                    rounds(t, count)
                del todo[:n]

            def select_samples():
                dve.wait_ge(aux_dve, sum(x[3] == "v" for x in AUX[:AUX_AT[("ssum", 0)] + 1]))
                dve.wait_ge(score_added, len(DOTS))
                for n in range(TOPK_S // 8):
                    take_top(scoreS[:, :], NS)
                link(dve.max(top8[0:NS, :], scoreS[:, :]))
                link(dve.memset(top8[0:NS, TOPK_S % 8:8], TAKEN))
                link(dve.match_replace(out=scoreS[:, :], in_to_replace=top8[0:NS, :], in_values=scoreS[:, :],
                                       imm_value=TAKEN))
                mask_rest(scoreS[:, :]).then_inc(*tell(sel_made))

            dve.wait_ge(zeroed, 2)
            for job in range(G0):
                aux(job)
                if job == 3:
                    select_samples()
                some_rounds({2: 4, 3: 1, 4: 1, 5: 2}.get(job, 0))
                read_tiles(job)
            assert not todo
            dve.wait_ge(lo_made, POOL_SPLITS)
            split_lo(POOL_SPLITS)
            split_lo(POOL_SPLITS + 1)
            for t in (1, 2, 3):
                x = mask_rest(score[:, t - 1, 0:P * (t + 1)])
            link(x)
            dve.wait_ge(t_act, act_tiles(J_WIN, 4))
            gv = gates[:, 0, :].rearrange("p (h b) -> p h b", b=3)[:, :, 0]
            link(ts(gv, gv, tb("vis"), None, ALU.mult))

            dve.wait_ge(aux_act, sum(x[3] == "a" for x in AUX))

            def mask_max(u):
                own()
                kind, b = UNITS[u][:2]
                src = [bank[(AT[u] + g) % 4] for g in range(2)]
                s = stats[:, u % 4, :]
                if kind == "T":
                    dve.wait_ge(s_done, AT[u] + 1)
                    dve.wait_ge(zeroed, 3)
                    for g in range(2):
                        x = cp(kz[DSA][64 * g:64 * g + 64, g, :], src[0][64 * g:64 * g + 64, :])
                    x.then_inc(*tell(masked))
                    return
                if kind == "K":
                    m = KV_ORDER.index((b, UNITS[u][2]))
                    dve.wait_ge(s_done, AT[u] + 1)
                    dve.wait_ge(roped, NT * G0)
                    dve.wait_ge(stored["win"], 32)
                    if m >= 2:
                        dve.wait_ge(s_done, AT[UNITS.index(("S", *KV_ORDER[m - 2])) + 1])
                    cp(kTs[:, m % 2, 0:2, :].rearrange("p s n -> p (s n)"), src[0][:, :]).then_inc(*tell(masked))
                    return
                if u >= 4 and REAL[u - 4]:
                    dve.wait_ge(scaled, TURNS[u - 3])
                if kind == "P":
                    t = UNITS[u][3]
                    n = NCP if b == CMP else P * (t + 1)
                    m = (tb("mcmp")[:, 32 * t:32 * t + NCP] if b == CMP else
                         score[:, t - 1, 0:n] if b == DSA and t else tb("mrow")[:, SEQ - n:SEQ])
                    g2 = 2
                else:
                    T = UNITS[u][2]
                    n = NCS if b == CMP else NKS
                    m = (tb("mrow")[:, 0:n] if b == CMP else selS[:, T, :] if b == DSA
                         else tb("msamp")[:, NKS * T:NKS * T + NKS])
                    g2 = 1
                for g in range(g2):
                    dve.wait_ge(s_done, AT[u] + g + 1)
                    dve.tensor_tensor_reduce(out=src[g][:, 0:n], in0=src[g][:, 0:n], in1=m, scale=-SCALE, scalar=-TAKEN,
                                             op0=ALU.add, op1=ALU.min, accum_out=s[:, 2 + g:3 + g])\
                        .then_inc(*tell(masked))

            def gate_over_sum(u):
                own()
                if not REAL[u]:
                    return
                kind, b = UNITS[u][:2]
                s = stats[:, u % 4, :]
                dve.wait_ge(exped, SIG[u + 1])
                g2 = 2 if kind == "P" else 1
                if b == DSA:
                    dve.reciprocal(s[:, 6:6 + g2], s[:, 4:4 + g2]).then_inc(*tell(r_made))
                    return
                link(dve.reciprocal(s[:, 6:6 + g2], s[:, 4:4 + g2]))
                if kind == "P":
                    j, t = UNITS[u][2:]
                    gate = gates[:, t, :].rearrange("p (g j b) -> p g j b", g=2, j=4)[:, :, j, b]
                else:
                    gate = grow[:, UNITS[u][2], b:b + 1]
                tt(s[:, 6:6 + g2], s[:, 6:6 + g2], gate, ALU.mult).then_inc(*tell(r_made))

            def copy_turned(u):
                if UNITS[u][0] != "P":
                    return
                own()
                kind, b = UNITS[u][:2]
                dve.wait_ge(pt_done, TURNS[u] + 2)
                if ORD[u] == 0:
                    dve.wait_ge(stored["win"], 32)
                if ORD[u] >= 2:
                    dve.wait_ge(pv_done, ORD[u] - 1)
                pt = probT[:, ORD[u] % 2]
                if kind == "P" and b == CMP:
                    x = cp(pt[0:NCP, 1, 0:P], bank[5][0:NCP, 0:P])
                else:
                    n = P * (UNITS[u][3] + 1)
                    x = cp(pt[:, 1, 0:n], bank[5][:, 0:n])
                x.then_inc(*tell(pt_dve))

            def copy_out(w):
                own()
                if w == 0:
                    for name in ("idx", "kv", "dkv"):
                        dve.wait_ge(stored[name], 32)
                kind, j = OWNERS[w]
                src = bank[6 + w % 2]
                dve.wait_ge(pv_done, ORD[LAST_OF[w]] + 1)
                if kind in "nd":
                    cp(oT[:, j + (4 if kind == "d" else 0), 0:SEQ], src[:, :]).then_inc(*tell(o_copied))
                    return
                b0 = 4 if kind == "D" else 0
                for g in range(2):
                    x = cp(oT[64 * g:64 * g + 64, b0:b0 + 4, SEQ + 16 * j:SEQ + 16 * j + 16]
                           .rearrange("p j (s t) -> p j s t", s=4),
                           src[64 * g:64 * g + 64, 0:P].rearrange("p (s g j t) -> p g j s t", s=4, g=2, j=4)[:, g])
                x.then_inc(*tell(o_copied))

            for i in range(len(UNITS) + LAG + 2):
                if i < len(UNITS):
                    mask_max(i)
                if 0 <= i - 1 < len(UNITS):
                    gate_over_sum(i - 1)
                if 0 <= i - LAG < len(UNITS):
                    copy_turned(i - LAG)
                for w, u in LAST_OF.items():
                    if u == i - LAG - 2:
                        copy_out(w)
            dve.wait_ge(o_copied, len(OWNERS))
            for job in range(G0, len(JOBS)):
                g = job - G0
                kind, c = JOBS[job]
                for t in range(4 if kind != "y" else 0):
                    if t % blocks_of(job) == 0:
                        split_lo(FIRST[job] + t // blocks_of(job) + 2)
                    if kind == "z":
                        n = 4 * c + t
                        dve.wait_ge(g_act, GA[g] + t + 1)
                        own()
                        x = oT[:, n, :]
                        tt(x, x, zs[:, n % 2, :], ALU.mult).then_inc(*tell(z_mul))
                        own()
                        dve.wait_ge(oz_hi, n + 1)
                        tt(oz[1][:, n, :], x, oz[0][:, n, :].bitcast(F32), ALU.subtract).then_inc(*tell(oz_lo))
                    elif kind in ("un", "ud"):
                        gate = sg if kind == "un" else sg2
                        dst = mt if kind == "un" else gate
                        dve.wait_ge(g_act, GA[g])
                        tile_ready(dve, job, t)
                        own()
                        if kind == "un" and c:
                            dve.wait_ge(mT_hi, t + 1)
                        tt(part(dst, t), product(job, t), part(gate, t), ALU.mult).then_inc(*tell(g_dve))
                        if kind == "ud":
                            own()
                            tt(mt[:, t, :], mt[:, t, :], gate[:, t, :], ALU.add).then_inc(*tell(m_made))
                            own()
                            dve.wait_ge(mT_hi, 4 * c + t + 1)
                            tt(mT[1][:, 4 * c + t, :], mt[:, t, :], mT[0][:, 4 * c + t, :].bitcast(F32),
                               ALU.subtract).then_inc(*tell(mT_lo))
                if kind == "y":
                    for n in before_evac(job):
                        split_lo(n)
                    if c == 0:
                        dve.wait_ge(in_xy, 16 * NT)
                    for t in range(NT):
                        r = rows(t)
                        tile_ready(dve, job, t)
                        own()
                        gate = (gateS if t == 4 else gateP)[0:r, 512 * c:512 * c + 512]
                        tmp = sg[0:r, t % 4, 0:512]
                        tt(tmp, bank[t][0:r, :], gate, ALU.mult).then_inc(*tell(g_dve))
                        dve.wait_ge(g_dve, GV[g] + t + 1)
                        y = yb[0:r, t, 512 * c:512 * c + 512]
                        tt(y, y, tmp, ALU.add).then_inc(*tell(y_sum))
                        if c:
                            dve.wait_ge(y_sq, NT + t + 1)
                            link(tt(norm[0:r, 12 + t:13 + t], norm[0:r, 2 * t:2 * t + 1],
                                    norm[0:r, 2 * t + 1:2 * t + 2], ALU.add))
                            ts(norm[0:r, 12 + t:13 + t], norm[0:r, 12 + t:13 + t], 1.0 / D, EPS, ALU.mult, ALU.add)\
                                .then_inc(*tell(y_ms))
                            dve.wait_ge(y_root, t + 1)
                            link(dve.reciprocal(norm[0:r, 24 + t:25 + t], norm[0:r, 18 + t:19 + t]))
                            if t == 0:
                                dve.wait_ge(in_fg, 16)
                            stt(out=yb[0:r, t, :], in0=yb[0:r, t, :], scalar=norm[0:r, 24 + t:25 + t],
                                in1=fgb[0:r, :], op0=ALU.mult, op1=ALU.mult).then_inc(*tell(y_out))
                    for n in after_evac(job):
                        split_lo(n)
                if kind == "ud" and c == 1:
                    dve.wait_ge(ab_done, 2)
                    cp(gateP[:, 0:512], bank[5][:, :])
                    cp(gateP[:, 512:1024], bank[6][:, :])
                    cp(gateS[:, 0:512], bank[7][0:NS, :]).then_inc(*tell(gate_made))
                    dve.wait_ge(ab_done, 3)
                    link(cp(gateS[:, 512:1024], bank[7][0:NS, :]))


INPUTS = ["x_prompt", "x_sample", "cache_nsa_kv", "cache_dsa_kv", "cache_dsa_idx_k", "state_nsa_win_kv", "page_table",
          "c_prompt", "c_sample", "norm_g", "w_ada", "b_ada", "w_in", "cmp_pe", "cmp_w1", "cmp_w2", "w_up_nsa",
          "w_up_dsa", "w_out", "final_g"]
OUTPUTS = [("y_p", (1, SEQ, D)), ("y_s", (NSEQ, NEW, D)), ("nsa_p", (1, 1, SEQ, 4, 2, HD)),
           ("dsa_p", (1, 1, SEQ, 2, 2, HD)), ("idx_p", (1, 1, SEQ, HD)), ("win_p", (1, 1, SEQ, 2, 2, HD)),
           ("nsa_s", (1, NSEQ, NEW, 4, 2, HD)), ("dsa_s", (1, NSEQ, NEW, 2, 2, HD)), ("idx_s", (1, NSEQ, NEW, HD)),
           ("win_s", (1, NSEQ, PAST, 2, 2, HD))]


def kernel(**inputs):
    import numpy as np
    import concourse.bacc as bacc
    from concourse.bass_utils import run_bass_kernel_spmd

    nc = bacc.Bacc("TRN2", target_bir_lowering=False, num_devices=1)
    arrays, args, outs = {}, {}, {}
    for name in INPUTS + ["tables"]:
        x = tables() if name == "tables" else np.ascontiguousarray(inputs[name])
        arrays[f"in_{name}"] = x
        args[name] = nc.dram_tensor(f"in_{name}", x.shape, mybir.dt.from_np(x.dtype), kind="ExternalInput").ap()
    for name, shape in OUTPUTS:
        outs[name] = nc.dram_tensor(f"out_{name}", shape, F32, kind="ExternalOutput").ap()
    build(nc, args, outs)
    r = run_bass_kernel_spmd(nc, [arrays], core_ids=[0])
    return tuple(r.results[0][f"out_{name}"] for name, _ in OUTPUTS)
```

```python
from contextlib import ExitStack

import concourse.bass as bass
from concourse import mybir

F32 = mybir.dt.float32
F32R = mybir.dt.float32r
I32 = mybir.dt.int32
ALU = mybir.AluOpType
ACT = mybir.ActivationFunctionType
AX = mybir.AxisListType

P = 128
D = 1024
KT = D // P
SEQ = 512
NSEQ, NEW = 8, 4
NS = NSEQ * NEW
TOK = SEQ + NS
PAST = 256
PAGE = 128
NPAGE = PAST // PAGE
NT = 5
HD = 64
TOPK_P, TOPK_S = 128, (PAST + NEW) // 4
NCP, NCS = 31, 15
R_PROMPT, R_PE, R_SAMPLE = (0, 21 * P), (4 * P, 25 * P), 5 * P
R_BASE = (0, R_SAMPLE)
R_ALL = 26 * P + 16
R_COLS = 21 * 16


def r_col(n, at):
    return (at - R_BASE[n]) // 8


NKS = PAST + NS
EPS = 1e-6
NEG = -1e30
TAKEN = -3e38
SCALE = HD ** -0.5
IDX_SCALE = (HD ** -0.5) * (4 ** -0.5)

NQ, NKV, DQ, DKV, IQ, NZ, DZ, MG = 0, 512, 1816, 2328, 2584, 1304, 2908, 3420
T_JOBS = [(IQ, 324), (NKV, 512), (NQ, 512), (DQ, 512), (NKV + 512, 280), (DKV, 256)]
J_IDX, J_KV, J_NQ, J_DQ, J_WIN, J_DKV = range(6)
ROPED = [(0, 5), (256, 2), (0, 8), (0, 8), (0, 2), (0, 2)]
STG = [0, 1, 0, 1, 2, 0]
ACT_READS = [1, 1, 1, 0, 1, 1]
CMP, SLC, WIN, DSA = range(4)
PLAIN, ROT, DSAQ = range(3)
G_JOBS = [("z", 0), ("z", 1)] + [(k, c) for c in range(2) for k in ("mn", "un", "md", "ud")] + [("y", 0), ("y", 1)]
JOBS = [("T", i) for i in range(6)] + G_JOBS
G_EVAC = {"z": "a", "mn": "a", "md": "a", "un": "v", "ud": "v", "y": "v"}

PIECES = [2 if k in ("un", "ud") else 4 for k, _ in JOBS]
FIRST = [sum(PIECES[:i]) for i in range(len(JOBS) + 1)]



def _plan_aux():
    aux = []

    def add(at, kind, n, e):
        aux.append((at, kind, n, e))

    def queries(at, which, pairs):
        for j in pairs:
            add(at, "q", (which, j), "av"[j % 2])

    for kind, n, e in (("mod", (4, 0), "a"), ("qi", 0, "a"), ("modT", (4, 0), "v"), ("qi", 1, "v"), ("ki", 0, "a"),
                       ("si", 0, "v")):
        add(1, kind, n, e)
    for kind, n, e in (("cmpT", 0, "v"), ("cmpT", 1, "a"), ("k", SLC, "a"), ("kn", SLC, "v"), ("ikT", 0, "a"),
                       ("ikT", 1, "v"), ("ikT", 2, "a"), ("ikT", 3, "v")):
        add(2, kind, n, e)
    for t in (1, 2, 3):
        for h in range(4):
            add(2, "dots", (t, h), "a")
            if (t, h) == (1, 1):
                add(2, "sdots", 0, "a")
    add(2, "ssum", 0, "v")
    queries(3, PLAIN, range(4))
    add(3, "qs", PLAIN, "v")
    queries(3, ROT, range(2))
    for n in range(4):
        add(3, "raw", (0, n), "av"[n % 2])
    queries(3, ROT, range(2, 4))
    for kind, n, e in (("qs", ROT, "v"), ("hid", 0, "a"), ("mod", (4, 1), "a"), ("ck", 0, "v"), ("modT", (4, 1), "v")):
        add(3, kind, n, e)
    queries(4, DSAQ, range(2))
    for n in range(4):
        add(4, "raw", (1, n), "av"[n % 2])
    queries(4, DSAQ, range(2, 4))
    for kind, n, e in (("qs", DSAQ, "v"), ("hid", 1, "a"), ("mod", (5, 0), "a"), ("cvp", 0, "v"), ("cvs", 0, "a"),
                       ("cvs", 1, "v"), ("modT", (5, 0), "v")):
        add(4, kind, n, e)
    for kind, n, e in (("mod", (5, 1), "a"), ("selx", 0, "a"), ("selx", 1, "a"), ("modT", (5, 1), "v"),
                       ("grow", 0, "v"), ("grow", 1, "v"), ("k", WIN, "a"), ("kn", WIN, "v")):
        add(5, kind, n, e)
    return aux


AUX = _plan_aux()
AUX_AT = {(k, n): i for i, (_, k, n, _) in enumerate(AUX)}



def _plan_units():
    units = []
    for T in range(2):
        for j in (2 * T, 2 * T + 1):
            if j % 2:
                units.append(("K", SLC, T))
            units.extend(("P", b, j, t) for t in (3, 2, 1, 0) for b in (CMP, SLC, WIN))
        units += [("S", CMP, T), ("K", WIN, T), ("S", SLC, T), ("S", WIN, T)]
    units.insert(4, ("T", DSA))
    for j in range(4):
        if j in (2, 3):
            units.append(("K", DSA, j - 2))
        units.extend(("P", DSA, j, t) for t in (3, 2, 1, 0))
    return units + [("S", DSA, 0), ("S", DSA, 1)]


UNITS = _plan_units()
LAG = 3
OWNERS = [("n", 0), ("n", 1), ("N", 0), ("n", 2), ("n", 3), ("N", 1), ("d", 0), ("d", 1), ("d", 2), ("d", 3), ("D", 0),
          ("D", 1)]


def owner(u):
    kind, b = u[0], u[1]
    return OWNERS.index((("nd" if kind == "P" else "ND")[b == DSA], u[2]))


REAL = [u[0] in "PS" for u in UNITS]
ORD = [sum(REAL[:i]) for i in range(len(UNITS) + 1)]
ORDP = [sum(u[0] == "P" for u in UNITS[:i]) for i in range(len(UNITS) + 1)]
AT = [sum(1 + (u[0] != "S") for u in UNITS[:i]) for i in range(len(UNITS) + 1)]
SIG = [sum(1 + (u[0] == "P") for u in UNITS[:i]) for i in range(len(UNITS) + 1)]
TURNS = [sum({"P": 2, "S": 1}.get(u[0], 0) for u in UNITS[:i]) for i in range(len(UNITS) + 1)]
LAST_OF = {owner(u): i for i, u in enumerate(UNITS) if REAL[i]}
FIRST_OF = {w: min(i for i, u in enumerate(UNITS) if REAL[i] and owner(u) == w) for w in LAST_OF}
KV_ORDER = [(u[1], u[2]) for u in UNITS if u[0] == "K"]


def kv_slot(b, T):
    return KV_ORDER.index((b, T)) % 2


LOADS = []


def _plan_loads():
    def weights(job):
        LOADS.extend(("w", job, e) for e in range(PIECES[job] // 2))

    LOADS.extend(("ada", c, e) for c in range(4) for e in range(2))
    weights(0)
    for job, extra in ((1, [("ada", 4, 0)]), (2, []),
                       (3, [("cmpw", 0, 0), ("ada", 4, 1)]),
                       (4, [("cmpw", 1, 0), ("ada", 5, 0)]), (5, [("ada", 5, 1)])):
        LOADS.extend([("w", job, 0), *extra, ("w", job, 1)])
    LOADS.append(("w", 6, 0))
    LOADS.extend(("kv", b, T) for b, T in KV_ORDER)
    LOADS.append(("w", 6, 1))
    for job in range(7, len(JOBS)):
        weights(job)


_plan_loads()
SLOTS = 2
FIRST_SLOTS, N_FIRST = 4, 8


H_ORDER = [0, 1, KT, *range(2, KT)]


CACHED_BEFORE = [("w", 1, 0), ("w", 3, 0), ("cmpw", 1, 0)]


def slot(i):
    return i % (FIRST_SLOTS if i < N_FIRST else SLOTS)


def before_in_slot(i):
    return max((k for k in range(i) if slot(k) == slot(i)), default=None)


LOAD_AT = {key: i for i, key in enumerate(LOADS)}
PE_LOADS = [i for i, key in enumerate(LOADS) if key[0] != "w"]
N_DMAS = {"w": 1, "ada": 1, "cmpw": 1, "kv": 8}


def dmas_of(key):
    if key[0] == "w" and JOBS[key[1]][0] in ("un", "ud", "z"):
        return 2
    if key[0] == "kv" and key[1] == WIN:
        return 1
    return N_DMAS[key[0]]


TAB = {}


def _table_columns():
    at = 0
    for name, n in (("ident", 128), ("brow", 192), ("gsel", 9), ("mrow", 512), ("mcmp", 128), ("cos", 320),
                    ("sin", 320), ("msamp", 576), ("expand", 256), ("headmask", 24), ("hsum", 32), ("midx", 288),
                    ("vis", 1)):
        TAB[name] = (at, at + n)
        at += n
    return at


NTAB = _table_columns()
TAB_A = TAB["mrow"][0]


def tables():
    import numpy as np
    t = np.zeros((P, NTAB), np.float32)

    def put(name, x):
        t[:x.shape[0], TAB[name][0]:TAB[name][0] + x.shape[1]] = x

    p = np.arange(P)
    put("ident", np.eye(P))
    put("mrow", np.concatenate([np.zeros((P, 384)), np.where(p[None] <= p[:, None], 0.0, NEG)], 1))
    ends = np.arange(NCP) * 16 + 31
    mc = np.zeros((P, 4, 32))
    for i in range(4):
        mc[:, i, :NCP] = np.where(ends[None] <= (i * P + p)[:, None], 0.0, NEG)
    put("mcmp", mc.reshape(P, 128))
    inv = np.float32(10000.0) ** (-np.arange(32, dtype=np.float32) / np.float32(32))
    pos = np.zeros((NT, P), np.float32)
    pos[:4] = np.arange(SEQ).reshape(4, P)
    pos[4, :NS] = PAST + np.arange(NS) % NEW
    ang = (pos[:, :, None] * inv).astype(np.float32).transpose(1, 0, 2).astype(np.float64)
    put("cos", np.concatenate([np.cos(ang), np.cos(ang)], 2).reshape(P, 320))
    put("sin", np.concatenate([-np.sin(ang), np.sin(ang)], 2).reshape(P, 320))
    s4, g, j, tt = p // 32, p % 32 // 16, p % 16 // 4, p % 4
    ks, kt = np.arange(NS) // NEW, np.arange(NS) % NEW
    ms = np.zeros((P, 2, NKS))
    ex = np.zeros((NS, 2, P))
    for T in range(2):
        seq = 4 * T + s4
        ms[:, T, PAST:] = np.where((ks[None] == seq[:, None]) & (kt[None] <= tt[:, None]), 0.0, NEG)
        ex[seq * NEW + tt, T, p] = 1
    put("msamp", ms.reshape(P, -1))
    put("expand", ex.reshape(NS, -1))
    hm = np.zeros((P, 8, 3))
    hm[p, g * 4 + j] = 1
    put("headmask", hm.reshape(P, 24))
    put("hsum", np.tile(np.eye(32), (4, 1)))
    mi = np.zeros((NS, NKS))
    mi[:, PAST:] = np.where((ks[None] == ks[:, None]) & (kt[None] <= kt[:, None]), 0.0, NEG)
    put("midx", mi)
    gs = np.zeros((P, 9))
    for q in range(4):
        gs[32 * q + np.arange(9), np.arange(9)] = 1
    put("gsel", gs)
    put("vis", (p >= 31).astype(np.float32)[:, None])
    put("brow", np.repeat(np.eye(6), 32, axis=1))
    return t


def spread(ap, at, n):
    dims = [list(d) for d in ap.ap]
    return bass.AP(ap.tensor, ap.offset, dims[:at] + [[0, n]] + dims[at:])


def build(nc, a, o):
    ctx = ExitStack()
    with ctx:
        def sb(name, shape, dt=F32, st=ctx):
            return st.enter_context(nc.sbuf_tensor(name, shape, dt))

        def sem(name):
            return ctx.enter_context(nc.semaphore(name))

        tab = sb("tab", [P, NTAB])

        def tb(name, rows=P):
            return tab[0:rows, TAB[name][0]:TAB[name][1]]

        ident = tb("ident")
        hT = [sb(f"hT_{n}", [P, KT, TOK], F32R) for n in ("hi", "lo")]
        stage = [sb(f"stage{i}", [P, 2048]) for i in range(SLOTS)]
        whl = [[sb(f"w_{n}{i}", [P, 2, 512], F32R) for i in range(2)] for n in ("hi", "lo")]
        cT = sb("cT", [P, KT, 32])
        gateT = sb("gateT", [P, KT, 9])
        bada = sb("b_ada", [6, 512])
        gates = sb("gates", [P, NT, 24])
        grow = sb("gate_rows", [P, 2, 3])
        gtmp = sb("gate_tmp", [P, 24])
        gT = sb("norm_gT", [P, KT])
        norm = sb("norm_stats", [P, 32])
        stats = sb("softmax_stats", [P, 4, 8])
        pages = sb("page_row", [1, NSEQ * NPAGE], I32)
        top8 = sb("top8", [P, 8])

        abc = ExitStack()
        qT = [sb(f"qT_{n}", [P, 4, SEQ], F32, abc) for n in ("plain", "rot", "dsa")]
        qTi = sb("qT_idx", [P, 2, TOK], F32, abc)
        kz2 = sb("kz_win_dsa", [P, 2, 2, SEQ], F32, abc)
        kz = [None, sb("kz_slc", [P, 2, SEQ], F32, abc), kz2[:, 0], kz2[:, 1]]
        kzi = sb("kz_idx", [P, 2, SEQ], F32, abc)
        knew = [None] + [sb(f"k_new_{n}", [P, NS], F32, abc) for n in ("slc", "win", "dsa")]
        kni = sb("k_new_idx", [HD, NS], F32, abc)
        ckz = sb("ckz", [P, 2, 32], F32, abc)
        ckS = sb("ck_sample", [P, NSEQ * NCS], F32, abc)
        cvP = sb("cv_prompt", [32, P], F32, abc)
        cvS = sb("cv_sample", [16, NSEQ, P], F32, abc)
        V = [None] + [sb(f"v_{n}", [P, NT, P], F32, abc) for n in ("slc", "win", "dsa")]
        qS = [sb(f"q_sample_{n}", [P, 2 * P], F32, abc) for n in ("plain", "rot", "dsa")]
        score = sb("score", [P, 3, SEQ], F32, abc)
        scoreS = sb("score_sample", [NS, NKS], F32, abc)
        selS = sb("sel_sample", [P, 2, NKS], F32, abc)
        ab = ExitStack()
        stg = sb("staging", [P, 3, NT * 512], F32, ab)
        rope_b = sb("rope_b", [P, 2, 512], F32, ab)
        rT = sb("rT", [P, R_ALL], F32, ab)
        aT = sb("cmp_act", [P, R_COLS], F32, ab)
        w2 = sb("cmp_w2", [P, 2, HD], F32, ab)
        relu_d = sb("relu_dots", [P, 2, 512], F32, ab)
        relu_s = sb("relu_dots_sample", [P, NKS], F32, ab)
        iw = sb("idx_w", [P, NT, 4], F32, ab)
        iwr = sb("idx_w_rows", [P, 1], F32, ab)
        AB = sb("mod_AB", [P, 2, KT, 9], F32, ab)
        ab.close()
        c_only = ExitStack()
        oT = sb("oT", [P, 8, TOK], F32, c_only)
        probT = sb("probT", [P, 2, 2, SEQ], F32, c_only)
        kTs = sb("kT_sample", [P, 2, 4, PAST], F32, c_only)
        sb("rope_tail", [P, 256], F32, c_only)
        prob = sb("prob", [P, 4, 2, SEQ], F32, c_only)
        c_only.close()
        abc.close()
        d = ctx
        oz = [sb(f"oz_{n}", [P, 8, TOK], F32R, d) for n in ("hi", "lo")]
        zs = sb("silu_z", [P, 2, TOK], F32, d)
        mT = [sb(f"mT_{n}", [P, KT, TOK], F32R, d) for n in ("hi", "lo")]
        sg = sb("sig_n", [P, 4, TOK], F32, d)
        sg2 = sb("sig_d", [P, 4, TOK], F32, d)
        mt = sb("merged", [P, 4, TOK], F32, d)
        yb = sb("y", [P, NT, D], F32, d)
        fgb = sb("final_g", [P, D], F32, d)
        gateP = sb("gate_prompt", [P, D], F32, d)
        xs = stg[:, :, :].rearrange("p a n -> p (a n)")[:, 0:NT * D].rearrange("p (t n) -> p t n", t=NT)
        mod = stg[:, 2, 0:2048]
        rb_all = rope_b[:, :, :].rearrange("p a n -> p (a n)")
        c_raw = relu_d[:, :, :].rearrange("p a n -> p (a n)")
        ring = stage + [qT[q][:, :, :].rearrange("p j n -> p (j n)") for q in (PLAIN, ROT)]
        rTs = rT[:, R_SAMPLE:R_SAMPLE + 16 * P]
        cached = kz2[:, :, :, :].rearrange("p a g n -> p (a g n)")
        ng8 = aT[0:8, 0:P]
        pe32 = aT[0:32, P:2 * P]
        ikTs = rTs[0:HD, :]
        iqz = qT[DSAQ][0:HD, 0:2, :].rearrange("p j n -> p (j n)")
        iqa = qT[DSAQ][0:HD, 2, 0:P]
        gateS = sg2[:, :, :].rearrange("p a n -> p (a n)")[0:NS, 0:D]
        gate_p = zs[:, :, :].rearrange("p a n -> p (a n)")[:, 0:D].rearrange("p (k n) -> p k n", k=KT)
        mod_part = relu_d[:, 0, :]

        psum = ctx.enter_context(nc.psum_tensor("psum", [P, 8, 512], F32))
        bank = [psum[:, i, :] for i in range(8)]

        in_tab, in_tab2, in_c, in_small = sem("in_tab"), sem("in_tab2"), sem("in_c"), sem("in_small")
        in_w2, in_cached = sem("in_w2"), sem("in_cached")
        in_x = [sem(f"in_x{t}") for t in range(NT)]
        in_pages = sem("in_pages")
        loaded = [sem(f"loaded{i}") for i in range(FIRST_SLOTS)]
        pe_freed = sem("pe_freed")
        hi_made, lo_made = sem("hi_made"), sem("lo_made")
        piece_used = sem("piece_used")
        act_step, dve_step, pool_step = sem("act_step"), sem("dve_step"), sem("pool_step")
        zeroed = sem("zeroed")
        csilu, c_turned, cT_made = sem("csilu"), sem("c_turned"), sem("cT_made")
        small_made = sem("small_made")
        mod_done, mod_copied = sem("mod_done"), sem("mod_copied")
        ab_done, ab_made = sem("ab_done"), sem("ab_made")
        squared, ms_made, rooted, xn_made = sem("squared"), sem("ms_made"), sem("rooted"), sem("xn_made")
        x_turned, h_made, h_hi, h_lo = sem("x_turned"), sem("h_made"), sem("h_hi"), sem("h_lo")
        t_done, t_dve, t_act = sem("t_done"), sem("t_dve"), sem("t_act")
        roped = sem("roped")
        aux_done, aux_act, aux_dve = sem("aux_done"), sem("aux_act"), sem("aux_dve")
        score_added = sem("score_added")
        iq_laid, sdots_weighted, sel_made = sem("iq_laid"), sem("sdots_weighted"), sem("sel_made")
        stored = {n: sem(f"stored_{n}") for n in ("idx", "kv", "dkv", "win", "old", "y")}
        s_done, masked, exped = sem("scores_done"), sem("masked"), sem("exped")
        r_made, scaled = sem("r_made"), sem("scaled")
        pt_done, pt_act, pt_dve = sem("pt_done"), sem("pt_act"), sem("pt_dve")
        pv_done, o_copied = sem("pv_done"), sem("o_copied")
        g_done, g_act, g_dve = sem("g_done"), sem("g_act"), sem("g_dve")
        z_mul, oz_hi, oz_lo = sem("z_mul"), sem("oz_hi"), sem("oz_lo")
        m_made, mT_hi, mT_lo = sem("m_made"), sem("mT_hi"), sem("mT_lo")
        in_fg, in_xy = sem("in_fg"), sem("in_xy")
        gate_spread, gate_done, gate_made = sem("gate_spread"), sem("gate_done"), sem("gate_made")
        y_sum, y_sq, y_ms, y_root, y_out = sem("y_sum"), sem("y_sq"), sem("y_ms"), sem("y_root"), sem("y_out")

        def arrived(eng, key):
            i = LOAD_AT[key]
            eng.wait_ge(loaded[slot(i)], 16 * sum(dmas_of(LOADS[k]) for k in range(i + 1) if slot(k) == slot(i)))

        def staged(key):
            return ring[slot(LOAD_AT[key])]

        def rows(t):
            return NS if t == 4 else P

        def act_tiles(job, t):
            return 5 * sum(ACT_READS[:job]) + (t + 1 if ACT_READS[job] else 0)

        def aux_wait(eng, kind, n):
            i = AUX_AT[(kind, n)]
            e = AUX[i][3]
            eng.wait_ge(aux_act if e == "a" else aux_dve, sum(x[3] == e for x in AUX[:i + 1]))

        def aux_last_read(job):
            return sum(x[0] <= job + 1 for x in AUX)

        def job_pieces(job):
            return range(FIRST[job], FIRST[job + 1])

        G0 = 6
        POOL_SPLITS = FIRST[G0]
        GA, GV = [0], [0]
        for kind, _ in G_JOBS:
            tiles = NT if kind == "y" else 4
            GA.append(GA[-1] + tiles * (G_EVAC[kind] == "a"))
            GV.append(GV[-1] + tiles * (G_EVAC[kind] == "v"))

        def g_read(eng, g, t):
            if G_EVAC[G_JOBS[g][0]] == "a":
                eng.wait_ge(g_act, GA[g] + t + 1)
            else:
                eng.wait_ge(g_dve, GV[g] + t + 1)

        def g_signals(g):
            return sum({"y": 4, "un": 2, "ud": 2}.get(k, 0) for k, _ in G_JOBS[:g])

        def tile_ready(eng, job, t):
            g = job - G0
            if g >= 0 and G_JOBS[g][0] != "y":
                each = blocks_of(job)
                if t % each == each - 1:
                    eng.wait_ge(piece_used, FIRST[job] + t // each + 1)
                else:
                    eng.wait_ge(g_done, g_signals(g) + t // 2 + 1)
            elif t == NT - 1:
                eng.wait_ge(piece_used, FIRST[job + 1])
            elif g < 0:
                eng.wait_ge(t_done, (NT - 1) * job + t + 1)
            else:
                eng.wait_ge(g_done, g_signals(g) + t + 1)

        def halves(x):
            return x.rearrange("p (h n) -> p h n", h=2)

        def part(x, b):
            return halves(x[:, b, :])

        def product(job, t):
            b = 4 * (job - G0) + t
            return psum[:, 2 * (b % 4):2 * (b % 4) + 2, 0:TOK // 2]

        def piece(n):
            job = max(j for j in range(len(JOBS)) if FIRST[j] <= n)
            q = n - FIRST[job]
            w = T_JOBS[JOBS[job][1]][1] if JOBS[job][0] == "T" else 512
            return ("w", job, q // 2), q % 2, w

        def w_part(which, n, w):
            return whl[which][n % 2][:, :, :].rearrange("p k n -> p (k n)")[:, 0:2 * w]

        def split_views(n, which):
            key, half, w = piece(n)
            kind = JOBS[key[1]][0]
            dst, hi = w_part(which, n, w), w_part(0, n, w)
            if kind == "T" or kind == "y":
                return [(dst, staged(key)[:, 2 * w * half:2 * w * half + 2 * w], hi)]
            m = {"z": 64, "un": 256, "ud": 256}.get(kind, P)
            src = staged(key)[:, :].rearrange("p (k n) -> p k n", n=2 * m)[:, :, half * m:half * m + m]
            return [(dst.rearrange("p (k n) -> p k n", n=m), src, hi.rearrange("p (k n) -> p k n", n=m))]

        def blocks_of(job):
            return 2 if JOBS[job][0] in ("un", "ud") else 1

        def h_part(x, k):
            return x[:, k, 0:SEQ] if k < KT else x[:, :, SEQ:TOK]

        def h_flat(i, k):
            return rope_b[:, i % 2, :] if k < KT else rope_b[:, i % 2, 0:KT * NS].rearrange("p (k n) -> p k n", k=KT)

        def by_group(x):
            return x.rearrange("p (g j d) -> p g j d", g=2, j=4)

        def by_pair(x):
            return x.rearrange("p (j g d) -> p g j d", g=2, j=4)

        def before_evac(job):
            return range(FIRST[job] + 2, min(FIRST[job + 1] + 1, FIRST[-1]))

        def after_evac(job):
            return range(min(FIRST[job + 1] + 1, FIRST[-1]), min(FIRST[job + 1] + 2, FIRST[-1]))

        def moves(kind, n, src, copy):
            if kind == "qi":
                return copy(qTi[:, n, 0:SEQ], src[:, :])
            if kind in ("ki", "k"):
                dst = kzi if kind == "ki" else kz[n]
                hi = 0 if kind == "ki" else 64
                copy(dst[0:64, 0, :], src[0:64, :])
                return copy(dst[64:128, 1, :], src[hi:hi + 64, :])
            if kind == "kn":
                return copy(knew[n][:, :], src[:, 0:NS])
            if kind == "cmpT":
                v = src[:, :].rearrange("p (q r) -> p r q", r=2)
                for g in range(2):
                    for r in range(2):
                        at = R_PROMPT[n] + PAST * g
                        last = copy(rT[64 * r:64 * r + 64, at:at + PAST], v[64 * g:64 * g + 64, r, :])
                return last
            if kind == "ikT":
                return copy(ikTs[:, 512 * n:512 * n + 512], src[0:HD, :])
            if kind == "q":
                return copy(qT[n[0]][:, n[1], :], src[:, :])
            if kind == "qs":
                for g in range(2):
                    v = qS[n][64 * g:64 * g + 64, :].rearrange("p (s g j t) -> p g j s t", s=NSEQ, g=2, j=4)
                    last = copy(v[:, g], src[64 * g:64 * g + 64, 0:P].rearrange("p (j s t) -> p j s t", j=4, s=NSEQ))
                return last
            if kind == "raw":
                v = rTs[:, 512 * n[1]:512 * n[1] + 512].rearrange("p (s g q) -> p s g q", s=2, g=2)
                w = src[:, :].rearrange("p (s r q) -> p s r q", s=2, r=2)
                for g in range(2):
                    for r in range(2):
                        last = copy(v[64 * r:64 * r + 64, :, g, :], w[64 * g:64 * g + 64, :, r, :])
                return last
            if kind == "ck":
                copy(ckz[0:64, 0, 0:NCP], src[0:64, 0:NCP])
                copy(ckz[64:128, 1, 0:NCP], src[64:128, 0:NCP])
                return copy(ckS[:, :], src[:, 32:32 + NSEQ * NCS])
            if kind == "cvp":
                return copy(cvP[0:NCP, :], src[0:NCP, 0:P])
            assert kind == "cvs"
            return copy(cvS[0:NCS, 4 * n:4 * n + 4, :], src[0:NCS, :].rearrange("p (s c) -> p s c", s=4))

        DOTS = [x[2] for x in AUX if x[1] == "dots"]

        block = ctx.enter_context(nc.Block())

        @block.sync
        def _(sp):
            sp.dma_start(c_raw[0:1, :], a["c_prompt"]).then_inc(in_c, 16)
            sp.dma_start(c_raw[1:9, :], a["c_sample"]).then_inc(in_c, 16)
            sp.dma_start(tab[:, 0:TAB_A], a["tables"][:, 0:TAB_A]).then_inc(in_tab, 16)
            sp.dma_start(ng8, a["norm_g"].rearrange("l (k p) -> (l k) p", p=P)).then_inc(in_small, 16)
            sp.dma_start(pe32, a["cmp_pe"][0].rearrange("s (i r) d -> (s i) (r d)", r=2)).then_inc(in_small, 16)
            sp.dma_start(bada[:, :], a["b_ada"].rearrange("l (c n) -> (l c) n", c=6)).then_inc(in_small, 16)
            sp.dma_start(pages[:, :], a["page_table"].rearrange("s n -> (s n)").rearrange("(a n) -> a n", a=1))\
                .then_inc(in_pages, 16)
            page_of = {}

            def page(i):
                return sp.value_load(pages[0:1, i:i + 1], min_val=0, max_val=a["cache_nsa_kv"].shape[1] - 1)

            def cached_rows(step):
                if step == 0:
                    sp.wait_ge(in_pages, 16)
                else:
                    sp.wait_ge(aux_done, AUX_AT[("ikT", 3) if step == 1 else ("raw", (0, 3))] + 1)
                for n in range(16):
                    pg = bass.ds(page(n), 1)
                    if step == 0:
                        sp.dma_start(cached[:, HD * n:HD * n + HD],
                                     a["cache_dsa_idx_k"][0, pg].rearrange("a p c -> (a p) c")).then_inc(in_cached, 16)
                    else:
                        v = cached.rearrange("p (s r c) -> p s r c", s=NSEQ, r=2)
                        h = n % NPAGE
                        sp.dma_start(v[64 * h:64 * h + 64, n // NPAGE, :, :],
                                     a["cache_nsa_kv"][0, pg, :, step - 1]
                                     .rearrange("a (q r) g d -> (a q) r (g d)", r=2)).then_inc(in_cached, 16)

            for i, key in enumerate(LOADS):
                kind, x, e = key
                if key in CACHED_BEFORE:
                    cached_rows(CACHED_BEFORE.index(key))
                former = before_in_slot(i)
                if former is not None:
                    old = LOADS[former]
                    if old[0] == "w":
                        sp.wait_ge(lo_made, FIRST[old[1]] + 2 * old[2] + 2)
                    else:
                        sp.wait_ge(pe_freed, PE_LOADS.index(former) + 1)
                s = slot(i)
                st = ring[s]
                if kind == "w":
                    job, c = JOBS[x]
                    if job in ("un", "ud"):
                        w = a["w_up_nsa" if job == "un" else "w_up_dsa"][0]
                        for g in range(2):
                            sp.dma_start(st[64 * g:64 * g + 64, :].rearrange("p (j n) -> p j n", j=4),
                                         w[256 * g:256 * g + 256, 512 * c:512 * c + 512]
                                         .rearrange("(j d) n -> d j n", j=4)).then_inc(loaded[s], 16)
                        continue
                    if job == "T":
                        w, at, n = a["w_in"][0], *T_JOBS[c]
                    elif job == "z":
                        w, at, n = a["w_in"][0], (NZ, DZ)[c], 512
                    elif job == "y":
                        w, at, n = a["w_out"][0], 512 * c, 512
                    else:
                        w, at, n = a["w_in"][0], MG + (D if job == "md" else 0) + 512 * c, 512
                    if job == "z":
                        v = st[:, :].rearrange("p (k g n) -> p k g n", k=KT, g=2)
                        for g in range(2):
                            lo = at + 256 * g + P * e
                            sp.dma_start(v[:, :, g, :], w[:, lo:lo + P].rearrange("(k p) n -> p k n", p=P))\
                                .then_inc(loaded[s], 16)
                    elif job in ("mn", "md"):
                        sp.dma_start(st[:, :].rearrange("p (k n) -> p k n", k=KT),
                                     w[:, at + 256 * e:at + 256 * e + 256].rearrange("(k p) n -> p k n", p=P))\
                            .then_inc(loaded[s], 16)
                    else:
                        sp.dma_start(st[:, 0:4 * n].rearrange("p (k n) -> p k n", k=4),
                                     w[512 * e:512 * e + 512, at:at + n].rearrange("(k p) n -> p k n", p=P))\
                            .then_inc(loaded[s], 16)
                elif kind == "ada":
                    sp.dma_start(st[:, :].rearrange("p (k n) -> p k n", k=4),
                                 a["w_ada"][0][512 * e:512 * e + 512, 512 * x:512 * x + 512]
                                 .rearrange("(k p) n -> p k n", p=P)).then_inc(loaded[s], 16)
                elif kind == "cmpw":
                    sp.dma_start(st[:, :].rearrange("p (i n) -> p i n", i=16),
                                 a["cmp_w1"][0][x].rearrange("(i p) n -> p i n", p=P)).then_inc(loaded[s], 16)
                else:
                    v = st[:, :].rearrange("p (n c) -> p n c", n=8)
                    if x == WIN:
                        sp.dma_start(v, a["state_nsa_win_kv"][0, 4 * e:4 * e + 4]
                                     .rearrange("s (h p) x g d -> p (s h) (x g d)", p=PAGE)).then_inc(loaded[s], 16)
                        continue
                    for n in range(8):
                        pg = bass.ds(page(8 * e + n), 1)
                        src = a["cache_nsa_kv"][0, pg, :, 2:4] if x == SLC else a["cache_dsa_kv"][0, pg]
                        sp.dma_start(v[:, n, :], src.rearrange("a p x g d -> (a p) (x g d)")).then_inc(loaded[s], 16)

        @block.gpsimd
        def _(pool):
            pool.memset(cT[:, :, :], 0.0)
            pool.memset(rT[:, R_PE[0]:R_PE[0] + P], 0.0)
            pool.memset(rT[:, R_PE[1]:R_ALL], 0.0).then_inc(zeroed, 1)
            pool.memset(kz[SLC][:, :, :], 0.0)
            pool.memset(kzi[:, :, :], 0.0)
            pool.memset(ckz[:, :, :], 0.0)
            for q in qS:
                pool.memset(q[:, :], 0.0)
            pool.memset(iqz, 0.0).then_inc(zeroed, 1)
            def stores(name, buf, n, prompt, sample):
                pool.dma_start(prompt, stg[:, buf, :].rearrange("p (t n) -> p t n", t=NT)[:, 0:4, n[0]:n[1]])\
                    .then_inc(stored[name], 16)
                pool.dma_start(sample, stg[0:NS, buf, 4 * 512 + n[0]:4 * 512 + n[1]]).then_inc(stored[name], 16)

            def split_lo(n):
                pool.wait_ge(hi_made, n + 1)
                arrived(pool, piece(n)[0])
                if n >= 2:
                    pool.wait_ge(piece_used, n - 1)
                for dst, src, hi in split_views(n, 1):
                    last = pool.tensor_tensor(dst, src, hi.bitcast(F32), ALU.subtract)
                last.then_inc(lo_made, 1)

            split_lo(0)
            split_lo(1)
            for job in range(6):
                if job == 1:
                    pool.dma_start(o["win_s"][0, :, 0:PAST - NEW].rearrange("s w x g d -> s (w x g d)"),
                                   a["state_nsa_win_kv"][0, :, NEW:PAST].rearrange("s w x g d -> s (w x g d)"))\
                        .then_inc(stored["old"], 16)
                for n in before_evac(job):
                    if n < POOL_SPLITS:
                        split_lo(n)
                c0, H = ROPED[job]
                for t in range(NT):
                    r = rows(t)
                    n = NT * job + t
                    dst = stg[0:r, STG[job], 512 * t + c0:512 * t + c0 + HD * H]
                    pool.wait_ge(t_dve, n + 1)
                    pool.tensor_tensor(dst, dst, rope_b[0:r, n % 2, 0:HD * H], ALU.add).then_inc(roped, 1)
                for m in after_evac(job):
                    if m < POOL_SPLITS:
                        split_lo(m)
                if job == 4:
                    pool.wait_ge(aux_done, AUX_AT[("raw", (1, 3))] + 1)
                    pool.memset(cached, 0.0).then_inc(zeroed, 1)
                pool.wait_ge(roped, NT * (job + 1))
                if job == J_IDX:
                    stores("idx", 0, (256, 320), o["idx_p"][0, 0].rearrange("(t p) c -> p t c", p=P),
                           o["idx_s"][0].rearrange("s t c -> (s t) c"))
                elif job == J_KV:
                    pool.wait_ge(t_act, act_tiles(J_KV, 4))
                    stores("kv", 1, (0, 512), o["nsa_p"][0, 0].rearrange("(t p) x g d -> p t (x g d)", p=P),
                           o["nsa_s"][0].rearrange("s t x g d -> (s t) (x g d)"))
                elif job == J_DKV:
                    pool.wait_ge(t_act, act_tiles(J_DKV, 4))
                    stores("dkv", 0, (0, 256), o["dsa_p"][0, 0].rearrange("(t p) x g d -> p t (x g d)", p=P),
                           o["dsa_s"][0].rearrange("s t x g d -> (s t) (x g d)"))
                elif job == J_WIN:
                    pool.wait_ge(t_act, act_tiles(J_WIN, 4))
                    stores("win", 2, (0, 256), o["win_p"][0, 0].rearrange("(t p) x g d -> p t (x g d)", p=P),
                           o["win_s"][0, :, PAST - NEW:PAST].rearrange("s t x g d -> s t (x g d)"))

            for u, unit in enumerate(UNITS):
                if not REAL[u]:
                    continue
                kind, b, _, t = (*unit, 0)[:4]
                pool.wait_ge(r_made, ORD[u] + 1)
                pool.wait_ge(exped, SIG[u + 1])
                s = stats[:, u % 4, :]
                if kind == "P":
                    n = NCP if b == CMP else P * (t + 1)
                    for g in range(2):
                        pool.tensor_scalar(prob[:, u % 4, g, 0:n], prob[:, u % 4, g, 0:n], s[:, 6 + g:7 + g], 1.0,
                                           ALU.mult, ALU.mult).then_inc(scaled, 1)
                else:
                    n = NCS if b == CMP else NKS
                    pool.tensor_scalar(prob[:, u % 4, 0, 0:n], prob[:, u % 4, 0, 0:n], s[:, 6:7], 1.0, ALU.mult,
                                       ALU.mult).then_inc(scaled, 1)

            for t in range(NT):
                pool.wait_ge(y_out, t + 1)
                dst = o["y_s"].rearrange("s t n -> (s t) n") if t == 4 else o["y_p"][0, P * t:P * t + P]
                pool.dma_start(dst, yb[0:rows(t), t, :]).then_inc(stored["y"], 16)
            pool.wait_ge(stored["y"], 16 * NT)
            for name in ("idx", "kv", "dkv", "win"):
                pool.wait_ge(stored[name], 32)
            pool.wait_ge(stored["old"], 16)

        @block.tensor
        def _(pe):
            mm = pe.matmul

            def three(out, left, right, first, last, **kw):
                mm(out, left[0], right[0], start=first, stop=False, skip_group_check=True)
                mm(out, left[1], right[0], start=False, stop=False, skip_group_check=True)
                return mm(out, left[0], right[1], start=False, stop=last, skip_group_check=True)

            pe.wait_ge(in_tab, 16)
            pe.wait_ge(csilu, 1)
            for k in range(KT):
                last = pe.transpose(bank[5][:, 9 * k:9 * k + 9], rb_all[0:9, P * k:P * k + P], ident[0:9, 0:9])
            last.then_inc(c_turned, 1)
            pe.wait_ge(in_small, 48)
            pe.transpose(bank[6][:, 0:8], ng8, ident[0:8, 0:8])
            pe.transpose(bank[6][:, 8:40], pe32, ident[0:32, 0:32]).then_inc(c_turned, 1)

            def modulation(c, e, out, alone):
                if e == 0:
                    mm(out[0:32, :], tb("brow", 6)[:, 32 * c:32 * c + 32], bada[:, :], start=True, stop=False,
                       skip_group_check=True)
                arrived(pe, ("ada", c, e))
                w = staged(("ada", c, e))[:, :].rearrange("p (k n) -> p k n", k=4)
                for k in range(4):
                    last = mm(out[32 * k:32 * k + 32, :], cT[:, 4 * e + k, :], w[:, k, :],
                              start=(k > 0 if e == 0 else alone), stop=(alone or e == 1), skip_group_check=True)
                last.then_inc(pe_freed, 1)

            def turn_x(k):
                for t in range(4):
                    last = pe.transpose(bank[k][:, P * t:P * t + P], xs[:, t, P * k:P * k + P], ident)
                last.then_inc(x_turned, 1)

            pe.wait_ge(cT_made, 1)
            pe.wait_ge(small_made, 1)
            for c in range(4):
                if c >= 2:
                    pe.wait_ge(mod_copied, c - 1)
                for e in range(2):
                    modulation(c, e, bank[5 + c % 2], False)
                pe.wait_ge(pe_freed, 2 * c + 2)
                pe.nop().then_inc(mod_done, 1)
                if c == 1:
                    for t in range(NT):
                        pe.wait_ge(xn_made, t + 1)
                    for k in range(KT):
                        last = pe.transpose(bank[7][:, 256 + NS * k:256 + NS * k + NS], xs[0:NS, 4, P * k:P * k + P],
                                            ident[0:NS, 0:NS])
                    last.then_inc(x_turned, 1)
                    turn_x(0)
                elif c == 2:
                    turn_x(1)
                    turn_x(2)
            turn_x(3)
            turn_x(4)
            pe.wait_ge(mod_copied, 4)
            for w in range(2):
                for k in range(KT):
                    last = mm(bank[7][:, 16 * (w * KT + k):16 * (w * KT + k) + 9],
                              mod[:, D * w + P * k:D * w + P * k + P], tb("gsel"), start=True, stop=True)
            last.then_inc(ab_done, 1)
            turn_x(5)
            turn_x(6)

            def token_major(job, left):
                for n in range(FIRST[job], FIRST[job + 1]):
                    pe.wait_ge(lo_made, n + 1)
                    q = n - FIRST[job]
                    _, _, w = piece(n)
                    if job == 0:
                        pe.wait_ge(h_lo, H_ORDER.index(2 * q + 1) + 1)
                    if JOBS[job] == ("y", 0):
                        pe.wait_ge(mT_lo, 2 * q + 2)
                    final = n == FIRST[job + 1] - 1
                    for t in range(NT):
                        r = rows(t)
                        if q == 0 and 0 < job < G0:
                            pe.wait_ge(t_dve, NT * (job - 1) + t + 1)
                        if q == 0 and job == 0:
                            pe.wait_ge(h_made, H_ORDER.index(t) + 1)
                            if t == 4:
                                pe.wait_ge(h_lo, H_ORDER.index(KT) + 1)
                        if q == 0 and JOBS[job] == ("y", 0):
                            g_read(pe, job - G0 - 1, t // 2)
                            g_read(pe, job - G0 - 2, t // 2)
                        if q == 0 and JOBS[job] == ("y", 1):
                            g_read(pe, job - G0 - 1, t)
                        for i in range(2):
                            k = 2 * q + i
                            last = three(bank[t][0:r, 0:w], [x[:, k, P * t:P * t + r] for x in left],
                                         [w_part(x, n, w)[:, i * w:i * w + w] for x in range(2)],
                                         q == 0 and i == 0, final and i == 1)
                        if final and t < NT - 1:
                            last.then_inc(t_done if job < G0 else g_done, 1)
                    last.then_inc(piece_used, 1)
                    if q == 0 and job == 0:
                        pe.wait_ge(h_made, H_ORDER.index(KT) + 1)
                        turn_x(7)
                    elif q == 0 and job < G0:
                        aux(job)
                    if JOBS[job] == ("y", 0) and q < 2:
                        residual_gate(q)

            def residual_gate(q):
                if q == 0:
                    g_read(pe, len(G_JOBS) - 3, 3)
                    g_read(pe, len(G_JOBS) - 4, 3)
                    pe.wait_ge(gate_spread, 1)
                    for k in range(KT):
                        mm(bank[5 + k // 4][:, P * (k % 4):P * (k % 4) + P], gate_p[:, k, :], ident, start=True, stop=True)
                else:
                    pe.wait_ge(gate_made, 1)
                for k in range(4):
                    last = mm(bank[7][0:NS, P * k:P * k + P], cT[:, 4 * q + k, :], ident, start=True, stop=True)
                last.then_inc(gate_done, 1)

            def feature_major(job):
                kind, c = JOBS[job]
                g = job - G0
                each = blocks_of(job)
                tiles = KT // each
                for n in range(FIRST[job], FIRST[job + 1]):
                    pe.wait_ge(lo_made, n + 1)
                    if n == FIRST[job] and kind in ("un", "ud"):
                        pe.wait_ge(oz_lo, 4 if kind == "un" else 8)
                    left = [w_part(x, n, 512).rearrange("p (k n) -> p k n", k=tiles) for x in range(2)]
                    for x in range(each):
                        b = each * (n - FIRST[job]) + x
                        if g:
                            g_read(pe, g - 1, b)
                        elif b == 2:
                            pe.wait_ge(pt_act, ORD[-1])
                            pe.wait_ge(pt_dve, ORDP[-1])
                        elif b == 3:
                            pe.wait_ge(o_copied, len(OWNERS))
                        out = product(job, b)
                        for k in range(tiles):
                            mov = [y[:, k + (4 if kind == "ud" else 0), :] for y in (oz if each == 2 else hT)]
                            for w, m in ((0, 0), (1, 0), (0, 1)):
                                for h in range(2):
                                    last = mm(out[:, h, :], left[w][:, k, P * x:P * x + P], halves(mov[m])[:, h, :],
                                              start=(k == 0 and w + m == 0), stop=(k == tiles - 1 and m == 1),
                                              skip_group_check=True)
                        if x < each - 1:
                            last.then_inc(g_done, 1)
                    last.then_inc(piece_used, 1)

            def stg_tile(buf, t):
                return stg[0:rows(t), buf, 512 * t:512 * t + 512]

            def turn_tiles(out, pick, m=P):
                for t in range(4):
                    last = pe.transpose(out[0:m, P * t:P * t + P], pick(t), ident)
                return last

            def aux(slot):
                for i, (at, kind, n, _) in enumerate(AUX):
                    if at != slot:
                        continue
                    out = bank[5 + i % 3]
                    if i >= 3:
                        e = AUX[i - 3][3]
                        pe.wait_ge(aux_act if e == "a" else aux_dve, sum(x[3] == e for x in AUX[:i - 2]))
                    if kind == "mod":
                        modulation(*n, out, True)
                        pe.wait_ge(pe_freed, PE_LOADS.index(LOAD_AT[("ada", *n)]) + 1)
                        last = pe.nop()
                    elif kind == "modT":
                        aux_wait(pe, "mod", n)
                        for k in range(4):
                            last = mm(out[:, 16 * k:16 * k + 9], mod_part[:, P * k:P * k + P], tb("gsel"),
                                      start=True, stop=True)
                    elif kind == "qi":
                        pe.wait_ge(roped, NT * (J_IDX + 1))
                        last = turn_tiles(out, lambda t: stg_tile(0, t)[:, P * n:P * n + P])
                    elif kind == "ki":
                        last = turn_tiles(out, lambda t: stg_tile(0, t)[:, 256:320], HD)
                    elif kind == "si":
                        src = stg_tile(0, 4)
                        pe.transpose(out[:, 0:NS], src[:, 0:P], ident[0:NS, 0:NS])
                        pe.transpose(out[:, NS:2 * NS], src[:, P:2 * P], ident[0:NS, 0:NS])
                        last = pe.transpose(out[0:HD, 2 * NS:3 * NS], src[:, 256:320], ident[0:NS, 0:NS])
                    elif kind == "cmpT":
                        pe.wait_ge(t_act, act_tiles(J_KV, 4))
                        last = turn_tiles(out, lambda t: stg_tile(1, t)[:, P * n:P * n + P])
                    elif kind in ("k", "kn"):
                        job, c0 = {SLC: (J_KV, 256), DSA: (J_DKV, 0), WIN: (J_WIN, 0)}[n]
                        pe.wait_ge(roped, NT * (job + 1))
                        if kind == "k":
                            last = turn_tiles(out, lambda t: stg_tile(STG[job], t)[:, c0:c0 + P])
                        else:
                            last = pe.transpose(out[:, 0:NS], stg_tile(STG[job], 4)[:, c0:c0 + P], ident[0:NS, 0:NS])
                    elif kind == "ikT":
                        pe.wait_ge(in_cached, 16 * 16)
                        for m in range(4):
                            at = HD * (4 * n + m)
                            last = pe.transpose(out[0:HD, P * m:P * m + P], cached[:, at:at + HD], ident)
                    elif kind == "sdots":
                        pe.wait_ge(iq_laid, 1)
                        for m in range(4):
                            aux_wait(pe, "ikT", m)
                        for s in range(NSEQ):
                            mm(out[:, 0:PAST], iqz[:, P * s:P * s + P], ikTs[:, PAST * s:PAST * s + PAST],
                               start=(s == 0), stop=(s == NSEQ - 1))
                        last = mm(out[:, PAST:NKS], iqa, kni[:, :], start=True, stop=True)
                    elif kind == "ssum":
                        pe.wait_ge(sdots_weighted, 1)
                        last = mm(out[0:NS, 0:NKS], tb("hsum"), relu_s[:, :], start=True, stop=True)
                    elif kind == "dots":
                        t, h = n
                        aux_wait(pe, "qi", h // 2)
                        aux_wait(pe, "ki", 0)
                        last = mm(out[:, 0:P * (t + 1)], qTi[:, h // 2, P * t:P * t + P],
                                  kzi[:, h % 2, 0:P * (t + 1)], start=True, stop=True)
                    elif kind in ("q", "qs"):
                        which, j = n if kind == "q" else (n, 0)
                        job, buf = {PLAIN: (J_NQ, 2), ROT: (J_NQ, 0), DSAQ: (J_DQ, 1)}[which]
                        if which == PLAIN:
                            pe.wait_ge(t_act, act_tiles(J_NQ, 4))
                        else:
                            pe.wait_ge(roped, NT * (job + 1))

                        def pair(t, j):
                            return stg_tile(buf, t)[:, P * j:P * j + P]
                        if kind == "q":
                            last = turn_tiles(out, lambda t: pair(t, j))
                        else:
                            for j in range(4):
                                last = pe.transpose(out[:, NS * j:NS * j + NS], pair(4, j), ident[0:NS, 0:NS])
                    elif kind == "raw":
                        s, m = n
                        pe.wait_ge(in_cached, 16 * 16 * (s + 2))
                        src = cached
                        src = src.rearrange("p (s r c) -> p s r c", s=NSEQ, r=2)
                        for x in range(4):
                            last = pe.transpose(out[:, P * x:P * x + P], src[:, 2 * m + x // 2, x % 2, :], ident)
                    elif kind == "hid":
                        arrived(pe, ("cmpw", n, 0))
                        for m in range(4):
                            aux_wait(pe, "raw", (n, m))
                        aux_wait(pe, "cmpT", 0)
                        aux_wait(pe, "cmpT", 1)
                        w1 = staged(("cmpw", n, 0))[:, :].rearrange("p (i n) -> p i n", i=16)
                        for i in range(16):
                            at = R_BASE[n] + i
                            last = mm(out[:, 0:R_COLS], w1[:, i, :], rT[:, at:at + 21 * P]
                                      .rearrange("p (x c) -> p x c", c=P)[:, :, 0:121:8], start=(i == 0), stop=(i == 15))
                        last.then_inc(pe_freed, 1)
                        pe.wait_ge(pe_freed, PE_LOADS.index(LOAD_AT[("cmpw", n, 0)]) + 1)
                        last = pe.nop()
                    elif kind == "ck":
                        aux_wait(pe, "hid", 0)
                        pe.wait_ge(in_w2, 16)
                        for g in range(2):
                            mm(out[64 * g:64 * g + 64, 0:NCP], w2[:, 0, :], aT[:, 32 * g:32 * g + NCP],
                               start=True, stop=True)
                            last = mm(out[64 * g:64 * g + 64, 32:32 + NSEQ * NCS], w2[:, 0, :],
                                      aT[:, r_col(0, R_SAMPLE):R_COLS]
                                      .rearrange("p (s g n) -> p s g n", s=NSEQ, g=2)[:, :, g, 0:NCS],
                                      start=True, stop=True)
                    elif kind == "cvp":
                        aux_wait(pe, "hid", 1)
                        for g in range(2):
                            at = r_col(1, R_PROMPT[1]) + 32 * g
                            last = mm(out[0:NCP, HD * g:HD * g + HD], aT[:, at:at + NCP],
                                      w2[:, 1, :], start=True, stop=True)
                    elif kind == "cvs":
                        for x in range(8):
                            at = 16 * (8 * n + x)
                            last = mm(out[0:NCS, HD * x:HD * x + HD], aT[:, at:at + NCS], w2[:, 1, :],
                                      start=True, stop=True)
                    elif kind == "selx":
                        pe.wait_ge(sel_made, 1)
                        last = mm(out[:, 0:NKS], tb("expand", NS)[:, P * n:P * n + P], scoreS[:, :], start=True,
                                  stop=True)
                    elif kind == "grow":
                        pe.wait_ge(t_act, act_tiles(J_WIN, 4))
                        last = mm(out[:, 0:24], tb("expand", NS)[:, P * n:P * n + P], gates[0:NS, 4, :], start=True,
                                  stop=True)
                    last.then_inc(aux_done, 1)

            pe.wait_ge(in_tab2, 16)
            for job in range(G0):
                token_major(job, hT)

            def keys(b, t):
                return NCP if b == CMP else P * (t + 1)

            def bank_free(h):
                if h < 4:
                    pe.wait_ge(t_dve, NT * (G0 - 1) + h + 1)
                    return
                u = max(i for i in range(len(UNITS)) if AT[i] <= h - 4)
                if UNITS[u][0] in "KT":
                    pe.wait_ge(exped if h - 4 > AT[u] else masked, SIG[u] + 1)
                else:
                    pe.wait_ge(exped, SIG[u] + h - 4 - AT[u] + 1)

            def scores(u):
                unit = UNITS[u]
                kind, b = unit[:2]
                out = [bank[(AT[u] + g) % 4] for g in range(2)]
                bank_free(AT[u])
                if kind in "PS" and b == DSA:
                    n = UNITS.index(("T", DSA))
                    pe.wait_ge(exped, SIG[n + 1])
                    pe.wait_ge(masked, SIG[n + 1])
                    pe.wait_ge(t_act, act_tiles(J_DKV, 4))
                if kind == "T":
                    pe.wait_ge(roped, NT * (J_DKV + 1))
                    turn_tiles(out[0], lambda t: stg_tile(STG[J_DKV], t)[:, 0:P]).then_inc(s_done, 1)
                    bank_free(AT[u] + 1)
                    pe.transpose(out[1][:, 0:NS], stg_tile(STG[J_DKV], 4)[:, 0:P], ident[0:NS, 0:NS]).then_inc(s_done, 1)
                elif kind == "P":
                    j, t = unit[2:]
                    left = qT[PLAIN if b == CMP else ROT if b < DSA else DSAQ][:, j, P * t:P * t + P]
                    for g in range(2):
                        if g:
                            bank_free(AT[u] + 1)
                        right = ckz[:, g, 0:NCP] if b == CMP else kz[b][:, g, 0:P * (t + 1)]
                        mm(out[g][:, 0:keys(b, t)], left, right, start=True, stop=True).then_inc(s_done, 1)
                elif kind == "K":
                    key = ("kv", b, unit[2])
                    arrived(pe, key)
                    raw = staged(key)[:, :].rearrange("p (n c) -> p n c", n=8)
                    for g in range(2):
                        if g:
                            bank_free(AT[u] + 1)
                        for n in range(4):
                            last = pe.transpose(out[g][:, P * n:P * n + P], raw[:, 4 * g + n, 0:P], ident)
                        last.then_inc(s_done, 1)
                else:
                    T = unit[2]
                    q = qS[PLAIN if b == CMP else ROT if b < DSA else DSAQ][:, P * T:P * T + P]
                    if b != CMP:
                        n = UNITS.index(("K", b, T))
                        pe.wait_ge(exped, SIG[n + 1])
                        pe.wait_ge(masked, SIG[n + 1])
                    for s in range(4):
                        right = (ckS[:, NCS * (4 * T + s):NCS * (4 * T + s) + NCS] if b == CMP
                                 else kTs[:, kv_slot(b, T), s, :])
                        last = mm(out[0][32 * s:32 * s + 32, 0:NCS if b == CMP else PAST], q[:, 32 * s:32 * s + 32],
                                  right, start=True, stop=True)
                    if b != CMP:
                        last = mm(out[0][:, PAST:NKS], q, knew[b][:, :], start=True, stop=True)
                    last.then_inc(s_done, 1)

            def turn(u):
                unit = UNITS[u]
                if not REAL[u]:
                    return
                kind, b = unit[:2]
                src = prob[:, u % 4]
                for g in range(2 if kind == "P" else 1):
                    pe.wait_ge(scaled, TURNS[u] + g + 1)
                    if g and ORDP[u]:
                        pe.wait_ge(pt_dve, ORDP[u])
                    elif not g and ORD[u]:
                        pe.wait_ge(pt_act, ORD[u])
                    if kind == "P" and b != CMP:
                        for n in range(unit[3] + 1):
                            last = pe.transpose(bank[4 + g][:, P * n:P * n + P], src[:, g, P * n:P * n + P], ident)
                    elif b == CMP:
                        n = NCP if kind == "P" else NCS
                        last = pe.transpose(bank[4 + g][0:n, 0:P], src[:, g, 0:n], ident)
                    else:
                        for n in range(2):
                            pe.transpose(bank[4][:, P * n:P * n + P], src[:, 0, P * n:P * n + P], ident)
                        last = pe.transpose(bank[4][0:NS, PAST:PAST + P], src[:, 0, PAST:NKS], ident)
                    last.then_inc(pt_done, 1)

            def values(u):
                unit = UNITS[u]
                if not REAL[u]:
                    return
                kind, b = unit[:2]
                w = owner(unit)
                out = bank[6 + w % 2]
                first = u == FIRST_OF[w]
                final = u == LAST_OF[w]
                pe.wait_ge(pt_act, ORD[u] + 1)
                pe.wait_ge(pt_dve, ORDP[u + 1])
                if first and w >= 2:
                    pe.wait_ge(o_copied, w - 1)
                pt = probT[:, ORD[u] % 2]
                if kind == "P":
                    t = unit[3]
                    blocks = [(n, P) for n in range(t + 1)] if b != CMP else [(0, NCP)]
                    for n, m in blocks:
                        for g in range(2):
                            v = cvP[0:m, HD * g:HD * g + HD] if b == CMP else V[b][:, n, HD * g:HD * g + HD]
                            last = mm(out[64 * g:64 * g + 64, P * t:P * t + P], v, pt[0:m, g, P * n:P * n + P],
                                      start=(first and n == 0), stop=final, skip_group_check=True)
                elif b == CMP:
                    for s in range(4):
                        last = mm(out[:, 32 * s:32 * s + 32], cvS[0:NCS, 4 * unit[2] + s, :],
                                  pt[0:NCS, 0, 32 * s:32 * s + 32], start=(first and s == 0), stop=final,
                                  skip_group_check=True)
                else:
                    T = unit[2]
                    mm(out[:, 0:P], V[b][0:NS, 4, :], pt[0:NS, 0, PAST:PAST + P], start=first, stop=False,
                       skip_group_check=True)
                    raw = staged(("kv", b, T))[:, :].rearrange("p (n c) -> p n c", n=8)
                    for s in range(4):
                        for n in range(2):
                            last = mm(out[:, 32 * s:32 * s + 32], raw[:, 2 * s + n, P:2 * P],
                                      pt[:, 0, P * n + 32 * s:P * n + 32 * s + 32], start=False, stop=final,
                                      skip_group_check=True)
                    last.then_inc(pe_freed, 1)
                    pe.wait_ge(pe_freed, PE_LOADS.index(LOAD_AT[("kv", b, T)]) + 1)
                    last = pe.nop()
                last.then_inc(pv_done, 1)

            pe.wait_ge(aux_act, sum(x[3] == "a" for x in AUX))
            pe.wait_ge(aux_dve, sum(x[3] == "v" for x in AUX))
            for i in range(len(UNITS) + LAG + 1):
                if i < len(UNITS):
                    scores(i)
                if 0 <= i - LAG < len(UNITS):
                    turn(i - LAG)
                if 0 <= i - LAG - 1 < len(UNITS):
                    values(i - LAG - 1)

            pe.wait_ge(exped, SIG[-1])
            for job in range(G0, len(JOBS)):
                if JOBS[job][0] == "y":
                    token_major(job, mT)
                else:
                    feature_major(job)

        @block.scalar
        def _(act):
            A = act.activation
            told = {}
            latest = []

            def tell(s):
                told[id(s)] = told.get(id(s), 0) + 1
                latest[:] = [s, told[id(s)]]
                return s, 1

            def own():
                if latest:
                    act.wait_ge(*latest)

            def link(ins):
                ins.then_inc(*tell(act_step))
                own()

            for t in range(NT):
                src = a["x_sample"].rearrange("s t n -> (s t) n") if t == 4 else a["x_prompt"][0, P * t:P * t + P]
                act.dma_start(xs[0:rows(t), t, :], src).then_inc(in_x[t], 16)
            act.wait_ge(in_c, 32)
            A(rb_all[0:9, :], c_raw[0:9, :], ACT.Silu).then_inc(*tell(csilu))
            for t in range(NT):
                act.wait_ge(in_x[t], 16)
                if t:
                    act.wait_ge(squared, t)
                A(rTs[0:rows(t), 0:D], xs[0:rows(t), t, :], ACT.Square, accum_out=norm[0:rows(t), t:t + 1])\
                    .then_inc(*tell(squared))
            act.wait_ge(ms_made, 2)
            A(norm[:, 16:20], norm[:, 8:12], ACT.Sqrt)
            A(norm[0:NS, 20:21], norm[0:NS, 12:13], ACT.Sqrt).then_inc(*tell(rooted))
            for c in range(4):
                act.wait_ge(mod_done, c + 1)
                if c == 3:
                    act.dma_start(tab[:, TAB_A:NTAB], a["tables"][:, TAB_A:NTAB]).then_inc(in_tab2, 16)
                    act.dma_start(w2[:, :, :], a["cmp_w2"][0].rearrange("s p d -> p s d")).then_inc(in_w2, 16)
                A(mod[:, 512 * c:512 * c + 512], bank[5 + c % 2][:, :], ACT.Copy).then_inc(*tell(mod_copied))
            def split_hi(n):
                own()
                arrived(act, piece(n)[0])
                if n >= 2:
                    act.wait_ge(piece_used, n - 1)
                for dst, src, _ in split_views(n, 0):
                    last = A(dst, src, ACT.Copy)
                last.then_inc(*tell(hi_made))

            split_hi(0)
            split_hi(1)
            for i, k in enumerate(H_ORDER):
                act.wait_ge(h_made, i + 1)
                own()
                A(h_part(hT[0], k), h_flat(i, k), ACT.Copy).then_inc(*tell(h_hi))

            def read_tiles(job):
                if not ACT_READS[job]:
                    return
                if job == J_KV:
                    act.wait_ge(x_turned, KT + 1)
                if job == J_NQ:
                    act.wait_ge(ab_done, 1)
                if job == J_DKV:
                    act.wait_ge(aux_done, aux_last_read(J_NQ))
                if job == J_WIN:
                    act.wait_ge(aux_done, aux_last_read(J_NQ))
                for t in range(NT):
                    r = rows(t)
                    tile_ready(act, job, t)
                    own()
                    ps = bank[t][0:r, :]
                    st = stg[0:r, STG[job], 512 * t:512 * t + 512]
                    if job == J_IDX:
                        last = A(iw[0:r, t, :], ps[:, 320:324], ACT.Copy)
                    elif job == J_KV:
                        A(st[:, 0:256], ps[:, 0:256], ACT.Copy)
                        A(st[:, 384:512], ps[:, 384:512], ACT.Copy)
                        last = A(V[SLC][0:r, t, :], ps[:, 384:512], ACT.Copy)
                    elif job == J_NQ:
                        last = A(by_pair(stg[0:r, 2, 512 * t:512 * t + 512]), by_group(ps[:, :]), ACT.Copy)
                    else:
                        A(st[:, 128:256], ps[:, 128:256], ACT.Copy)
                        last = A(V[DSA if job == J_DKV else WIN][0:r, t, :], ps[:, 128:256], ACT.Copy)
                        if job == J_WIN:
                            last = A(gates[0:r, t, :], ps[:, 256:280], ACT.Sigmoid)
                    last.then_inc(*tell(t_act))

            def aux(slot):
                for i, (at, kind, n, e) in enumerate(AUX):
                    if at != slot or e != "a":
                        continue
                    src = bank[5 + i % 3]
                    own()
                    if kind == "hid":
                        act.wait_ge(aux_done, i + 1)
                        if n:
                            act.wait_ge(aux_done, AUX_AT[("ck", 0)] + 1)
                        at = r_col(n, R_PE[n])
                        link(A(norm[:, 31:32], src[:, at:at + 1], ACT.Copy))
                        A(aT[:, :], src[:, 0:R_COLS], ACT.Silu, bias=norm[:, 31:32]).then_inc(*tell(aux_act))
                        continue
                    if kind == "dots":
                        d = DOTS.index(n)
                        if d >= 2:
                            act.wait_ge(score_added, d - 1)
                        act.wait_ge(aux_done, i + 1)
                        m = P * (n[0] + 1)
                        A(relu_d[:, d % 2, 0:m], src[:, 0:m], ACT.Relu, scale=IDX_SCALE).then_inc(*tell(aux_act))
                        continue
                    act.wait_ge(aux_done, i + 1)
                    if kind == "k" and n == WIN:
                        act.wait_ge(zeroed, 3)
                    if kind == "mod":
                        A(mod_part, src[:, :], ACT.Copy).then_inc(*tell(aux_act))
                        continue
                    if kind == "sdots":
                        A(relu_s[:, :], src[:, 0:NKS], ACT.Relu, scale=IDX_SCALE).then_inc(*tell(aux_act))
                        continue
                    if kind == "selx":
                        A(selS[:, n, :], src[:, 0:NKS], ACT.Copy).then_inc(*tell(aux_act))
                        continue
                    moves(kind, n, src, lambda o, x: A(o, x, ACT.Copy)).then_inc(*tell(aux_act))

            for job in range(G0):
                aux(job)
                for n in before_evac(job):
                    split_hi(n)
                read_tiles(job)
                for n in after_evac(job):
                    split_hi(n)

            act.wait_ge(aux_done, len(AUX))
            act.wait_ge(aux_dve, sum(x[3] == "v" for x in AUX))
            for i in range(len(UNITS) + LAG):
                u = i - LAG
                if u >= 0 and REAL[u]:
                    kind, b = UNITS[u][:2]
                    act.wait_ge(pt_done, TURNS[u] + 1)
                    if ORD[u] == 0:
                        act.wait_ge(stored["win"], 32)
                    own()
                    if ORD[u] >= 2:
                        act.wait_ge(pv_done, ORD[u] - 1)
                    pt = probT[:, ORD[u] % 2]
                    if kind == "P" and b == CMP:
                        x = A(pt[0:NCP, 0, 0:P], bank[4][0:NCP, 0:P], ACT.Copy)
                    elif kind == "P":
                        n = P * (UNITS[u][3] + 1)
                        x = A(pt[:, 0, 0:n], bank[4][:, 0:n], ACT.Copy)
                    elif b == CMP:
                        x = A(pt[0:NCS, 0, 0:P], bank[4][0:NCS, 0:P], ACT.Copy)
                    else:
                        A(pt[:, 0, 0:PAST], bank[4][:, 0:PAST], ACT.Copy)
                        x = A(pt[0:NS, 0, PAST:PAST + P], bank[4][0:NS, PAST:PAST + P], ACT.Copy)
                    x.then_inc(*tell(pt_act))
                if i < len(UNITS):
                    kind, b = UNITS[i][:2]
                    src = [bank[(AT[i] + g) % 4] for g in range(2)]
                    s = stats[:, i % 4, :]
                    if i >= 4 and REAL[i - 4]:
                        act.wait_ge(pt_done, TURNS[i - 3])
                    if kind == "K":
                        act.wait_ge(s_done, AT[i] + 2)
                        act.wait_ge(roped, NT * G0)
                        own()
                        m = KV_ORDER.index((b, UNITS[i][2]))
                        if m >= 2:
                            act.wait_ge(s_done, AT[UNITS.index(("S", *KV_ORDER[m - 2])) + 1])
                        A(kTs[:, m % 2, 2:4, :].rearrange("p s n -> p (s n)"), src[1][:, :], ACT.Copy)\
                            .then_inc(*tell(exped))
                    elif kind == "T":
                        act.wait_ge(s_done, AT[i] + 2)
                        own()
                        A(knew[DSA][:, :], src[1][:, 0:NS], ACT.Copy).then_inc(*tell(exped))
                    else:
                        n = (P * (UNITS[i][3] + 1) if kind == "P" else NKS) if b != CMP else NCP if kind == "P" else NCS
                        for g in range(2 if kind == "P" else 1):
                            act.wait_ge(masked, SIG[i] + g + 1)
                            own()
                            A(prob[:, i % 4, g, 0:n], src[g][:, 0:n], ACT.Exp, bias=s[:, 2 + g:3 + g],
                              scale=-1.0, accum_out=s[:, 4 + g:5 + g]).then_inc(*tell(exped))

            for job in range(G0, len(JOBS)):
                g = job - G0
                kind, c = JOBS[job]
                if kind == "mn" and c == 0:
                    act.wait_ge(oz_lo, 8)
                    for t in range(NT):
                        src = (a["x_sample"].rearrange("s t n -> (s t) n") if t == 4
                               else a["x_prompt"][0, P * t:P * t + P])
                        act.dma_start(yb[0:rows(t), t, :], src).then_inc(in_xy, 16)
                    act.dma_start(fgb[:, :], a["final_g"].rearrange("(a n) -> a n", a=1).to_broadcast([P, D]))\
                        .then_inc(in_fg, 16)
                for t in range(4 if kind != "y" else 0):
                    if t % blocks_of(job) == 0:
                        split_hi(FIRST[job] + t // blocks_of(job) + 2)
                    if kind == "z":
                        n = 4 * c + t
                        tile_ready(act, job, t)
                        own()
                        if n >= 2:
                            act.wait_ge(z_mul, n - 1)
                        A(halves(zs[:, n % 2, :]), product(job, t), ACT.Silu).then_inc(*tell(g_act))
                        act.wait_ge(z_mul, n + 1)
                        A(oz[0][:, n, :], oT[:, n, :], ACT.Copy).then_inc(*tell(oz_hi))
                    elif kind in ("mn", "md"):
                        tile_ready(act, job, t)
                        own()
                        if c == 1:
                            act.wait_ge(g_dve, GV[g - 3] + t + 1)
                        A(part(sg if kind == "mn" else sg2, t), product(job, t), ACT.Sigmoid).then_inc(*tell(g_act))
                    elif kind == "ud":
                        act.wait_ge(m_made, 4 * c + t + 1)
                        own()
                        A(mT[0][:, 4 * c + t, :], mt[:, t, :], ACT.Copy).then_inc(*tell(mT_hi))
                if kind == "y":
                    for n in before_evac(job):
                        split_hi(n)
                    for i in range(NT + c):
                        if i < NT:
                            r = rows(i)
                            act.wait_ge(y_sum, NT * c + i + 1)
                            own()
                            A(mt[0:r, 0, 0:512], yb[0:r, i, 512 * c:512 * c + 512], ACT.Square,
                              accum_out=norm[0:r, 2 * i + c:2 * i + c + 1]).then_inc(*tell(y_sq))
                        if c and i:
                            t = i - 1
                            r = rows(t)
                            own()
                            act.wait_ge(y_ms, t + 1)
                            A(norm[0:r, 18 + t:19 + t], norm[0:r, 12 + t:13 + t], ACT.Sqrt).then_inc(*tell(y_root))
                    for n in after_evac(job):
                        split_hi(n)

        @block.vector
        def _(dve):
            told = {}
            latest = []

            def tell(s):
                told[id(s)] = told.get(id(s), 0) + 1
                latest[:] = [s, told[id(s)]]
                return s, 1

            def own():
                if latest:
                    dve.wait_ge(*latest)

            def link(ins):
                ins.then_inc(*tell(dve_step))
                own()

            tt, ts, stt, cp = dve.tensor_tensor, dve.tensor_scalar, dve.scalar_tensor_tensor, dve.tensor_copy

            dve.wait_ge(c_turned, 1)
            dve.wait_ge(zeroed, 1)
            cp(cT[:, :, 0:9], bank[5][:, 0:72].rearrange("p (k n) -> p k n", k=KT)).then_inc(*tell(cT_made))
            dve.wait_ge(c_turned, 2)
            cp(gT[:, :], bank[6][:, 0:8])
            cp(rT[:, R_PE[0]:R_PE[0] + 16], bank[6][:, 8:24])
            cp(rT[:, R_PE[1]:R_PE[1] + 16], bank[6][:, 24:40]).then_inc(*tell(small_made))
            dve.wait_ge(squared, NT)
            ts(norm[:, 8:12], norm[:, 0:4], 1.0 / D, EPS, ALU.mult, ALU.add).then_inc(*tell(ms_made))
            ts(norm[0:NS, 12:13], norm[0:NS, 4:5], 1.0 / D, EPS, ALU.mult, ALU.add).then_inc(*tell(ms_made))
            dve.wait_ge(rooted, 1)
            link(dve.reciprocal(norm[:, 24:28], norm[:, 16:20]))
            link(dve.reciprocal(norm[0:NS, 28:29], norm[0:NS, 20:21]))
            for t in range(NT):
                r = rows(t)
                ts(xs[0:r, t, :], xs[0:r, t, :], norm[0:r, 24 + t:25 + t], None, ALU.mult).then_inc(*tell(xn_made))
            dve.wait_ge(small_made, 1)
            dve.wait_ge(ab_done, 1)
            mod_ps = bank[7][:, 0:256].rearrange("p (w k n) -> p w k n", w=2, k=KT)[:, :, :, 0:9]
            cp(AB[:, 0], mod_ps[:, 0])
            stt(out=AB[:, 1], in0=mod_ps[:, 1], scalar=1.0, in1=spread(gT[:, :], 2, 9), op0=ALU.add, op1=ALU.mult)\
                .then_inc(*tell(ab_made))
            dve.wait_ge(ab_made, 1)

            def lo_of_h(i):
                own()
                dve.wait_ge(h_hi, i + 1)
                k = H_ORDER[i]
                tt(h_part(hT[1], k), h_flat(i, k), h_part(hT[0], k).bitcast(F32), ALU.subtract).then_inc(*tell(h_lo))

            for i, k in enumerate(H_ORDER):
                if k == KT:
                    dve.wait_ge(x_turned, 1)
                    own()
                    tmp = h_flat(i, k).rearrange("p k (s t) -> p k s t", s=NSEQ)
                    link(tt(tmp, bank[7][:, 256:256 + KT * NS].rearrange("p (k s t) -> p k s t", k=KT, s=NSEQ),
                            spread(AB[:, 1, :, 1:9], 3, NEW), ALU.mult))
                    tt(tmp, tmp, spread(AB[:, 0, :, 1:9], 3, NEW), ALU.add).then_inc(*tell(h_made))
                else:
                    dve.wait_ge(x_turned, k + 2)
                    own()
                    ts(h_flat(i, k), bank[k][:, :], AB[:, 1, k, 0:1], AB[:, 0, k, 0:1], ALU.mult, ALU.add)\
                        .then_inc(*tell(h_made))
                if i:
                    lo_of_h(i - 1)
            lo_of_h(KT)
            dve.wait_ge(in_tab2, 16)

            def split_lo(n):
                own()
                dve.wait_ge(hi_made, n + 1)
                arrived(dve, piece(n)[0])
                for dst, src, hi in split_views(n, 1):
                    last = tt(dst, src, hi.bitcast(F32), ALU.subtract)
                last.then_inc(*tell(lo_made))

            def read_tiles(job):
                c0, H = ROPED[job]
                if job == J_IDX:
                    dve.wait_ge(x_turned, KT + 1)
                if job == J_NQ:
                    dve.wait_ge(stored["idx"], 32)
                    dve.wait_ge(aux_done, aux_last_read(J_IDX))
                if job == J_DQ:
                    dve.wait_ge(stored["kv"], 32)
                    dve.wait_ge(aux_done, aux_last_read(J_KV))
                if job in (J_DKV, J_WIN):
                    dve.wait_ge(aux_done, aux_last_read(J_NQ))
                for t in range(NT):
                    r = rows(t)
                    n = NT * job + t
                    tile_ready(dve, job, t)
                    if ACT_READS[job]:
                        dve.wait_ge(t_act, act_tiles(job, t))
                    own()
                    if n >= 2:
                        dve.wait_ge(roped, n - 1)
                    x = bank[t][0:r, c0:c0 + HD * H]
                    ra = stg[0:r, STG[job], 512 * t + c0:512 * t + c0 + HD * H]
                    rb = rope_b[0:r, n % 2, 0:HD * H]
                    cos = tb("cos", r)[:, HD * t:HD * t + HD]
                    sin = tb("sin", r)[:, HD * t:HD * t + HD]
                    if H == 8:
                        x, ra, rb = by_group(x), by_pair(ra), by_pair(rb)
                        cos, sin = (spread(spread(y, 1, 4), 1, 2) for y in (cos, sin))
                    else:
                        x, ra, rb = (y.rearrange("p (h d) -> p h d", h=H) for y in (x, ra, rb))
                        cos, sin = (spread(y, 1, H) for y in (cos, sin))
                    tt(ra, x, cos, ALU.mult)
                    tt(rb[..., 0:32], x[..., 32:64], sin[..., 0:32], ALU.mult)
                    tt(rb[..., 32:64], x[..., 0:32], sin[..., 32:64], ALU.mult).then_inc(*tell(t_dve))

            def aux(slot):
                for i, (at, kind, n, e) in enumerate(AUX):
                    if at != slot:
                        continue
                    src = bank[5 + i % 3]
                    own()
                    if kind == "dots":
                        d = DOTS.index(n)
                        t, h = n
                        m = P * (t + 1)
                        aux_wait(dve, "dots", n)
                        dve.wait_ge(t_act, act_tiles(J_IDX, 4))
                        if d:
                            dve.wait_ge(score_added, d)
                        acc = tb("mrow")[:, SEQ - m:SEQ] if h == 0 else score[:, t - 1, 0:m]
                        stt(out=score[:, t - 1, 0:m], in0=relu_d[:, d % 2, 0:m], scalar=iw[:, t, h:h + 1], in1=acc,
                            op0=ALU.mult, op1=ALU.add).then_inc(*tell(score_added))
                        continue
                    if kind == "sdots":
                        aux_wait(dve, "sdots", 0)
                        dve.wait_ge(t_act, act_tiles(J_IDX, 4))
                        for h in range(4):
                            x = cp(iwr[NS * h:NS * h + NS, :], iw[0:NS, 4, h:h + 1])
                        link(x)
                        ts(relu_s[:, :], relu_s[:, :], iwr[:, 0:1], None, ALU.mult).then_inc(*tell(sdots_weighted))
                        continue
                    if e != "v":
                        continue
                    if kind == "modT":
                        dve.wait_ge(aux_done, i + 1)
                        own()
                        c, e = n
                        dst = gateT[:, 4 * (c - 4):4 * (c - 4) + 4, :]
                        part_t = src[:, 0:64].rearrange("p (k n) -> p k n", k=4)[:, :, 0:9]
                        if e == 0:
                            cp(dst, part_t).then_inc(*tell(aux_dve))
                        else:
                            tt(dst, dst, part_t, ALU.add).then_inc(*tell(aux_dve))
                        continue
                    if kind == "ck":
                        rounds(2, 8)
                    elif kind == "cvp":
                        rounds(2, 4)
                        rounds(3, 4)
                    dve.wait_ge(aux_done, i + 1)
                    if kind == "ssum":
                        tt(scoreS[:, :], src[0:NS, 0:NKS], tb("midx", NS), ALU.add).then_inc(*tell(aux_dve))
                    elif kind == "grow":
                        link(tt(gtmp[:, :], src[:, 0:24], tb("headmask"), ALU.mult))
                        dve.tensor_reduce(grow[:, n, :], gtmp[:, :].rearrange("p (h b) -> p b h", b=3), AX.X, ALU.add)\
                            .then_inc(*tell(aux_dve))
                    elif kind == "si":
                        cp(qTi[:, :, SEQ:TOK], src[:, 0:2 * NS].rearrange("p (j n) -> p j n", j=2))
                        cp(kni[:, :], src[0:HD, 2 * NS:3 * NS]).then_inc(*tell(aux_dve))
                        aux_wait(dve, "si", 0)
                        dve.wait_ge(zeroed, 2)
                        for h in range(4):
                            x = qTi[64 * (h % 2):64 * (h % 2) + 64, h // 2, SEQ:TOK]
                            dst = bass.AP(iqz.tensor, iqz.offset + NS * h, [iqz.ap[0], [P + NEW, NSEQ], [1, NEW]])
                            cp(dst, x.rearrange("p (s t) -> p s t", s=NSEQ))
                            y = cp(iqa[:, NS * h:NS * h + NS], x)
                        y.then_inc(*tell(iq_laid))
                    else:
                        moves(kind, n, src, lambda o, x: cp(o, x)).then_inc(*tell(aux_dve))

            def take_top(row, n):
                link(dve.max(top8[0:n, :], row))
                link(dve.match_replace(out=row, in_to_replace=top8[0:n, :], in_values=row, imm_value=TAKEN))

            def rounds(t, count):
                for _ in range(count):
                    take_top(score[:, t - 1, 0:P * (t + 1)], P)

            def mask_rest(row):
                own()
                return ts(row, row, 0.99 * TAKEN, NEG, ALU.is_gt, ALU.mult)

            def select_samples():
                dve.wait_ge(aux_dve, sum(x[3] == "v" for x in AUX[:AUX_AT[("ssum", 0)] + 1]))
                dve.wait_ge(score_added, len(DOTS))
                for n in range(TOPK_S // 8):
                    take_top(scoreS[:, :], NS)
                link(dve.max(top8[0:NS, :], scoreS[:, :]))
                link(dve.memset(top8[0:NS, TOPK_S % 8:8], TAKEN))
                link(dve.match_replace(out=scoreS[:, :], in_to_replace=top8[0:NS, :], in_values=scoreS[:, :],
                                       imm_value=TAKEN))
                mask_rest(scoreS[:, :]).then_inc(*tell(sel_made))

            dve.wait_ge(zeroed, 2)
            for job in range(G0):
                aux(job)
                if job == 2:
                    rounds(1, 16)
                elif job == 3:
                    select_samples()
                    rounds(2, 4)
                elif job > 3:
                    rounds(3, 4)
                read_tiles(job)
            dve.wait_ge(t_act, act_tiles(J_WIN, 4))
            gv = gates[:, 0, :].rearrange("p (h b) -> p h b", b=3)[:, :, 0]
            link(ts(gv, gv, tb("vis"), None, ALU.mult))

            dve.wait_ge(aux_act, sum(x[3] == "a" for x in AUX))

            def mask_max(u):
                own()
                kind, b = UNITS[u][:2]
                src = [bank[(AT[u] + g) % 4] for g in range(2)]
                s = stats[:, u % 4, :]
                if kind == "T":
                    dve.wait_ge(s_done, AT[u] + 1)
                    dve.wait_ge(zeroed, 3)
                    for g in range(2):
                        x = cp(kz[DSA][64 * g:64 * g + 64, g, :], src[0][64 * g:64 * g + 64, :])
                    x.then_inc(*tell(masked))
                    return
                if kind == "K":
                    m = KV_ORDER.index((b, UNITS[u][2]))
                    dve.wait_ge(s_done, AT[u] + 1)
                    dve.wait_ge(roped, NT * G0)
                    dve.wait_ge(stored["win"], 32)
                    if m >= 2:
                        dve.wait_ge(s_done, AT[UNITS.index(("S", *KV_ORDER[m - 2])) + 1])
                    cp(kTs[:, m % 2, 0:2, :].rearrange("p s n -> p (s n)"), src[0][:, :]).then_inc(*tell(masked))
                    return
                if u >= 4 and REAL[u - 4]:
                    dve.wait_ge(scaled, TURNS[u - 3])
                if kind == "P":
                    t = UNITS[u][3]
                    n = NCP if b == CMP else P * (t + 1)
                    m = (tb("mcmp")[:, 32 * t:32 * t + NCP] if b == CMP else
                         score[:, t - 1, 0:n] if b == DSA and t else tb("mrow")[:, SEQ - n:SEQ])
                    g2 = 2
                else:
                    T = UNITS[u][2]
                    n = NCS if b == CMP else NKS
                    m = (tb("mrow")[:, 0:n] if b == CMP else selS[:, T, :] if b == DSA
                         else tb("msamp")[:, NKS * T:NKS * T + NKS])
                    g2 = 1
                for g in range(g2):
                    dve.wait_ge(s_done, AT[u] + g + 1)
                    dve.tensor_tensor_reduce(out=src[g][:, 0:n], in0=src[g][:, 0:n], in1=m, scale=-SCALE, scalar=-TAKEN,
                                             op0=ALU.add, op1=ALU.min, accum_out=s[:, 2 + g:3 + g])\
                        .then_inc(*tell(masked))

            def gate_over_sum(u):
                own()
                if not REAL[u]:
                    return
                kind, b = UNITS[u][:2]
                s = stats[:, u % 4, :]
                dve.wait_ge(exped, SIG[u + 1])
                g2 = 2 if kind == "P" else 1
                if b == DSA:
                    dve.reciprocal(s[:, 6:6 + g2], s[:, 4:4 + g2]).then_inc(*tell(r_made))
                    return
                link(dve.reciprocal(s[:, 6:6 + g2], s[:, 4:4 + g2]))
                if kind == "P":
                    j, t = UNITS[u][2:]
                    gate = gates[:, t, :].rearrange("p (g j b) -> p g j b", g=2, j=4)[:, :, j, b]
                else:
                    gate = grow[:, UNITS[u][2], b:b + 1]
                tt(s[:, 6:6 + g2], s[:, 6:6 + g2], gate, ALU.mult).then_inc(*tell(r_made))

            def copy_turned(u):
                if UNITS[u][0] != "P":
                    return
                own()
                kind, b = UNITS[u][:2]
                dve.wait_ge(pt_done, TURNS[u] + 2)
                if ORD[u] == 0:
                    dve.wait_ge(stored["win"], 32)
                if ORD[u] >= 2:
                    dve.wait_ge(pv_done, ORD[u] - 1)
                pt = probT[:, ORD[u] % 2]
                if kind == "P" and b == CMP:
                    x = cp(pt[0:NCP, 1, 0:P], bank[5][0:NCP, 0:P])
                else:
                    n = P * (UNITS[u][3] + 1)
                    x = cp(pt[:, 1, 0:n], bank[5][:, 0:n])
                x.then_inc(*tell(pt_dve))

            def copy_out(w):
                own()
                if w == 0:
                    for name in ("idx", "kv", "dkv"):
                        dve.wait_ge(stored[name], 32)
                kind, j = OWNERS[w]
                src = bank[6 + w % 2]
                dve.wait_ge(pv_done, ORD[LAST_OF[w]] + 1)
                if kind in "nd":
                    cp(oT[:, j + (4 if kind == "d" else 0), 0:SEQ], src[:, :]).then_inc(*tell(o_copied))
                    return
                b0 = 4 if kind == "D" else 0
                for g in range(2):
                    x = cp(oT[64 * g:64 * g + 64, b0:b0 + 4, SEQ + 16 * j:SEQ + 16 * j + 16]
                           .rearrange("p j (s t) -> p j s t", s=4),
                           src[64 * g:64 * g + 64, 0:P].rearrange("p (s g j t) -> p g j s t", s=4, g=2, j=4)[:, g])
                x.then_inc(*tell(o_copied))

            for i in range(len(UNITS) + LAG + 2):
                if i == 5:
                    dve.wait_ge(lo_made, POOL_SPLITS)
                    split_lo(POOL_SPLITS)
                    split_lo(POOL_SPLITS + 1)
                elif i in (8, 12, 16, 20):
                    rounds(3, 1)
                elif i == 24:
                    for t in (1, 2, 3):
                        x = mask_rest(score[:, t - 1, 0:P * (t + 1)])
                    link(x)
                if i < len(UNITS):
                    mask_max(i)
                if 0 <= i - LAG < len(UNITS):
                    copy_turned(i - LAG)
                if 0 <= i - 1 < len(UNITS):
                    gate_over_sum(i - 1)
                for w, u in LAST_OF.items():
                    if u == i - LAG - 2:
                        copy_out(w)
            dve.wait_ge(o_copied, len(OWNERS))
            for job in range(G0, len(JOBS)):
                g = job - G0
                kind, c = JOBS[job]
                if kind == "mn" and c == 0:
                    cp(gate_p, spread(gateT[:, :, 0], 2, P))
                    cp(cT[:, :, :].rearrange("p k (s t) -> p k s t", t=NEW), spread(gateT[:, :, 1:9], 3, NEW))\
                        .then_inc(*tell(gate_spread))
                for t in range(4 if kind != "y" else 0):
                    if t % blocks_of(job) == 0:
                        split_lo(FIRST[job] + t // blocks_of(job) + 2)
                    if kind == "z":
                        n = 4 * c + t
                        dve.wait_ge(g_act, GA[g] + t + 1)
                        own()
                        x = oT[:, n, :]
                        tt(x, x, zs[:, n % 2, :], ALU.mult).then_inc(*tell(z_mul))
                        own()
                        dve.wait_ge(oz_hi, n + 1)
                        tt(oz[1][:, n, :], x, oz[0][:, n, :].bitcast(F32), ALU.subtract).then_inc(*tell(oz_lo))
                    elif kind in ("un", "ud"):
                        gate = sg if kind == "un" else sg2
                        dst = mt if kind == "un" else gate
                        dve.wait_ge(g_act, GA[g])
                        tile_ready(dve, job, t)
                        own()
                        if kind == "un" and c:
                            dve.wait_ge(mT_hi, t + 1)
                        tt(part(dst, t), product(job, t), part(gate, t), ALU.mult).then_inc(*tell(g_dve))
                        if kind == "ud":
                            own()
                            tt(mt[:, t, :], mt[:, t, :], gate[:, t, :], ALU.add).then_inc(*tell(m_made))
                            own()
                            dve.wait_ge(mT_hi, 4 * c + t + 1)
                            tt(mT[1][:, 4 * c + t, :], mt[:, t, :], mT[0][:, 4 * c + t, :].bitcast(F32),
                               ALU.subtract).then_inc(*tell(mT_lo))
                if kind == "y":
                    for n in before_evac(job):
                        split_lo(n)
                        if job == len(JOBS) - 2 and n == FIRST[job] + 2:
                            dve.wait_ge(gate_done, 1)
                            cp(gateP[:, 0:512], bank[5][:, :])
                            cp(gateP[:, 512:1024], bank[6][:, :])
                            cp(gateS[:, 0:512], bank[7][0:NS, :]).then_inc(*tell(gate_made))
                            dve.wait_ge(gate_done, 2)
                            link(cp(gateS[:, 512:1024], bank[7][0:NS, :]))
                    if c == 0:
                        dve.wait_ge(in_xy, 16 * NT)
                    for i in range(NT + 2 * c):
                        if i < NT:
                            r = rows(i)
                            tile_ready(dve, job, i)
                            own()
                            gate = (gateS if i == 4 else gateP)[0:r, 512 * c:512 * c + 512]
                            tmp = sg[0:r, i % 4, 0:512]
                            tt(tmp, bank[i][0:r, :], gate, ALU.mult).then_inc(*tell(g_dve))
                            dve.wait_ge(g_dve, GV[g] + i + 1)
                            y = yb[0:r, i, 512 * c:512 * c + 512]
                            tt(y, y, tmp, ALU.add).then_inc(*tell(y_sum))
                        if c and 0 <= i - 1 < NT:
                            t = i - 1
                            r = rows(t)
                            own()
                            dve.wait_ge(y_sq, NT + t + 1)
                            link(tt(norm[0:r, 12 + t:13 + t], norm[0:r, 2 * t:2 * t + 1],
                                    norm[0:r, 2 * t + 1:2 * t + 2], ALU.add))
                            ts(norm[0:r, 12 + t:13 + t], norm[0:r, 12 + t:13 + t], 1.0 / D, EPS, ALU.mult, ALU.add)\
                                .then_inc(*tell(y_ms))
                        if c and i >= 2:
                            t = i - 2
                            r = rows(t)
                            own()
                            dve.wait_ge(y_root, t + 1)
                            link(dve.reciprocal(norm[0:r, 24 + t:25 + t], norm[0:r, 18 + t:19 + t]))
                            if t == 0:
                                dve.wait_ge(in_fg, 16)
                            stt(out=yb[0:r, t, :], in0=yb[0:r, t, :], scalar=norm[0:r, 24 + t:25 + t],
                                in1=fgb[0:r, :], op0=ALU.mult, op1=ALU.mult).then_inc(*tell(y_out))
                    for n in after_evac(job):
                        split_lo(n)


INPUTS = ["x_prompt", "x_sample", "cache_nsa_kv", "cache_dsa_kv", "cache_dsa_idx_k", "state_nsa_win_kv", "page_table",
          "c_prompt", "c_sample", "norm_g", "w_ada", "b_ada", "w_in", "cmp_pe", "cmp_w1", "cmp_w2", "w_up_nsa",
          "w_up_dsa", "w_out", "final_g"]
OUTPUTS = [("y_p", (1, SEQ, D)), ("y_s", (NSEQ, NEW, D)), ("nsa_p", (1, 1, SEQ, 4, 2, HD)),
           ("dsa_p", (1, 1, SEQ, 2, 2, HD)), ("idx_p", (1, 1, SEQ, HD)), ("win_p", (1, 1, SEQ, 2, 2, HD)),
           ("nsa_s", (1, NSEQ, NEW, 4, 2, HD)), ("dsa_s", (1, NSEQ, NEW, 2, 2, HD)), ("idx_s", (1, NSEQ, NEW, HD)),
           ("win_s", (1, NSEQ, PAST, 2, 2, HD))]


def kernel(**inputs):
    import numpy as np
    import concourse.bacc as bacc
    from concourse.bass_utils import run_bass_kernel_spmd

    nc = bacc.Bacc("TRN2", target_bir_lowering=False, num_devices=1)
    arrays, args, outs = {}, {}, {}
    for name in INPUTS + ["tables"]:
        x = tables() if name == "tables" else np.ascontiguousarray(inputs[name])
        arrays[f"in_{name}"] = x
        args[name] = nc.dram_tensor(f"in_{name}", x.shape, mybir.dt.from_np(x.dtype), kind="ExternalInput").ap()
    for name, shape in OUTPUTS:
        outs[name] = nc.dram_tensor(f"out_{name}", shape, F32, kind="ExternalOutput").ap()
    build(nc, args, outs)
    r = run_bass_kernel_spmd(nc, [arrays], core_ids=[0])
    return tuple(r.results[0][f"out_{name}"] for name, _ in OUTPUTS)
```
